# Optimizing a Trainium2 kernel written in Bass

```python
import jax, jax.numpy as jnp
from jax import lax
import numpy as np
import math

D_MODEL = 1024
BATCH = 1
SEQ = 512
DEPTH = 2

N_MIXERS = 3
BLOCK = 128
ROPE_THETA = 500000.0
ROPE_FRAC = 4
EPS = 1e-6
NEG_INF = -1e30

A_HEADS = 8
A_QK_DIM = 128
A_ROPE_DIM = A_QK_DIM // ROPE_FRAC
A_NOPE_DIM = A_QK_DIM - A_ROPE_DIM
A_V_DIM = 128
A_KV_RANK = 256
IDX_HEADS = 16
IDX_DIM = 64
TOPK_MAX = 256

B_HEADS = 16
B_KV_HEADS = 4
B_HEAD_DIM = 64
B_WINDOW = 128

C_HEADS = 8
C_HEAD_DIM = 128
C_BRANCHES = ((128, 1), (512, 4), (2048, 16))

MEM_LEN = 256
MEM_HEADS = 4
MEM_HEAD_DIM = 64
MEM_WIDTH = MEM_HEADS * MEM_HEAD_DIM

D_FF = 2816
CONV_WIDTH = 3

MIX_WIDTH = 1024
OUT_IN = MIX_WIDTH + MEM_WIDTH
A_SPLITS = (A_HEADS * A_QK_DIM, A_KV_RANK, A_ROPE_DIM, IDX_HEADS * IDX_DIM, IDX_DIM, IDX_HEADS, MEM_WIDTH)
B_SPLITS = (B_HEADS * B_HEAD_DIM, B_KV_HEADS * B_HEAD_DIM, B_KV_HEADS * B_HEAD_DIM, MEM_WIDTH)
C_SPLITS = (C_HEADS * C_HEAD_DIM, C_HEADS * C_HEAD_DIM, C_HEADS * C_HEAD_DIM, MEM_WIDTH)
N_A = len(range(0, DEPTH, N_MIXERS))
N_B = len(range(1, DEPTH, N_MIXERS))
N_C = len(range(2, DEPTH, N_MIXERS))


def rmsnorm(x, g):
    xf = x.astype(jnp.float32)
    y = xf * lax.rsqrt(jnp.mean(xf * xf, axis=-1, keepdims=True) + EPS)
    return (y * g.astype(jnp.float32)).astype(x.dtype)

def split_cols(t, sizes):
    return jnp.split(t, np.cumsum(sizes)[:-1].tolist(), axis=-1)

def rope_tables(positions, rot_dim):
    inv = ROPE_THETA ** (-jnp.arange(0, rot_dim, 2, dtype=jnp.float32) / rot_dim)
    ang = positions.astype(jnp.float32)[..., None] * inv
    return jnp.cos(ang), jnp.sin(ang)

def apply_partial_rope(x, cos, sin):
    half = cos.shape[-1]
    rot = 2 * half
    xf = x[..., :rot].astype(jnp.float32)
    x1, x2 = xf[..., :half], xf[..., half:]
    c, s = cos[:, :, None, :], sin[:, :, None, :]
    xr = jnp.concatenate([x1 * c - x2 * s, x2 * c + x1 * s], axis=-1).astype(x.dtype)
    return jnp.concatenate([xr, x[..., rot:]], axis=-1)

def banded_window_attention(q, k, v, max_dist, scale, sink=None):
    B, n = q.shape[0], q.shape[1]
    nb = -(-n // BLOCK)
    pad = nb * BLOCK - n
    if pad:
        q = jnp.pad(q, ((0, 0), (0, pad), (0, 0), (0, 0), (0, 0)))
        k = jnp.pad(k, ((0, 0), (0, pad), (0, 0), (0, 0)))
        v = jnp.pad(v, ((0, 0), (0, pad), (0, 0), (0, 0)))
    qb = q.reshape(B, nb, BLOCK, *q.shape[2:])
    kb = k.reshape(B, nb, BLOCK, *k.shape[2:])
    vb = v.reshape(B, nb, BLOCK, *v.shape[2:])
    prev = ((0, 0), (1, 0), (0, 0), (0, 0), (0, 0))
    kk = jnp.concatenate([jnp.pad(kb[:, :-1], prev), kb], axis=2)
    vv = jnp.concatenate([jnp.pad(vb[:, :-1], prev), vb], axis=2)
    s = jnp.einsum('bnqhgd,bnkhd->bnhgqk', qb, kk).astype(jnp.float32) * scale
    qi = jnp.arange(BLOCK)[:, None]
    kj = jnp.arange(2 * BLOCK)[None, :]
    dist = BLOCK + qi - kj
    band = (dist >= 0) & (dist <= max_dist)
    blk = jnp.arange(nb)[:, None, None]
    mask = band[None] & ((blk > 0) | (kj >= BLOCK)[None])
    s = jnp.where(mask[None, :, None, None], s, NEG_INF)
    m = jnp.max(s, axis=-1)
    if sink is not None:
        sk = sink.astype(jnp.float32)[None, None, :, :, None]
        m = jnp.maximum(m, sk)
    p = jnp.exp(s - m[..., None])
    l = jnp.sum(p, axis=-1)
    if sink is not None:
        l = l + jnp.exp(sk - m)
    p = p / l[..., None]
    o = jnp.einsum('bnhgqk,bnkhd->bnqhgd', p, vv.astype(jnp.float32))
    o = o.reshape(B, nb * BLOCK, *o.shape[3:])[:, :n].astype(q.dtype)
    lse = (m + jnp.log(l)).transpose(0, 1, 4, 2, 3)
    lse = lse.reshape(B, nb * BLOCK, *lse.shape[3:])[:, :n]
    return o, lse

def dsa_attention(q_nope, q_rope, c_kv, k_rope, q_idx, k_idx, w_idx, w_uk, w_uv):
    B, S = q_nope.shape[0], q_nope.shape[1]
    topk = min(TOPK_MAX, S // 4)
    nb = S // BLOCK
    scale = A_QK_DIM ** -0.5
    q_lat = jnp.einsum('bshn,rhn->bshr', q_nope, w_uk)
    key_pos = jnp.arange(S)

    def to_blocks(t):
        return t.reshape(B, nb, BLOCK, *t.shape[2:]).swapaxes(0, 1)

    def one_block(args):
        ql, qr, qi, wi, t = args
        dots = jnp.einsum('bqhd,bsd->bqhs', qi, k_idx).astype(jnp.float32)
        score = jnp.einsum('bqhs,bqh->bqs', jax.nn.relu(dots), wi.astype(jnp.float32))
        causal = key_pos[None, :] <= t[:, None]
        score = jnp.where(causal[None], score, -jnp.inf)
        _, idx = lax.top_k(score, topk)
        c_sel = jax.vmap(lambda c, i: c[i])(c_kv, idx)
        kr_sel = jax.vmap(lambda c, i: c[i])(k_rope, idx)
        s = (jnp.einsum('bqhr,bqkr->bqhk', ql, c_sel)
             + jnp.einsum('bqhe,bqke->bqhk', qr, kr_sel)).astype(jnp.float32) * scale
        valid = idx <= t[None, :, None]
        s = jnp.where(valid[:, :, None, :], s, NEG_INF)
        p = jax.nn.softmax(s, axis=-1)
        return jnp.einsum('bqhk,bqkr->bqhr', p, c_sel.astype(jnp.float32)).astype(ql.dtype)

    t_ids = jnp.arange(S).reshape(nb, BLOCK)
    o_lat = lax.map(one_block, (to_blocks(q_lat), to_blocks(q_rope), to_blocks(q_idx), to_blocks(w_idx), t_ids))
    o_lat = o_lat.swapaxes(0, 1).reshape(B, S, A_HEADS, A_KV_RANK)
    return jnp.einsum('bshr,rhv->bshv', o_lat, w_uv)

def mixer_a(h, cos32, sin32, cos16, sin16, w_in, kv_norm, w_uk, w_uv):
    B, S, _ = h.shape
    q, c_kv, k_rope, q_idx, k_idx, w_idx, q_mem = split_cols(h @ w_in, A_SPLITS)
    q = apply_partial_rope(q.reshape(B, S, A_HEADS, A_QK_DIM), cos32, sin32)
    q_rope, q_nope = q[..., :A_ROPE_DIM], q[..., A_ROPE_DIM:]
    k_rope = apply_partial_rope(k_rope[:, :, None, :], cos32, sin32)[:, :, 0]
    c_kv = rmsnorm(c_kv, kv_norm)
    q_idx = apply_partial_rope(q_idx.reshape(B, S, IDX_HEADS, IDX_DIM), cos16, sin16)
    k_idx = apply_partial_rope(k_idx[:, :, None, :], cos16, sin16)[:, :, 0]
    w_idx = w_idx * (IDX_HEADS * IDX_DIM) ** -0.5
    o = dsa_attention(q_nope, q_rope, c_kv, k_rope, q_idx, k_idx, w_idx, w_uk, w_uv)
    return o.reshape(B, S, A_HEADS * A_V_DIM), q_mem

def mixer_b(h, cos16, sin16, w_in, sinks):
    B, S, _ = h.shape
    q, k, v, q_mem = split_cols(h @ w_in, B_SPLITS)
    group = B_HEADS // B_KV_HEADS
    q = apply_partial_rope(q.reshape(B, S, B_HEADS, B_HEAD_DIM), cos16, sin16)
    k = apply_partial_rope(k.reshape(B, S, B_KV_HEADS, B_HEAD_DIM), cos16, sin16)
    v = v.reshape(B, S, B_KV_HEADS, B_HEAD_DIM)
    q = q.reshape(B, S, B_KV_HEADS, group, B_HEAD_DIM)
    o, _ = banded_window_attention(q, k, v, B_WINDOW - 1, B_HEAD_DIM ** -0.5,
                                   sink=sinks.reshape(B_KV_HEADS, group))
    return o.reshape(B, S, B_HEADS * B_HEAD_DIM), q_mem

def dilate(t, d):
    B, S = t.shape[0], t.shape[1]
    return t.reshape(B, S // d, d, *t.shape[2:]).swapaxes(1, 2).reshape(B * d, S // d, *t.shape[2:])

def undilate(t, d, B):
    n = t.shape[1]
    return t.reshape(B, d, n, *t.shape[2:]).swapaxes(1, 2).reshape(B, n * d, *t.shape[2:])

def mixer_c(h, cos32, sin32, w_in):
    B, S, _ = h.shape
    q, k, v, q_mem = split_cols(h @ w_in, C_SPLITS)
    q = apply_partial_rope(q.reshape(B, S, C_HEADS, C_HEAD_DIM), cos32, sin32)
    k = apply_partial_rope(k.reshape(B, S, C_HEADS, C_HEAD_DIM), cos32, sin32)
    v = v.reshape(B, S, C_HEADS, C_HEAD_DIM)
    outs, lses = [], []
    for window, d in C_BRANCHES:
        o_g, lse_g = banded_window_attention(dilate(q, d)[:, :, :, None], dilate(k, d), dilate(v, d),
                                             window // d, C_HEAD_DIM ** -0.5)
        outs.append(undilate(o_g[:, :, :, 0], d, B))
        lses.append(undilate(lse_g[..., 0], d, B))
    alpha = jax.nn.softmax(jnp.stack(lses), axis=0)
    o = jnp.sum(alpha[..., None] * jnp.stack(outs).astype(jnp.float32), axis=0).astype(h.dtype)
    return o.reshape(B, S, C_HEADS * C_HEAD_DIM), q_mem

def memory_cross_attention(q_mem, mem_n, w_mem_kv):
    B, S, _ = q_mem.shape
    k, v = jnp.split(mem_n @ w_mem_kv, 2, axis=-1)
    k = k.reshape(B, -1, MEM_HEADS, MEM_HEAD_DIM)
    v = v.reshape(B, -1, MEM_HEADS, MEM_HEAD_DIM)
    q = q_mem.reshape(B, S, MEM_HEADS, MEM_HEAD_DIM)
    s = jnp.einsum('bshd,bmhd->bhsm', q, k).astype(jnp.float32) * MEM_HEAD_DIM ** -0.5
    p = jax.nn.softmax(s, axis=-1)
    o = jnp.einsum('bhsm,bmhd->bshd', p, v.astype(jnp.float32)).astype(q_mem.dtype)
    return o.reshape(B, S, MEM_WIDTH)

def conv_glu_ffn(h, w_up, conv_w, conv_b, w_down):
    S = h.shape[1]
    a, b = jnp.split(h @ w_up, 2, axis=-1)
    a_pad = jnp.pad(a, ((0, 0), (CONV_WIDTH - 1, 0), (0, 0)))
    a = sum(conv_w[j] * a_pad[:, j:j + S] for j in range(CONV_WIDTH)) + conv_b
    return (jax.nn.silu(a) * b) @ w_down

def first_inputs(seed: int = 0) -> dict:
    key = jax.random.key(seed)
    ks = iter(jax.random.split(key, 40))

    def w(shape, fan_in):
        return jax.random.normal(next(ks), shape, jnp.float32) * fan_in ** -0.5

    def gain(shape):
        return 1.0 + 0.02 * jax.random.normal(next(ks), shape, jnp.float32)

    x = jax.random.normal(next(ks), (BATCH, SEQ, D_MODEL), jnp.float32)
    mem = jax.random.normal(next(ks), (BATCH, MEM_LEN, D_MODEL), jnp.float32)
    offset = jax.random.randint(next(ks), (BATCH, 1), 0, 4096, dtype=jnp.int32)
    positions = offset + jnp.arange(SEQ, dtype=jnp.int32)[None, :]
    return {
        'x': x, 'mem': mem, 'positions': positions,
        'g_mix': gain((DEPTH, D_MODEL)), 'g_ffn': gain((DEPTH, D_MODEL)),
        'g_mem': gain((D_MODEL,)), 'g_final': gain((D_MODEL,)),
        'w_mem_kv': w((DEPTH, D_MODEL, 2 * MEM_WIDTH), D_MODEL),
        'a_w_in': w((N_A, D_MODEL, sum(A_SPLITS)), D_MODEL),
        'a_kv_norm': gain((N_A, A_KV_RANK)),
        'a_w_uk': w((N_A, A_KV_RANK, A_HEADS, A_NOPE_DIM), A_KV_RANK),
        'a_w_uv': w((N_A, A_KV_RANK, A_HEADS, A_V_DIM), A_KV_RANK),
        'a_w_out': w((N_A, OUT_IN, D_MODEL), OUT_IN),
        'b_w_in': w((N_B, D_MODEL, sum(B_SPLITS)), D_MODEL),
        'b_sinks': 0.5 * jax.random.normal(next(ks), (N_B, B_HEADS), jnp.float32),
        'b_w_out': w((N_B, OUT_IN, D_MODEL), OUT_IN),
        'c_w_in': w((N_C, D_MODEL, sum(C_SPLITS)), D_MODEL),
        'c_w_out': w((N_C, OUT_IN, D_MODEL), OUT_IN),
        'f_w_up': w((DEPTH, D_MODEL, 2 * D_FF), D_MODEL),
        'f_conv_w': w((DEPTH, CONV_WIDTH, D_FF), CONV_WIDTH),
        'f_conv_b': 0.02 * jax.random.normal(next(ks), (DEPTH, D_FF), jnp.float32),
        'f_w_down': w((DEPTH, D_FF, D_MODEL), D_FF),
    }

def first_block(x, mem, positions, g_mix, g_ffn, g_mem, g_final, w_mem_kv,
              a_w_in, a_kv_norm, a_w_uk, a_w_uv, a_w_out,
              b_w_in, b_sinks, b_w_out, c_w_in, c_w_out,
              f_w_up, f_conv_w, f_conv_b, f_w_down):
    cos32, sin32 = rope_tables(positions, A_QK_DIM // ROPE_FRAC)
    cos16, sin16 = rope_tables(positions, B_HEAD_DIM // ROPE_FRAC)
    mem_n = rmsnorm(mem, g_mem)
    for i in range(DEPTH):
        kind, j = i % N_MIXERS, i // N_MIXERS
        h = rmsnorm(x, g_mix[i])
        if kind == 0:
            mix, q_mem = mixer_a(h, cos32, sin32, cos16, sin16, a_w_in[j], a_kv_norm[j], a_w_uk[j], a_w_uv[j])
            w_out = a_w_out[j]
        elif kind == 1:
            mix, q_mem = mixer_b(h, cos16, sin16, b_w_in[j], b_sinks[j])
            w_out = b_w_out[j]
        else:
            mix, q_mem = mixer_c(h, cos32, sin32, c_w_in[j])
            w_out = c_w_out[j]
        mem_o = memory_cross_attention(q_mem, mem_n, w_mem_kv[i])
        x = x + jnp.concatenate([mix, mem_o], axis=-1) @ w_out
        x = x + conv_glu_ffn(rmsnorm(x, g_ffn[i]), f_w_up[i], f_conv_w[i], f_conv_b[i], f_w_down[i])
    return rmsnorm(x, g_final)


N_A_LAYERS = DEPTH // 2
N_B_LAYERS = DEPTH - N_A_LAYERS

EXPAND = 2
CONV_D = EXPAND * D_MODEL

N_HEADS = 16
HEAD_DIM = D_MODEL // N_HEADS
N_KV_GROUPS = 4
HEADS_PER_GROUP = N_HEADS // N_KV_GROUPS
ATTN_D = N_HEADS * HEAD_DIM
KV_D = N_KV_GROUPS * HEAD_DIM
N_BRANCH = 3
N_KV_STREAMS = 6
ROT_DIM = HEAD_DIM // 4
CMP_BLOCK = 32
CMP_STRIDE = 16
CMP_R = CMP_BLOCK // CMP_STRIDE
CMP_HIDDEN = 4 * HEAD_DIM
SLC_BLOCK = 64
SLC_RATIO = SLC_BLOCK // CMP_STRIDE
N_SELECT = 16
N_LOCAL = 2
WINDOW = 512
Q_BLOCK = 64
FORCE_SCORE = 1e4


def rmsnorm_2(x, g):
    xf = x.astype(jnp.float32)
    y = xf * lax.rsqrt(jnp.mean(xf * xf, axis=-1, keepdims=True) + EPS)
    return (y * g.astype(jnp.float32)).astype(x.dtype)

def partial_rope(x):
    S = x.shape[1]
    pos = jnp.arange(S, dtype=jnp.float32)
    inv = ROPE_THETA ** (-jnp.arange(0, ROT_DIM, 2, dtype=jnp.float32) / ROT_DIM)
    ang = pos[:, None] * inv[None, :]
    cos = jnp.cos(ang)[None, :, None, :]
    sin = jnp.sin(ang)[None, :, None, :]
    xr = x[..., :ROT_DIM].astype(jnp.float32)
    x1, x2 = xr[..., :ROT_DIM // 2], xr[..., ROT_DIM // 2:]
    rot = jnp.concatenate([x1 * cos - x2 * sin, x2 * cos + x1 * sin], axis=-1).astype(x.dtype)
    return jnp.concatenate([rot, x[..., ROT_DIM:]], axis=-1)

def masked_softmax(s, mask, axis=-1):
    s = jnp.where(mask, s.astype(jnp.float32), -jnp.inf)
    m = jnp.max(s, axis=axis, keepdims=True)
    m = jnp.where(jnp.isfinite(m), m, 0.0)
    e = jnp.where(mask, jnp.exp(s - m), 0.0)
    d = jnp.sum(e, axis=axis, keepdims=True)
    return e / jnp.maximum(d, 1e-30)

def short_conv_layer(x, norm_g, w_in, conv_w, w_out):
    S = x.shape[1]
    h = rmsnorm_2(x, norm_g)
    proj = h @ w_in
    b, c, u, z = jnp.split(proj, 4, axis=-1)
    vp = jnp.pad(c * u, ((0, 0), (CONV_WIDTH - 1, 0), (0, 0)))
    conv = conv_w[0] * vp[:, 0:S]
    for k in range(1, CONV_WIDTH):
        conv = conv + conv_w[k] * vp[:, k:k + S]
    y = b * conv * jax.nn.silu(z)
    return x + y @ w_out

def compress_blocks(kv, pos_emb, w1, w2):
    B, S, G, D = kv.shape
    chunks = kv.reshape(B, S // CMP_STRIDE, CMP_STRIDE, G, D)
    n_cmp = S // CMP_STRIDE - CMP_R + 1
    blocks = jnp.concatenate([chunks[:, r:r + n_cmp] for r in range(CMP_R)], axis=2)
    blocks = blocks + pos_emb[None, None, :, None, :]
    flat = blocks.transpose(0, 1, 3, 2, 4).reshape(B, n_cmp, G, CMP_BLOCK * D)
    return jax.nn.gelu(flat @ w1) @ w2

def shared_kv(h, norm_g, w_kv, cmp_pos_k, cmp_w1_k, cmp_w2_k, cmp_pos_v, cmp_w1_v, cmp_w2_v):
    B, S, _ = h.shape
    kv = (rmsnorm_2(h, norm_g) @ w_kv).reshape(B, S, N_KV_STREAMS, N_KV_GROUPS, HEAD_DIM)
    k_c, v_c, k_s, v_s, k_w, v_w = [kv[:, :, i] for i in range(N_KV_STREAMS)]
    k_cmp = compress_blocks(k_c, cmp_pos_k, cmp_w1_k, cmp_w2_k)
    v_cmp = compress_blocks(v_c, cmp_pos_v, cmp_w1_v, cmp_w2_v)
    return (k_cmp, v_cmp, partial_rope(k_s), v_s, partial_rope(k_w), v_w)

def nsa_attention(q, q_rot, gates, k_cmp, v_cmp, k_slc, v_slc, k_win, v_win):
    B, S, H, D = q.shape
    G, I = N_KV_GROUPS, HEADS_PER_GROUP
    n_blk = S // Q_BLOCK
    n_cmp = k_cmp.shape[1]
    n_sb = S // SLC_BLOCK
    n_sel = min(N_SELECT, n_sb)
    scale = HEAD_DIM ** -0.5
    cmp_end = jnp.arange(n_cmp) * CMP_STRIDE + CMP_BLOCK - 1
    kb_slc = k_slc.reshape(B, n_sb, SLC_BLOCK, G, D).transpose(0, 3, 1, 2, 4)
    vb_slc = v_slc.reshape(B, n_sb, SLC_BLOCK, G, D).transpose(0, 3, 1, 2, 4)
    k_win_p = jnp.pad(k_win, ((0, 0), (WINDOW, 0), (0, 0), (0, 0)))
    v_win_p = jnp.pad(v_win, ((0, 0), (WINDOW, 0), (0, 0), (0, 0)))
    bi = jnp.arange(B)[:, None, None, None]
    gi = jnp.arange(G)[None, None, :, None]
    blk_ids = jnp.arange(n_sb)

    def to_blocks(a):
        return a.reshape(B, n_blk, Q_BLOCK, G, I, a.shape[-1]).transpose(1, 0, 2, 3, 4, 5)

    def block_fn(args):
        blk, qc, qr, g = args
        start = blk * Q_BLOCK
        t = start + jnp.arange(Q_BLOCK)

        s_c = jnp.einsum('bqgid,bngd->bqgin', qc, k_cmp) * scale
        m_c = (cmp_end[None, :] <= t[:, None])[None, :, None, None, :]
        p_c = masked_softmax(s_c, m_c)
        o_c = jnp.einsum('bqgin,bngd->bqgid', p_c.astype(v_cmp.dtype), v_cmp)

        p_grp = jnp.pad(p_c.sum(axis=3), ((0, 0), (0, 0), (0, 0), (CMP_R - 1, CMP_R - 1)))
        imp = 0.0
        for m in range(SLC_RATIO):
            for n in range(CMP_R):
                off = CMP_R - 1 + m - n
                imp = imp + p_grp[..., off:off + SLC_RATIO * (n_sb - 1) + 1:SLC_RATIO]
        cur = t // SLC_BLOCK
        valid = blk_ids[None, :] <= cur[:, None]
        forced = (blk_ids[None, :] == 0) | (valid & (blk_ids[None, :] > cur[:, None] - N_LOCAL))
        score = jnp.where(forced[None, :, None, :], FORCE_SCORE, imp)
        score = jnp.where(valid[None, :, None, :], score, -jnp.inf)
        top_s, idx = lax.top_k(score, n_sel)
        sel_ok = jnp.isfinite(top_s)

        kg = kb_slc[bi, gi, idx]
        vg = vb_slc[bi, gi, idx]
        s_s = jnp.einsum('bqgid,bqgnld->bqginl', qr, kg) * scale
        kpos = idx[..., None] * SLC_BLOCK + jnp.arange(SLC_BLOCK)
        m_s = sel_ok[..., None] & (kpos <= t[None, :, None, None, None])
        p_s = masked_softmax(s_s.reshape(B, Q_BLOCK, G, I, n_sel * SLC_BLOCK),
                             m_s.reshape(B, Q_BLOCK, G, 1, n_sel * SLC_BLOCK))
        p_s = p_s.reshape(B, Q_BLOCK, G, I, n_sel, SLC_BLOCK).astype(vg.dtype)
        o_s = jnp.einsum('bqginl,bqgnld->bqgid', p_s, vg)

        kw = lax.dynamic_slice_in_dim(k_win_p, start, WINDOW + Q_BLOCK, axis=1)
        vw = lax.dynamic_slice_in_dim(v_win_p, start, WINDOW + Q_BLOCK, axis=1)
        kpos_w = start - WINDOW + jnp.arange(WINDOW + Q_BLOCK)
        m_w = ((kpos_w[None, :] <= t[:, None]) & (kpos_w[None, :] > t[:, None] - WINDOW)
               & (kpos_w[None, :] >= 0))
        s_w = jnp.einsum('bqgid,bkgd->bqgik', qr, kw) * scale
        p_w = masked_softmax(s_w, m_w[None, :, None, None, :]).astype(vw.dtype)
        o_w = jnp.einsum('bqgik,bkgd->bqgid', p_w, vw)

        return g[..., 0:1] * o_c + g[..., 1:2] * o_s + g[..., 2:3] * o_w

    xs = (jnp.arange(n_blk), to_blocks(q), to_blocks(q_rot), to_blocks(gates))
    out = lax.map(block_fn, xs)
    return out.transpose(1, 0, 2, 3, 4, 5).reshape(B, S, H, D)

def nsa_layer(x, kvs, norm_g, w_in, w_out):
    B, S, _ = x.shape
    h = rmsnorm_2(x, norm_g)
    proj = h @ w_in
    q = proj[..., :ATTN_D].reshape(B, S, N_HEADS, HEAD_DIM)
    gates = jax.nn.sigmoid(proj[..., ATTN_D:ATTN_D + N_HEADS * N_BRANCH]
                           .reshape(B, S, N_HEADS, N_BRANCH))
    z = proj[..., ATTN_D + N_HEADS * N_BRANCH:]
    o = nsa_attention(q, partial_rope(q), gates, *kvs)
    y = o.reshape(B, S, ATTN_D) * jax.nn.silu(z)
    return x + y @ w_out

def second_inputs(seed: int = 0) -> dict:
    key = jax.random.key(seed)
    ks = jax.random.split(key, 20)
    f = jnp.float32
    nrm = lambda k, shape, s: jax.random.normal(k, shape, f) * s
    gain = lambda k, shape: 1.0 + 0.01 * jax.random.normal(k, shape, f)
    b_in_cols = ATTN_D + N_HEADS * N_BRANCH + ATTN_D
    return {
        "x": jax.random.normal(ks[0], (BATCH, SEQ, D_MODEL), f),
        "a_norm": gain(ks[1], (N_A_LAYERS, D_MODEL)),
        "a_w_in": nrm(ks[2], (N_A_LAYERS, D_MODEL, 4 * CONV_D), D_MODEL ** -0.5),
        "a_conv_w": nrm(ks[3], (N_A_LAYERS, CONV_WIDTH, CONV_D), CONV_WIDTH ** -0.5),
        "a_w_out": nrm(ks[4], (N_A_LAYERS, CONV_D, D_MODEL), CONV_D ** -0.5),
        "kv_norm": gain(ks[5], (D_MODEL,)),
        "w_kv": nrm(ks[6], (D_MODEL, N_KV_STREAMS * KV_D), D_MODEL ** -0.5),
        "cmp_pos_k": nrm(ks[7], (CMP_BLOCK, HEAD_DIM), 0.1),
        "cmp_w1_k": nrm(ks[8], (CMP_BLOCK * HEAD_DIM, CMP_HIDDEN), (CMP_BLOCK * HEAD_DIM) ** -0.5),
        "cmp_w2_k": nrm(ks[9], (CMP_HIDDEN, HEAD_DIM), CMP_HIDDEN ** -0.5),
        "cmp_pos_v": nrm(ks[10], (CMP_BLOCK, HEAD_DIM), 0.1),
        "cmp_w1_v": nrm(ks[11], (CMP_BLOCK * HEAD_DIM, CMP_HIDDEN), (CMP_BLOCK * HEAD_DIM) ** -0.5),
        "cmp_w2_v": nrm(ks[12], (CMP_HIDDEN, HEAD_DIM), CMP_HIDDEN ** -0.5),
        "b_norm": gain(ks[13], (N_B_LAYERS, D_MODEL)),
        "b_w_in": nrm(ks[14], (N_B_LAYERS, D_MODEL, b_in_cols), D_MODEL ** -0.5),
        "b_w_out": nrm(ks[15], (N_B_LAYERS, ATTN_D, D_MODEL), ATTN_D ** -0.5),
        "final_norm": gain(ks[16], (D_MODEL,)),
    }

def second_block(x, a_norm, a_w_in, a_conv_w, a_w_out, kv_norm, w_kv, cmp_pos_k, cmp_w1_k,
              cmp_w2_k, cmp_pos_v, cmp_w1_v, cmp_w2_v, b_norm, b_w_in, b_w_out, final_norm):
    h = x
    kvs = None
    for layer in range(DEPTH):
        if layer < N_A_LAYERS:
            h = short_conv_layer(h, a_norm[layer], a_w_in[layer], a_conv_w[layer], a_w_out[layer])
        else:
            if layer == N_A_LAYERS:
                kvs = shared_kv(h, kv_norm, w_kv, cmp_pos_k, cmp_w1_k, cmp_w2_k,
                                cmp_pos_v, cmp_w1_v, cmp_w2_v)
            j = layer - N_A_LAYERS
            h = nsa_layer(h, kvs, b_norm[j], b_w_in[j], b_w_out[j])
    return rmsnorm_2(h, final_norm)


def setup_inputs(seed=0):
    out = dict(first_inputs(seed))
    for name, value in second_inputs(seed + 1).items():
        if name != "x":
            out[name + "_2"] = value
    return out


def reference(
    x, mem, positions, g_mix, g_ffn, g_mem, g_final, w_mem_kv, a_w_in, a_kv_norm, a_w_uk,
    a_w_uv, a_w_out, b_w_in, b_sinks, b_w_out, c_w_in, c_w_out, f_w_up, f_conv_w, f_conv_b,
    f_w_down, a_norm_2, a_w_in_2, a_conv_w_2, a_w_out_2, kv_norm_2, w_kv_2, cmp_pos_k_2,
    cmp_w1_k_2, cmp_w2_k_2, cmp_pos_v_2, cmp_w1_v_2, cmp_w2_v_2, b_norm_2, b_w_in_2, b_w_out_2,
    final_norm_2,
):
    x = first_block(
        x, mem, positions, g_mix, g_ffn, g_mem, g_final, w_mem_kv, a_w_in, a_kv_norm, a_w_uk,
        a_w_uv, a_w_out, b_w_in, b_sinks, b_w_out, c_w_in, c_w_out, f_w_up, f_conv_w, f_conv_b,
        f_w_down,
    )
    return second_block(
        x, a_norm_2, a_w_in_2, a_conv_w_2, a_w_out_2, kv_norm_2, w_kv_2, cmp_pos_k_2,
        cmp_w1_k_2, cmp_w2_k_2, cmp_pos_v_2, cmp_w1_v_2, cmp_w2_v_2, b_norm_2, b_w_in_2,
        b_w_out_2, final_norm_2,
    )


_drawn_inputs = setup_inputs


def setup_inputs(seed=0):
    import zlib

    import numpy as np

    out = dict(_drawn_inputs(seed))
    spreads = {}
    factors = {'g_mem': 8.0,
     'a_kv_norm': 6.797,
     'b_sinks': 5.94,
     'f_conv_b': 2.875,
     'a_norm_2': 5.295,
     'kv_norm_2': 64.0,
     'cmp_pos_k_2': 58.858,
     'cmp_pos_v_2': 30.176,
     'b_norm_2': 64.0,
     'final_norm_2': 29.799,
     'g_ffn': 3.87}
    for name, (base, spread) in spreads.items():
        noise = np.random.default_rng([zlib.crc32(name.encode()), seed]).standard_normal(out[name].shape)
        drawn = base * np.exp(spread * noise) if base else spread * noise
        out[name] = __import__('jax').numpy.asarray(drawn.astype(out[name].dtype))
    for name, factor in factors.items():
        out[name] = (out[name] * factor).astype(out[name].dtype)
    return out
```

```python
import concourse.bass as bass
from concourse import mybir
from contextlib import ExitStack

P = 128
S = 512
D = 1024
DT = D // P
NB = S // P
CB = 8
CW = CB * P
MEM = 256
FT = 2816 // P
CT = 2048 // P
DOWN_CHUNKS = -(-FT // CB)
EPS = 1e-6
NEG = -1e30
TAKEN = -3e38
TOPK = 128
NCMP = 32
FPAD = 544
TWO_PI = 6.283185307179586
PI_HI = 6.28125
PI_LO = TWO_PI - PI_HI
ROUNDER = 12582912.0

STAGES = [("mem", 8), ("afront", 4), ("idx", 8), ("aq", 16), ("amem", 2), ("aout", 16), ("up0", 2 * FT),
          ("down0", DT * DOWN_CHUNKS), ("bfront", 4), ("bq", 8), ("bmem", 2), ("bout", 16), ("up1", 2 * FT),
          ("down1", DT * DOWN_CHUNKS), ("conv", 4 * CT), ("cout", 2 * DT), ("cmp_kv", 4), ("cmp", 9), ("nkv", 8),
          ("gates", 1), ("nz", 8), ("nq", 8), ("nout", DT)]
CH, NCHUNKS = {}, 0
for _name, _count in STAGES:
    CH[_name] = NCHUNKS
    NCHUNKS += _count

TILES = [("mem", 8), ("afront", 4), ("idx", 8), ("aq", 24), ("amem", 2), ("aout", 8), ("up0", 2 * FT), ("down0", 8),
         ("bfront", 4), ("bq", 8), ("bmem", 2), ("bout", 8), ("up1", 2 * FT), ("down1", 8), ("conv", 4 * CT),
         ("cout", 8), ("cmp_kv", 4), ("cmp", 6), ("nkv", 8), ("gates", 1), ("nz", 8), ("nq", 8), ("nout", 8)]
TL, _t = {}, 0
for _name, _count in TILES:
    TL[_name] = _t
    _t += _count

ROPES = [("krope", 1), ("kidx", 1), ("idx", 8), ("aq", 8), ("bk", 2), ("bq", 8), ("nk_s", 2), ("nk_w", 2),
         ("nq", 8)]
RP, _t = {}, 0
for _name, _count in ROPES:
    RP[_name] = _t
    _t += _count

NORMS = [("mem", 8), ("amix", 8), ("ckv", 2), ("affn", 8), ("bmix", 8), ("bffn", 8), ("final1", 8), ("conv", 8),
         ("kv2", 8), ("q2", 8), ("final2", 8)]
NQ = {name: q for q, (name, _) in enumerate(NORMS)}
PLAIN = ("final1", "final2")
SBASE = [sum(k for n, k in NORMS[:q] if n not in PLAIN) for q in range(len(NORMS) + 1)]
RESIDUALS = {name: DT * k for k, name in enumerate(("aout", "down0", "bout", "down1", "cout", "nout"))}
NBASE = [sum(k for _, k in NORMS[:q]) for q in range(len(NORMS) + 1)]

TURNS = [("memv", 4), ("widx", 1), ("bv", 2), ("cmpv", 1), ("nv_s", 2), ("nv_w", 2), ("gates", 1)]
TN, _t = {}, 0
for _name, _count in TURNS:
    TN[_name] = _t
    _t += _count


class Attention:

    def __init__(self, name, tiles, units, chunks, dv, scale, first_score, first_unit, first_tile, out0):
        self.name, self.tiles, self.units, self.chunks, self.dv, self.scale = name, tiles, units, chunks, dv, scale
        self.first_score, self.first_unit, self.first_tile, self.out0 = first_score, first_unit, first_tile, out0
        self.n = len(units)

    def keys(self, j):
        _, b, branch = self.units[j]
        if branch == "mem":
            return 0, MEM
        if branch == "band":
            return (0, P) if b == 0 else ((b - 1) * P, 2 * P)
        if branch == "cmp":
            return 0, NCMP
        return 0, (b + 1) * P


IDX_UNITS = [(hh, b) for hh in range(2) for b in range(1, NB)]
IDX_SCORES = 8 * len(IDX_UNITS)


def _attentions():
    made, score, unit, tile = {}, IDX_SCORES, 0, 0
    pair = [(hh, b) for hh in range(2) for b in range(NB)]
    for name, tiles, units, chunks, dv, dim, out0 in (
            ("aq", 8, [(0, b, "topk") for b in range(NB)], 2, 128, 128, 0),
            ("amem", 2, [(hh, b, "mem") for hh, b in pair], 1, 64, 64, 8),
            ("bq", 8, [(hh, b, "band") for hh, b in pair], 1, 64, 64, 0),
            ("bmem", 2, [(hh, b, "mem") for hh, b in pair], 1, 64, 64, 8),
            ("nq", 8, [(hh, b, br) for hh, b in pair for br in ("cmp", "slc", "win")], 1, 64, 64, 0)):
        made[name] = Attention(name, tiles, units, chunks, dv, float(dim) ** -0.5, score, unit, tile, out0)
        score += tiles * len(units)
        unit += tiles * len(units)
        tile += tiles
    return made


ATT = _attentions()

VECS = [("g_mix", 16), ("g_ffn", 16), ("g_mem", 8), ("g_final", 8), ("a_norm", 8), ("kv_norm", 8), ("b_norm", 8),
        ("final_norm", 8), ("a_kv_norm", 2), ("f_conv_w", 2 * 3 * FT), ("f_conv_b", 2 * FT), ("a_conv_w", 3 * CT),
        ("sinks", 16), ("pos_k", 18), ("pos_v", 18)]
VC, NVEC = {}, 0
for _name, _count in VECS:
    VC[_name] = NVEC
    NVEC += _count
CONSTS = [("ident", P), ("causal", S), ("band", 2 * P), ("cmp", NB * NCMP), ("half", 2), ("inv128", 1), ("sgn128", 1),
          ("inv64", 1), ("sgn64", 1), ("rowvalid", 1)]
CC, NCONST = {}, 0
for _name, _count in CONSTS:
    CC[_name] = NCONST
    NCONST += _count

SHUF128 = [(i + 16) % 32 for i in range(32)]
SHUF64 = [(i + 8) % 16 if i < 16 else i for i in range(32)]


class At:

    def __init__(self, base, i=0, per=0):
        assert per % 2 == 0
        self.v = base + i * per if per else base
        self.par = base % 2
        self.half = base // 2 + i * (per // 2) if per else base // 2
        self.args = (base, i, per)

    def __add__(self, k):
        return At(self.args[0] + k, *self.args[1:])


class Links:

    def __init__(self, eng, sem):
        self.eng, self.sem, self.n, self.shift = eng, sem, 0, 0

    def mark(self, instruction):
        self.n += 1
        instruction.then_inc(self.sem, 1)

    def catch(self):
        self.eng.wait_ge(self.sem, self.shift + self.n)

    def __call__(self, instruction):
        self.mark(instruction)
        self.catch()

    def begin(self, i, per):
        self.shift, self.at = i * per, self.n

    def end(self, per, trips):
        assert self.n - self.at == per, (self.n - self.at, per)
        self.n, self.shift = self.at + per * trips, 0



def build(nc, wstream, xin, memin, posin, vecin, cstin, tab2in, out):
    f32, f32r, i32 = mybir.dt.float32, mybir.dt.float32r, mybir.dt.int32
    ALU, ACT = mybir.AluOpType, mybir.ActivationFunctionType
    ds = bass.ds
    place = [-(-nc.sbuf_base // 32) * 32]

    def put(name, cols, dt=f32, at=None):
        if at is None:
            at, place[0] = place[0], place[0] + -(-4 * cols // 32) * 32
            assert place[0] <= nc.sbuf_top, (name, place[0] - nc.sbuf_top)
        return nc.alloc_sbuf_tensor_at(name, [P, cols], dt, offset=at)

    xT = put("xT", DT * S)
    h_hi, h_lo = put("h_hi", DT * S, f32r), put("h_lo", DT * S, f32r)
    raw = put("raw", 2 * CW)
    w_hi, w_lo = put("w_hi", 2 * CW, f32r), put("w_lo", 2 * CW, f32r)
    vec, cst, ones = put("vec", NVEC), put("cst", NCONST), put("ones", P)
    tab64 = put("tab64", 2 * S)
    v4, r4, mhalf = put("v4", 8), put("r4", 8), put("mhalf", 8)
    stats = put("stats", 16)
    m8 = put("m8", 24)
    widx = put("widx", NB * 16)
    KB = 1024
    mem1 = place[0]
    place[0] += 6 * KB
    mem_k1, mem_v1 = put("mem_k1", 4 * MEM, at=mem1), put("mem_v1", 2 * MEM, at=mem1 + 4 * KB)

    sc0 = place[0]
    place[0] += 30 * KB
    s_sb, p_sb, pT = put("s_sb", 2 * S, at=sc0), put("p_sb", 2 * S, at=sc0 + 4 * KB), put("pT", 2 * S, at=sc0 + 8 * KB)
    o_sb, qraw, rtmp = put("o_sb", S, at=sc0 + 12 * KB), put("qraw", S, at=sc0 + 14 * KB), put("rtmp", S, at=sc0 + 16 * KB)
    qs, qn = put("qs", 2 * S, at=sc0 + 18 * KB), put("qn", 2 * S, at=sc0 + 22 * KB)
    vraw, ysb = put("vraw", S, at=sc0 + 26 * KB), put("ysb", S, at=sc0 + 28 * KB)
    ktmp, fraw = put("ktmp", 2 * S, at=sc0 + 4 * KB), put("fraw", 2 * S, at=sc0 + 8 * KB)
    nsink = put("nsink", 16)
    fa, fb, fc = put("fa", S, at=sc0), put("fb", S, at=sc0 + 2 * KB), put("fc", S, at=sc0 + 4 * KB)
    fd, fe, fg = put("fd", S, at=sc0 + 6 * KB), put("fe", S, at=sc0 + 8 * KB), put("fg", S, at=sc0 + 10 * KB)
    sq, hf, diag = put("sq", 2 * S, at=sc0 + 12 * KB), put("hf", 2 * S, at=sc0 + 16 * KB), put("diag", S, at=sc0 + 20 * KB)

    g0 = place[0]
    half = FT * S * 4
    place[0] += 2 * half
    assert place[0] <= nc.sbuf_top, place[0] - nc.sbuf_top
    g1 = g0 + half
    G_hi, G_lo = put("G_hi", FT * S, f32r, at=g0), put("G_lo", FT * S, f32r, at=g1)
    memn_hi, memn_lo = put("memn_hi", DT * MEM, f32r, at=g0), put("memn_lo", DT * MEM, f32r, at=g0 + 8 * KB)
    memT = put("memT", DT * MEM, at=g1)
    a_k, a_v = put("a_k", 2 * S, at=g0 + 20 * KB), put("a_v", 2 * S, at=g0 + 24 * KB)
    c_hi, c_lo = put("c_hi", 2 * S, f32r, at=g0 + 28 * KB), put("c_lo", 2 * S, f32r, at=g0 + 32 * KB)
    kidx, tab128 = put("kidx", 2 * S, at=g0 + 36 * KB), put("tab128", 2 * S, at=g0 + 40 * KB)
    bias_a, score = put("bias_a", 3 * S, at=g1 + 20 * KB), put("score", 3 * S, at=g1 + 26 * KB)
    mem_k0, mem_v0 = put("mem_k0", 4 * MEM, at=g1 + 32 * KB), put("mem_v0", 2 * MEM, at=g1 + 36 * KB)
    ckv = put("ckv", 2 * S, at=g1 + 38 * KB)
    posi, posf = put("posi", S, i32, at=g1 + 8 * KB), put("posf", S, at=g1 + 10 * KB)
    ang, turns = put("ang", S, at=g1 + 12 * KB), put("turns", S, at=g1 + 14 * KB)
    b_k, b_v = put("b_k", 8 * S, at=g0 + 20 * KB), put("b_v", NB * 256, at=g0 + 36 * KB)
    f_hi = [put("fk_hi", 4 * FPAD, f32r, at=g0), put("fv_hi", 4 * FPAD, f32r, at=g0 + 16 * FPAD)]
    f_lo = [put("fk_lo", 4 * FPAD, f32r, at=g1), put("fv_lo", 4 * FPAD, f32r, at=g1 + 16 * FPAD)]
    n_k = {"slc": put("n_ks", 8 * S, at=g0 + 18 * KB), "win": put("n_kw", 8 * S, at=g1 + 18 * KB)}
    n_v = {"slc": put("n_vs", NB * 256, at=g0 + 34 * KB), "win": put("n_vw", NB * 256, at=g0 + 38 * KB)}
    cmp_k, cmp_v = put("cmp_k", 2 * 4 * NCMP, at=g0 + 42 * KB), put("cmp_v", 4 * 64, at=g0 + 43 * KB)
    gate = put("gate", NB * 48, at=g1 + 34 * KB)
    hidx, hidt = put("hidx", P, at=g1 + 36 * KB), put("hidt", P, at=g1 + 36 * KB + 512)
    hidf = put("hidf", 4 * P, at=g1 + 37 * KB)
    hid_hi, hid_lo = put("hid_hi", 4 * P, f32r, at=g1 + 39 * KB), put("hid_lo", 4 * P, f32r, at=g1 + 41 * KB)
    pos_hi, pos_lo = put("pos_hi", 36, f32r, at=g1 + 43 * KB), put("pos_lo", 36, f32r, at=g1 + 43 * KB + 256)
    hb = put("hb", 4, at=g1 + 43 * KB + 512)
    zsil = put("zsil", 8 * S, at=g1)
    mem_k, mem_v = [mem_k0, mem_k1], [mem_v0, mem_v1]

    ident = cst[:, CC["ident"]:CC["ident"] + P]

    def V(name, k=0):
        return vec[:, VC[name] + k:VC[name] + k + 1]

    def VD(name, k):
        return vec[:, ds(k + VC[name], 1)]

    def C(name, k=0, n=1):
        return cst[:, CC[name] + k:CC[name] + k + n]

    def causal(b):
        return C("causal", (NB - 1 - b) * P, (b + 1) * P)

    def ST(k, par):
        return stats[:, 2 * k + par:2 * k + par + 1]

    MX, MMX, NEGM, LSUM, ESINK, LTOT, RL = range(7)

    with ExitStack() as ctx:
        def sem(name):
            return ctx.enter_context(nc.semaphore(name))

        def bank(name):
            return ctx.enter_context(nc.psum_tensor(name, [P, 512], f32))

        pj = [bank("pj0"), bank("pj1")]
        ps = [bank("ps0"), bank("ps1")]
        pt = [bank("pt0"), bank("pt1")]
        po, px = bank("po"), bank("px")

        ld = {n: sem(f"loaded_{n}") for n in ("mem", "x", "vec", "cst", "pos", "tab2")}
        chunk_loaded = [sem("chunk_loaded0"), sem("chunk_loaded1")]
        hi_ready = sem("hi_ready")
        lo_ready = sem("lo_ready")
        chunk_used = sem("chunk_used")
        pj_free = [sem("pj_free0"), sem("pj_free1")]
        setup = sem("setup")
        x_ready = sem("x_ready")
        sq_ready, sq_used = sem("sq_ready"), sem("sq_used")
        var_ready, rs_ready = sem("var_ready"), sem("rs_ready")
        diag_ready, factor_ready = sem("diag_ready"), sem("factor_ready")
        hf_ready, hhi_ready, h_ready = sem("hf_ready"), sem("hhi_ready"), sem("h_ready")
        score_done, score_taken = sem("score_done"), sem("score_taken")
        idx_added = sem("idx_added")
        max_ready, exp_done, p_ready = sem("max_ready"), sem("exp_done"), sem("p_ready")
        p_turned, pT_ready, pv_done = sem("p_turned"), sem("pT_ready"), sem("pv_done")
        o_copied, o_turned = sem("o_copied"), sem("o_turned")
        out_hi, out_ready = sem("out_hi"), sem("out_ready")
        y_ready = sem("y_ready")
        roped = sem("roped")
        v_turned = sem("v_turned")
        act_ready, g_hi_ready, g_ready = sem("act_ready"), sem("g_hi_ready"), sem("g_ready")
        f_hi_ready, f_hi_done, f_ready = sem("f_hi_ready"), sem("f_hi_done"), sem("f_ready")
        pos_hi_ready, pos_ready = sem("pos_hi_ready"), sem("pos_ready")
        hid_x, hid_th, hid_f, hid_hi_ready, hid_ready = (
            sem(n) for n in ("hid_x", "hid_th", "hid_f", "hid_hi_ready", "hid_ready"))
        gate_done = sem("gate_done")
        zeroed = sem("zeroed")
        dve_step = sem("dve_step")
        angle_ready, sin_ready = sem("angle_ready"), sem("sin_ready")
        settled = sem("settled")
        stored = sem("stored")

        block = ctx.enter_context(nc.Block())

        @block.sync
        def _(sp):
            sp.dma_start(memT[:, :], memin).then_inc(ld["mem"], 16)
            sp.dma_start(vec[:, :], vecin).then_inc(ld["vec"], 16)
            sp.dma_start(cst[:, :], cstin).then_inc(ld["cst"], 16)
            sp.dma_start(posi[:, :], posin).then_inc(ld["pos"], 16)
            sp.dma_start(xT[:, :], xin).then_inc(ld["x"], 16)
            with sp.Fori(0, NCHUNKS // 2) as i:
                for par in range(2):
                    c = At(par, i, 2)
                    sp.wait_ge(lo_ready, c.v + 1)
                    sp.dma_start(raw[:, par * CW:(par + 1) * CW],
                                 wstream[ds(c.v, 1), :, :].rearrange("a p c -> p (a c)")).then_inc(chunk_loaded[par], 16)
            sp.wait_ge(h_ready, NBASE[-1])
            sp.dma_start(out, xT[:, :]).then_inc(stored, 16)
            sp.wait_ge(stored, 16)

        NORM = {
            "mem": (memT, MEM, "g_mem", 0, memn_hi, memn_lo), "amix": (xT, S, "g_mix", 0, h_hi, h_lo),
            "ckv": (ckv, S, "a_kv_norm", 0, c_hi, c_lo), "affn": (xT, S, "g_ffn", 0, h_hi, h_lo),
            "bmix": (xT, S, "g_mix", DT, h_hi, h_lo), "bffn": (xT, S, "g_ffn", DT, h_hi, h_lo),
            "final1": (xT, S, "g_final", 0, None, None), "conv": (xT, S, "a_norm", 0, h_hi, h_lo),
            "kv2": (xT, S, "kv_norm", 0, h_hi, h_lo), "q2": (xT, S, "b_norm", 0, h_hi, h_lo),
            "final2": (xT, S, "final_norm", 0, None, None)}
        SUMS = [ps[0], ps[1], pt[0], pt[1]]

        def settle(eng):
            eng.sem_inc(settled, 1)

        def sl(start, n):
            return slice(start, start + n) if isinstance(start, int) else ds(start, n)

        def attention_tiles(eng, ph, tile, links=None, per=0):
            trips = ph.tiles // 2 - 1
            if trips:
                with eng.Fori(0, trips) as i:
                    if links:
                        links.begin(i, per)
                    for j in range(2):
                        tile(ph, i, j, True)
                if links:
                    links.end(per, trips)
            tile(ph, trips, 0, True)
            tile(ph, trips, 1, False)

        def next_chunk(ph, i, j, c):
            return At(CH[ph.name] + (j + 1) * ph.chunks + c, i, 2 * ph.chunks)

        def next_tile(ph, i, j, k):
            per = 3 if ph.name == "aq" else ph.chunks
            return At(TL[ph.name] + (j + 1) * per + k, i, 2 * per)

        @block.gpsimd
        def _(pool):
            nc.gpsimd.memset(ones[:, :], 1.0)
            nc.gpsimd.memset(mhalf[:, :], -0.5)
            nc.gpsimd.memset(score[:, :], 0.0)
            nc.gpsimd.memset(v4[:, :], 1.0).then_inc(setup, 1)

            def inverse_root(name):
                q = NQ[name]
                pool.wait_ge(var_ready, q + 1)
                nc.gpsimd.tensor_tensor(r4[:, :], v4[:, :], mhalf[:, :], ALU.pow).then_inc(rs_ready, 1)

            pool.wait_ge(setup, 1)
            for name in ("mem", "amix", "ckv", "affn"):
                inverse_root(name)
            pool.wait_ge(x_ready, RESIDUALS["down0"] + DT)
            nc.gpsimd.memset(b_k[:, :], 0.0).then_inc(zeroed, 1)
            inverse_root("bmix")
            pool.wait_ge(roped, RP["nk_s"] + 1)
            pool.dma_start(tab64[:, :], tab2in).then_inc(ld["tab2"], 16)
            for name in ("bffn", "final1", "conv"):
                inverse_root(name)
            pool.wait_ge(x_ready, RESIDUALS["cout"] + DT)
            for tile in (*f_hi, *f_lo):
                nc.gpsimd.memset(tile[:, :].bitcast(f32), 0.0)
            nc.gpsimd.memset(n_k["win"][:, :], 0.0)
            nc.gpsimd.memset(n_k["slc"][:, :], 0.0).then_inc(zeroed, 1)
            for name in ("kv2", "q2", "final2"):
                inverse_root(name)

        @block.scalar
        def _(act):
            act.sem_inc(sq_used, 2)

            def split_hi(c):
                if isinstance(c.v, int) and c.v >= NCHUNKS:
                    return
                act.wait_ge(chunk_loaded[c.par], c.half * 16 + 16)
                act.wait_ge(chunk_used, c.v + 1)
                nc.scalar.activation(w_hi[:, c.par * CW:(c.par + 1) * CW], raw[:, c.par * CW:(c.par + 1) * CW],
                                     ACT.Copy).then_inc(hi_ready, 1)

            def take(dst, t, c, n=S, func=ACT.Copy, scale=1.0, rows=slice(0, P)):
                act.wait_ge(chunk_used, c.v + 3)
                nc.scalar.activation(dst, pj[t.par][rows, 0:n], func, scale=scale).then_inc(pj_free[t.par], 1)

            def norm(name, waits):
                src, n, _, _, hi, _ = NORM[name]
                q = NQ[name]
                k = NORMS[q][1]
                for m in range(k):
                    s = NBASE[q] + m
                    sem_, value = waits(m)
                    act.wait_ge(sem_, value)
                    act.wait_ge(sq_used, s + 1)
                    nc.scalar.activation(sq[:, (s % 2) * S:(s % 2) * S + n], src[:, m * n:(m + 1) * n],
                                         ACT.Square).then_inc(sq_ready, 1)
                if hi is None:
                    return
                for m in range(k):
                    s = SBASE[q] + m
                    act.wait_ge(hf_ready, s + 1)
                    nc.scalar.activation(hi[:, m * n:(m + 1) * n], hf[:, (s % 2) * S:(s % 2) * S + n],
                                         ACT.Copy).then_inc(hhi_ready, 1)

            def after(name):
                return lambda m: (x_ready, RESIDUALS[name] + m + 1)

            def turn(t, c, number, dst, src, n=S, func=ACT.Copy, scale=1.0):
                take(vraw[:, 0:n], t, c, n)
                act.wait_ge(v_turned, number + 1)
                return nc.scalar.activation(dst, src, func, scale=scale)

            def bank3(number, lo, n):
                return pt[number % 2][:, :].rearrange("p (b c) -> p b c", b=NB)[:, :, lo:lo + n]

            def query(ph, i, j, first=False):
                c, t = next_chunk(ph, i, j, 0), next_tile(ph, i, j, 0)
                par = (j + 1) % 2
                split_hi(c + 2)
                if ph.units[0][2] == "mem":
                    take(qs[:, par * S:(par + 1) * S], t, c)
                else:
                    r = RP[ph.name] + 1 + j + i * 2
                    act.wait_ge(roped, r + 1)
                    dst = qn[:, par * S:(par + 1) * S] if ph.name == "nq" else qraw[:, :]
                    take(dst, t, c)
                if ph.name == "aq":
                    split_hi(c + 3)
                    take(a_k[0:96, par * S:(par + 1) * S], t + 1, c + 1, rows=slice(0, 96))
                    take(a_v[:, par * S:(par + 1) * S], t + 2, c + 1)

            def tile(ph, i, j, more):
                t = i * 2 + j
                sink = ph.units[0][2] == "band"

                def softmax(u):
                    a = ph.first_unit + t * ph.n + u
                    par = u % 2
                    w = ph.keys(u)[1]
                    act.wait_ge(max_ready, a + 1)
                    act.wait_ge(p_turned, a + 1)
                    if sink:
                        h = t * 2 + ph.units[u][0]
                        settle(act)
                        nc.scalar.activation(ST(ESINK, par), nsink[:, sl(h, 1)], ACT.Exp, scale=-1.0, bias=ST(NEGM, par))
                    nc.scalar.activation(p_sb[:, par * S:par * S + w], s_sb[:, par * S:par * S + w], ACT.Exp,
                                         scale=ph.scale, bias=ST(NEGM, par),
                                         accum_out=ST(LSUM, par)).then_inc(exp_done, 1)

                def bring(u):
                    a = ph.first_unit + t * ph.n + u
                    par = u % 2
                    w = ph.keys(u)[1]
                    act.wait_ge(p_turned, a + 3)
                    act.wait_ge(pv_done, a + 1)
                    rows = slice(0, min(w, P))
                    n = max(w, P)
                    nc.scalar.activation(pT[rows, par * S:par * S + n], pt[par][rows, 0:n],
                                         ACT.Copy).then_inc(pT_ready, 1)

                softmax(0)
                softmax(1)
                for u in range(ph.n):
                    bring(u)
                    if u == 1 and more:
                        query(ph, i, j)
                    if u + 2 < ph.n:
                        softmax(u + 2)
                k = ph.first_tile + t
                act.wait_ge(pv_done, ph.first_unit + t * ph.n + ph.n - 1 + 3)
                act.wait_ge(o_turned, k + 1)
                nc.scalar.activation(o_sb[:, :], po[:, :], ACT.Copy).then_inc(o_copied, 1)
                o = (ph.out0 + t) * S
                if ph.name == "nq":
                    act.wait_ge(y_ready, t + 1)
                    src = ysb
                else:
                    act.wait_ge(o_turned, k + 2)
                    src = px
                settle(act)
                nc.scalar.activation(G_hi[:, sl(o, S)], src[:, :], ACT.Copy).then_inc(out_hi, 1)

            def attention(name):
                ph = ATT[name]
                query(ph, 0, -1)
                attention_tiles(act, ph, tile)

            def splits(stage, per, trips):
                with act.Fori(0, trips) as i:
                    for k in range(per):
                        split_hi(At(CH[stage] + k + 2, i, per))

            def feed_forward(l):
                up, base = CH[f"up{l}"], TL[f"up{l}"]
                with act.Fori(0, FT) as i:
                    split_hi(At(up + 2, i, 2))
                    t = At(base, i, 2)
                    act.wait_ge(pj_free[t.par], t.half + 2)
                    nc.scalar.activation(fb[:, :], fa[:, :], ACT.Silu).then_inc(act_ready, 1)
                    split_hi(At(up + 3, i, 2))
                    t = At(base + 1, i, 2)
                    act.wait_ge(pj_free[t.par], t.half + 2)
                    settle(act)
                    nc.scalar.activation(G_hi[:, ds(i * S, S)], fc[:, :], ACT.Copy).then_inc(g_hi_ready, 1)
                splits(f"down{l}", 2 * DOWN_CHUNKS, DT // 2)

            split_hi(At(0))
            split_hi(At(1))
            norm("mem", lambda m: (ld["mem"], 16))
            number = TN["memv"]
            for l in range(2):
                for k in range(4):
                    c, t = At(CH["mem"] + 4 * l + k), At(TL["mem"] + 4 * l + k)
                    split_hi(c + 2)
                    if k >= 2:
                        turn(t, c, number, mem_v[l][:, :].rearrange("p (b c) -> p b c", b=2)[:, :, (k - 2) * P:(k - 1) * P],
                             pt[number % 2][:, 0:MEM].rearrange("p (b c) -> p b c", b=2), n=MEM)
                        number += 1
            for k, tab in enumerate((tab64, tab128)):
                act.wait_ge(angle_ready, k + 1)
                nc.scalar.activation(tab[:, S:2 * S], ang[:, :], ACT.Sin)
                nc.scalar.activation(tab[:, 0:S], turns[:, :], ACT.Sin).then_inc(sin_ready, 1)
            norm("amix", lambda m: (ld["x"], 16))
            for k in range(4):
                c, t = At(CH["afront"] + k), At(TL["afront"] + k)
                split_hi(c + 2)
                if k < 2:
                    take(ckv[:, k * S:(k + 1) * S], t, c)
                elif k == 2:
                    act.wait_ge(roped, RP["krope"] + 1)
                    take(qraw[:, :], t, c)
                    act.wait_ge(v_turned, TN["widx"] + 1)
                    nc.scalar.activation(widx[:, :].rearrange("p (b c) -> p b c", b=NB), bank3(TN["widx"], 0, 16),
                                         ACT.Copy, scale=1024.0 ** -0.5)
                else:
                    act.wait_ge(roped, RP["kidx"] + 1)
                    take(qraw[:, :], t, c)
            tk = TL["afront"]
            act.wait_ge(roped, RP["idx"] + 1)
            norm("ckv", lambda m: (pj_free[(tk + m) % 2], (tk + m) // 2 + 2))

            def idx_query(i, j):
                c, t = At(CH["idx"] + 1 + j, i, 2), At(TL["idx"] + 1 + j, i, 2)
                split_hi(c + 2)
                act.wait_ge(roped, RP["idx"] + 1 + j + i * 2 + 1)
                take(qraw[:, :], t, c)

            def idx_tile(i, j, more):
                t = i * 2 + j
                for u, (hh, b) in enumerate(IDX_UNITS):
                    s = t * len(IDX_UNITS) + u
                    w = (b + 1) * P
                    act.wait_ge(score_done, s + 1)
                    act.wait_ge(idx_added, s + 1)
                    nc.scalar.activation(s_sb[:, (u % 2) * S:(u % 2) * S + w], ps[u % 2][:, 0:w],
                                         ACT.Relu).then_inc(score_taken, 1)
                    if u == 1 and more:
                        idx_query(i, j)

            idx_query(0, -1)
            with act.Fori(0, 3) as i:
                idx_tile(i, 0, True)
                idx_tile(i, 1, True)
            idx_tile(3, 0, True)
            idx_tile(3, 1, False)
            attention("aq")
            attention("amem")
            splits("aout", 4, DT // 2)
            norm("affn", after("aout"))
            feed_forward(0)

            norm("bmix", after("down0"))
            for k in range(2):
                c, t = At(CH["bfront"] + k), At(TL["bfront"] + k)
                split_hi(c + 2)
                act.wait_ge(roped, RP["bk"] + k + 1)
                take(qraw[:, :], t, c)
            for k in range(2):
                c, t = At(CH["bfront"] + 2 + k), At(TL["bfront"] + 2 + k)
                split_hi(c + 2)
                turn(t, c, TN["bv"] + k, b_v[:, :].rearrange("p (b c) -> p b c", b=NB)[:, :, k * P:(k + 1) * P],
                     bank3(TN["bv"] + k, 0, P))
            attention("bq")
            attention("bmem")
            splits("bout", 4, DT // 2)
            norm("bffn", after("bout"))
            feed_forward(1)
            norm("final1", after("down1"))

            norm("conv", lambda m: (h_ready, NBASE[NQ["final1"]] + m + 1))
            with act.Fori(0, CT) as i:
                c, t = At(CH["conv"], i, 4), At(TL["conv"], i, 4)
                split_hi(c + 2)
                take(fa[:, :], t, c)
                split_hi(c + 3)
                split_hi(c + 4)
                take(fd[:, :], t + 2, c + 2, func=ACT.Silu)
                split_hi(c + 5)
                act.wait_ge(pj_free[(t + 3).par], (t + 3).half + 2)
                settle(act)
                nc.scalar.activation(G_hi[:, ds(i * S, S)], fg[:, :], ACT.Copy).then_inc(g_hi_ready, 1)
            splits("cout", 4, DT // 2)
            norm("kv2", after("cout"))

            act.wait_ge(ld["vec"], 16)
            nc.scalar.activation(pos_hi[:, :], vec[:, VC["pos_k"]:VC["pos_k"] + 36], ACT.Copy).then_inc(pos_hi_ready, 1)
            act.wait_ge(zeroed, 2)
            for k in range(4):
                c, t = At(CH["cmp_kv"] + k), At(TL["cmp_kv"] + k)
                which, pair = k // 2, k % 2
                split_hi(c + 2)
                if k:
                    act.wait_ge(f_ready, k)
                act.wait_ge(chunk_used, c.v + 3)
                nc.scalar.activation(fraw[0:64, 0:S], pj[t.par][0:64, :], ACT.Copy)
                take(fraw[0:64, S:2 * S], t, c, rows=slice(64, P))
                act.wait_ge(pj_free[t.par], t.half + 2)
                low = f_hi[which][0:64, 2 * pair * FPAD:2 * (pair + 1) * FPAD].rearrange("p (g c) -> p g c", g=2)
                high = f_hi[which][64:P, 2 * pair * FPAD:2 * (pair + 1) * FPAD].rearrange("p (g c) -> p g c", g=2)
                nc.scalar.activation(low[:, :, 0:S], fraw[0:64, :].rearrange("p (g c) -> p g c", g=2),
                                     ACT.Copy).then_inc(f_hi_ready, 1)
                nc.scalar.activation(high[:, :, 0:S - 1], fraw[0:64, :].rearrange("p (g c) -> p g c", g=2)[:, :, 1:S],
                                     ACT.Copy).then_inc(f_hi_done, 1)
            for k in range(4):
                c = At(CH["cmp"] + 2 * k)
                split_hi(c + 2)
                split_hi(c + 3)
                act.wait_ge(hid_x, k + 1)
                nc.scalar.activation(hidt[:, :], hidt[:, :], ACT.Tanh, scale=0.7978845608028654).then_inc(hid_th, 1)
                act.wait_ge(hid_f, k + 1)
                nc.scalar.activation(hid_hi[:, k * P:(k + 1) * P], hidf[:, k * P:(k + 1) * P],
                                     ACT.Copy).then_inc(hid_hi_ready, 1)
            c, t = At(CH["cmp"] + 8), At(TL["cmp"] + 5)
            split_hi(c + 2)
            turn(t, c, TN["cmpv"], cmp_v[0:NCMP, :].rearrange("p (g c) -> p g c", g=4),
                 pt[TN["cmpv"] % 2][0:NCMP, :].rearrange("p (g c) -> p g c", g=4)[:, :, 0:64], n=P)

            for s, (kn, vn, branch) in enumerate((("nk_s", "nv_s", "slc"), ("nk_w", "nv_w", "win"))):
                for k in range(2):
                    c, t = At(CH["nkv"] + 4 * s + k), At(TL["nkv"] + 4 * s + k)
                    split_hi(c + 2)
                    act.wait_ge(roped, RP[kn] + k + 1)
                    take(qraw[:, :], t, c)
                for k in range(2):
                    c, t = At(CH["nkv"] + 4 * s + 2 + k), At(TL["nkv"] + 4 * s + 2 + k)
                    split_hi(c + 2)
                    turn(t, c, TN[vn] + k,
                         n_v[branch][:, :].rearrange("p (b c) -> p b c", b=NB)[:, :, k * P:(k + 1) * P],
                         bank3(TN[vn] + k, 0, P))
            act.wait_ge(roped, RP["nq"] + 1)
            norm("q2", after("cout"))
            c, t = At(CH["gates"]), At(TL["gates"])
            split_hi(c + 2)
            turn(t, c, TN["gates"], gate[:, :].rearrange("p (b c) -> p b c", b=NB), bank3(TN["gates"], 0, 48),
                 func=ACT.Sigmoid).then_inc(gate_done, 1)
            with act.Fori(0, 4) as i:
                for k in range(2):
                    c, t = At(CH["nz"] + k, i, 2), At(TL["nz"] + k, i, 2)
                    split_hi(c + 2)
                    take(zsil[:, ds((i * 2 + k) * S, S)], t, c, func=ACT.Silu)
            attention("nq")
            with act.Fori(0, DT // 2 - 1) as i:
                for k in range(2):
                    split_hi(At(CH["nout"] + k + 2, i, 2))
            norm("final2", after("nout"))

        @block.vector
        def _(dve):
            link = Links(dve, dve_step)
            for b in range(2):
                dve.sem_inc(pj_free[b], 1)
            dve.sem_inc(lo_ready, 2)
            dve.sem_inc(score_taken, 2)
            dve.sem_inc(idx_added, 2)
            dve.sem_inc(roped, 1)
            dve.sem_inc(out_ready, 1)
            dve.sem_inc(g_ready, 1)
            dve.wait_ge(setup, 1)

            def split_lo(c):
                if isinstance(c.v, int) and c.v >= NCHUNKS:
                    return
                dve.wait_ge(hi_ready, c.v + 1)
                here = slice(c.par * CW, (c.par + 1) * CW)
                nc.vector.tensor_tensor(w_lo[:, here], raw[:, here], w_hi[:, here].bitcast(f32),
                                        ALU.subtract).then_inc(lo_ready, 1)

            def complete(c):
                dve.wait_ge(chunk_used, c.v + 3)

            def norm(name):
                src, n, gain, first, hi, lo = NORM[name]
                q = NQ[name]
                k = NORMS[q][1]
                blocks = n // P
                dve.wait_ge(sq_used, NBASE[q + 1] + 2)
                for b in range(blocks):
                    last = nc.vector.tensor_scalar(v4[:, b:b + 1], SUMS[b][:, 0:1], 1.0 / (k * P), EPS, ALU.mult, ALU.add)
                last.then_inc(var_ready, 1)
                dve.wait_ge(rs_ready, q + 1)
                for b in range(blocks):
                    last = nc.vector.tensor_scalar(diag[:, b * P:(b + 1) * P], ident, r4[:, b:b + 1], None, ALU.mult)
                last.then_inc(diag_ready, 1)
                dve.wait_ge(factor_ready, q + 1)

                def low(m):
                    s = SBASE[q] + m
                    dve.wait_ge(hhi_ready, s + 1)
                    here = slice(m * n, (m + 1) * n)
                    nc.vector.tensor_tensor(lo[:, here], hf[:, (s % 2) * S:(s % 2) * S + n], hi[:, here].bitcast(f32),
                                            ALU.subtract).then_inc(h_ready, 1)

                for m in range(k):
                    here = slice(m * n, (m + 1) * n)
                    if hi is None:
                        nc.vector.scalar_tensor_tensor(out=src[:, here], in0=src[:, here], scalar=V(gain, first + m),
                                                       in1=px[:, 0:n], op0=ALU.mult, op1=ALU.mult).then_inc(h_ready, 1)
                        continue
                    s = SBASE[q] + m
                    if m >= 2:
                        dve.wait_ge(h_ready, NBASE[q] + m - 1)
                    nc.vector.scalar_tensor_tensor(out=hf[:, (s % 2) * S:(s % 2) * S + n], in0=src[:, here],
                                                   scalar=V(gain, first + m), in1=px[:, 0:n],
                                                   op0=ALU.mult, op1=ALU.mult).then_inc(hf_ready, 1)
                    if m:
                        low(m - 1)
                if hi is not None:
                    low(k - 1)
                dve.wait_ge(h_ready, NBASE[q + 1])

            def rope(dst, src, tab, mask, t):
                dve.wait_ge(pj_free[t.par], t.half + 2)
                nc.vector.tensor_tensor(dst, src, tab[:, 0:S], ALU.mult)
                link(nc.vector.stream_shuffle(rtmp[:, :], src, mask))
                link(nc.vector.tensor_tensor(rtmp[:, :], rtmp[:, :], tab[:, S:2 * S], ALU.mult))
                return nc.vector.tensor_tensor(dst, dst, rtmp[:, :], ALU.add)

            def spread_keys(dst, pair):
                for g in range(2):
                    for hh in range(2):
                        col = ((2 * pair + g) * 2 + hh) * S
                        last = nc.vector.tensor_copy(dst[hh * 64:hh * 64 + 64, col:col + S], ktmp[g * 64:g * 64 + 64, 0:S])
                return last

            def query(ph, i, j):
                c, t = next_chunk(ph, i, j, 0), next_tile(ph, i, j, 0)
                par = (j + 1) % 2
                split_lo(c + 2)
                if ph.units[0][2] != "mem":
                    src = qn[:, par * S:(par + 1) * S] if ph.name == "nq" else qraw[:, :]
                    tab, mask = (tab128, SHUF128) if ph.name == "aq" else (tab64, SHUF64)
                    rope(qs[:, par * S:(par + 1) * S], src, tab, mask, t).then_inc(roped, 1)
                if ph.name == "aq":
                    split_lo(c + 3)

            def bias(ph, u):
                _, b, branch = ph.units[u]
                if branch == "topk" and b:
                    return bias_a[:, (b - 1) * S:(b - 1) * S + (b + 1) * P]
                if branch == "mem":
                    return C("causal", 0, MEM)
                if branch == "band":
                    return C("band", P, P) if b == 0 else C("band", 0, 2 * P)
                if branch == "cmp":
                    return C("cmp", b * NCMP, NCMP)
                return causal(b)

            def tile(ph, i, j, more):
                t = i * 2 + j
                sink = ph.units[0][2] == "band"

                def maximum(u):
                    s, a = ph.first_score + t * ph.n + u, ph.first_unit + t * ph.n + u
                    par = u % 2
                    w = ph.keys(u)[1]
                    dve.wait_ge(score_done, s + 1)
                    dve.wait_ge(exp_done, a + 1)
                    settle(dve)
                    nc.vector.tensor_tensor_reduce(out=s_sb[:, par * S:par * S + w], in0=ps[par][:, 0:w], in1=bias(ph, u),
                                                   scale=1.0, scalar=-3.0e38, op0=ALU.add, op1=ALU.max,
                                                   accum_out=ST(MX, par)).then_inc(score_taken, 1)
                    dve.wait_ge(score_taken, s + 3)
                    if sink:
                        h = t * 2 + ph.units[u][0]
                        nc.vector.tensor_scalar(ST(NEGM, par), ST(MX, par), -ph.scale, nsink[:, sl(h, 1)],
                                                ALU.mult, ALU.min).then_inc(max_ready, 1)
                    else:
                        nc.vector.tensor_scalar(ST(NEGM, par), ST(MX, par), -ph.scale, None, ALU.mult).then_inc(max_ready, 1)

                def normalise(u):
                    a = ph.first_unit + t * ph.n + u
                    par = u % 2
                    w = ph.keys(u)[1]
                    hh, b, branch = ph.units[u]
                    dve.wait_ge(exp_done, a + 3)
                    total = ST(LSUM, par)
                    if sink:
                        total = ST(LTOT, par)
                        link(nc.vector.tensor_tensor(total, ST(LSUM, par), ST(ESINK, par), ALU.add))
                    link(nc.vector.reciprocal(ST(RL, par), total))
                    p = p_sb[:, par * S:par * S + w]
                    if ph.name == "nq":
                        col = b * 48 + t * 6 + hh * 3 + ("cmp", "slc", "win").index(branch)
                        nc.vector.tensor_scalar(p, p, ST(RL, par), gate[:, sl(col, 1)], ALU.mult,
                                                ALU.mult).then_inc(p_ready, 1)
                    else:
                        nc.vector.tensor_scalar(p, p, ST(RL, par), None, ALU.mult).then_inc(p_ready, 1)

                maximum(0)
                maximum(1)
                normalise(0)
                normalise(1)
                for u in range(2, ph.n):
                    maximum(u)
                    if u > 2:
                        normalise(u - 1)
                    elif more:
                        query(ph, i, j)
                normalise(ph.n - 1)
                k = ph.first_tile + t
                o = (ph.out0 + t) * S
                src = px
                if ph.name == "nq":
                    dve.wait_ge(o_turned, k + 2)
                    nc.vector.tensor_tensor(ysb[:, :], px[:, :], zsil[:, sl(t * S, S)], ALU.mult).then_inc(y_ready, 1)
                    src = ysb
                dve.wait_ge(out_hi, k + 1)
                nc.vector.tensor_tensor(G_lo[:, sl(o, S)], src[:, :], G_hi[:, sl(o, S)].bitcast(f32),
                                        ALU.subtract).then_inc(out_ready, 1)

            LINKS = {"aq": 2 * (2 + 4), "amem": 0, "bq": 2 * (2 + 2 * 8), "bmem": 0, "nq": 2 * (2 + 24)}

            def attention(name):
                ph = ATT[name]
                query(ph, 0, -1)
                attention_tiles(dve, ph, tile, link, LINKS[name])

            def residual(stage, per):
                def two(i, last=False):
                    for j in range(2):
                        for k in range(per):
                            split_lo(At(CH[stage] + j * per + k + 2, i, 2 * per))
                        c, t = At(CH[stage] + (j + 1) * per - 1, i, 2 * per), At(TL[stage] + j, i, 2)
                        complete(c)
                        here = xT[:, sl((i * 2 + j) * S, S)]
                        nc.vector.tensor_tensor(here, here, pj[t.par][:, :], ALU.add).then_inc(pj_free[t.par], 1)
                        dve.wait_ge(pj_free[t.par], t.half + 2)
                        dve.sem_inc(x_ready, 1)

                trips = DT // 2 - (1 if stage == "nout" else 0)
                with dve.Fori(0, trips) as i:
                    two(i)
                if stage == "nout":
                    two(trips)

            def feed_forward(l):
                up, base = CH[f"up{l}"], TL[f"up{l}"]
                with dve.Fori(0, FT) as i:
                    link.begin(i, 2)
                    c, t = At(up, i, 2), At(base, i, 2)
                    split_lo(c + 2)
                    complete(c)
                    w = [VD("f_conv_w", i + (l * 3 + j) * FT) for j in range(3)]
                    a = pj[t.par]
                    link(nc.vector.tensor_scalar(fa[:, :], a[:, :], w[2], VD("f_conv_b", i + l * FT), ALU.mult, ALU.add))
                    link(nc.vector.scalar_tensor_tensor(out=fa[:, 1:S], in0=a[:, 0:S - 1], scalar=w[1], in1=fa[:, 1:S],
                                                        op0=ALU.mult, op1=ALU.add))
                    nc.vector.scalar_tensor_tensor(out=fa[:, 2:S], in0=a[:, 0:S - 2], scalar=w[0], in1=fa[:, 2:S],
                                                   op0=ALU.mult, op1=ALU.add).then_inc(pj_free[t.par], 1)
                    split_lo(c + 3)
                    complete(c + 1)
                    dve.wait_ge(act_ready, i + (l * FT + 1))
                    dve.wait_ge(g_ready, i + (l * FT + 1))
                    nc.vector.tensor_tensor(fc[:, :], fb[:, :], pj[(t + 1).par][:, :],
                                            ALU.mult).then_inc(pj_free[(t + 1).par], 1)
                    dve.wait_ge(g_hi_ready, i + (l * FT + 1))
                    nc.vector.tensor_tensor(G_lo[:, ds(i * S, S)], fc[:, :], G_hi[:, ds(i * S, S)].bitcast(f32),
                                            ALU.subtract).then_inc(g_ready, 1)
                link.end(2, FT)
                residual(f"down{l}", DOWN_CHUNKS)

            split_lo(At(0))
            split_lo(At(1))
            dve.wait_ge(ld["cst"], 16)
            dve.wait_ge(ld["vec"], 16)
            nc.vector.tensor_scalar(nsink[:, :], vec[:, VC["sinks"]:VC["sinks"] + 16], -1.0, None, ALU.mult)
            norm("mem")
            for l in range(2):
                for k in range(4):
                    c, t = At(CH["mem"] + 4 * l + k), At(TL["mem"] + 4 * l + k)
                    split_lo(c + 2)
                    if k < 2:
                        complete(c)
                        for hh in range(2):
                            last = nc.vector.tensor_scalar(mem_k[l][:, (2 * k + hh) * MEM:(2 * k + hh + 1) * MEM],
                                                           pj[t.par][:, 0:MEM], C("half", hh), None, ALU.mult)
                        last.then_inc(pj_free[t.par], 1)
            dve.wait_ge(ld["pos"], 16)
            link(nc.vector.tensor_copy(posf[:, :], posi[:, :]))
            for k, (width, tab) in enumerate((("64", tab64), ("128", tab128))):
                if k:
                    dve.wait_ge(sin_ready, k)
                link(nc.vector.tensor_scalar(ang[:, :], posf[:, :], C("inv" + width), None, ALU.mult))
                link(nc.vector.tensor_scalar(turns[:, :], ang[:, :], 1.0 / TWO_PI, ROUNDER, ALU.mult, ALU.add))
                link(nc.vector.tensor_scalar(turns[:, :], turns[:, :], ROUNDER, None, ALU.subtract))
                for part in (PI_HI, PI_LO):
                    link(nc.vector.scalar_tensor_tensor(out=ang[:, :], in0=turns[:, :], scalar=-part, in1=ang[:, :],
                                                        op0=ALU.mult, op1=ALU.add))
                link(nc.vector.tensor_scalar(ang[:, :], ang[:, :], 3.1415925, -3.1415925, ALU.min, ALU.max))
                link(nc.vector.scalar_tensor_tensor(out=turns[:, :], in0=ang[:, :], scalar=-1.0, in1=ang[:, :],
                                                    op0=ALU.mult, op1=ALU.max))
                nc.vector.tensor_scalar(turns[:, :], turns[:, :], -1.0, TWO_PI / 4, ALU.mult,
                                        ALU.add).then_inc(angle_ready, 1)
            for k, (width, tab) in enumerate((("64", tab64), ("128", tab128))):
                dve.wait_ge(sin_ready, k + 1)
                link(nc.vector.tensor_scalar(tab[:, S:2 * S], tab[:, S:2 * S], C("sgn" + width), None, ALU.mult))
            norm("amix")
            for k in range(4):
                c, t = At(CH["afront"] + k), At(TL["afront"] + k)
                split_lo(c + 2)
                if k == 2:
                    link(rope(ktmp[:, 0:S], qraw[:, :], tab128, SHUF128, t))
                    for par in range(2):
                        last = nc.vector.tensor_copy(a_k[96:P, par * S:(par + 1) * S], ktmp[96:P, 0:S])
                    last.then_inc(roped, 1)
                if k == 3:
                    link(rope(ktmp[:, S:2 * S], qraw[:, :], tab64, SHUF64, t))
                    for hh in range(2):
                        last = nc.vector.tensor_scalar(kidx[:, hh * S:(hh + 1) * S], ktmp[:, S:2 * S], C("half", hh), None,
                                                       ALU.mult)
                    last.then_inc(roped, 1)
            norm("ckv")

            def idx_query(i, j):
                c, t = At(CH["idx"] + 1 + j, i, 2), At(TL["idx"] + 1 + j, i, 2)
                par = (j + 1) % 2
                split_lo(c + 2)
                rope(qs[:, par * S:(par + 1) * S], qraw[:, :], tab64, SHUF64, t).then_inc(roped, 1)

            def idx_tile(i, j, more):
                t = i * 2 + j
                for u, (hh, b) in enumerate(IDX_UNITS):
                    s = t * len(IDX_UNITS) + u
                    w = (b + 1) * P
                    here = score[:, (b - 1) * S:(b - 1) * S + w]
                    dve.wait_ge(score_taken, s + 3)
                    dve.wait_ge(idx_added, s + 1)
                    nc.vector.scalar_tensor_tensor(out=here, in0=s_sb[:, (u % 2) * S:(u % 2) * S + w],
                                                   scalar=widx[:, sl(b * 16 + t * 2 + hh, 1)], in1=here,
                                                   op0=ALU.mult, op1=ALU.add).then_inc(idx_added, 1)
                    if u == 1 and more:
                        idx_query(i, j)

            idx_query(0, -1)
            with dve.Fori(0, 3) as i:
                link.begin(i, 4)
                idx_tile(i, 0, True)
                idx_tile(i, 1, True)
            link.end(4, 3)
            idx_tile(3, 0, True)
            idx_tile(3, 1, False)
            rows = [(b, score[:, (b - 1) * S:(b - 1) * S + (b + 1) * P], m8[:, (b - 1) * 8:b * 8]) for b in range(1, NB)]
            dve.wait_ge(idx_added, IDX_SCORES + 2)
            for b, here, _ in rows:
                link.mark(nc.vector.tensor_tensor(here, here, causal(b), ALU.add))
            link.catch()
            with dve.Fori(0, TOPK // 8) as i:
                link.begin(i, 6)
                for b, here, best in rows:
                    link.mark(nc.vector.max(best, here))
                link.catch()
                settle(dve)
                for b, here, best in rows:
                    link.mark(nc.vector.match_replace(here, best, here, TAKEN))
                link.catch()
            link.end(6, TOPK // 8)
            for b, here, _ in rows:
                link.mark(nc.vector.tensor_scalar(bias_a[:, (b - 1) * S:(b - 1) * S + (b + 1) * P], here, -2e38, NEG,
                                                  ALU.is_gt, ALU.mult))
            link.catch()
            attention("aq")
            attention("amem")
            residual("aout", 2)
            norm("affn")
            feed_forward(0)

            norm("bmix")
            dve.wait_ge(zeroed, 1)
            for k in range(4):
                c, t = At(CH["bfront"] + k), At(TL["bfront"] + k)
                split_lo(c + 2)
                if k < 2:
                    link(rope(ktmp[:, 0:S], qraw[:, :], tab64, SHUF64, t))
                    spread_keys(b_k, k).then_inc(roped, 1)
            attention("bq")
            attention("bmem")
            residual("bout", 2)
            norm("bffn")
            feed_forward(1)
            norm("final1")

            norm("conv")
            with dve.Fori(0, CT) as i:
                link.begin(i, 4)
                c, t = At(CH["conv"], i, 4), At(TL["conv"], i, 4)
                split_lo(c + 2)
                split_lo(c + 3)
                dve.wait_ge(pj_free[t.par], t.half + 2)
                complete(c + 1)
                nc.vector.tensor_tensor(fb[:, :], fa[:, :], pj[(t + 1).par][:, :],
                                        ALU.mult).then_inc(pj_free[(t + 1).par], 1)
                dve.wait_ge(pj_free[(t + 1).par], (t + 1).half + 2)
                w = [VD("a_conv_w", i + j * CT) for j in range(3)]
                link(nc.vector.tensor_scalar(fc[:, :], fb[:, :], w[2], None, ALU.mult))
                link(nc.vector.scalar_tensor_tensor(out=fc[:, 1:S], in0=fb[:, 0:S - 1], scalar=w[1], in1=fc[:, 1:S],
                                                    op0=ALU.mult, op1=ALU.add))
                link(nc.vector.scalar_tensor_tensor(out=fc[:, 2:S], in0=fb[:, 0:S - 2], scalar=w[0], in1=fc[:, 2:S],
                                                    op0=ALU.mult, op1=ALU.add))
                split_lo(c + 4)
                dve.wait_ge(pj_free[t.par], t.half + 1 + 2)
                link(nc.vector.tensor_tensor(fe[:, :], fc[:, :], fd[:, :], ALU.mult))
                split_lo(c + 5)
                complete(c + 3)
                dve.wait_ge(g_ready, i + (2 * FT + 1))
                nc.vector.tensor_tensor(fg[:, :], fe[:, :], pj[(t + 3).par][:, :],
                                        ALU.mult).then_inc(pj_free[(t + 3).par], 1)
                dve.wait_ge(g_hi_ready, i + (2 * FT + 1))
                nc.vector.tensor_tensor(G_lo[:, ds(i * S, S)], fg[:, :], G_hi[:, ds(i * S, S)].bitcast(f32),
                                        ALU.subtract).then_inc(g_ready, 1)
            link.end(4, CT)
            residual("cout", 2)
            norm("kv2")

            dve.wait_ge(pos_hi_ready, 1)
            nc.vector.tensor_tensor(pos_lo[:, :], vec[:, VC["pos_k"]:VC["pos_k"] + 36], pos_hi[:, :].bitcast(f32),
                                    ALU.subtract).then_inc(pos_ready, 1)
            dve.wait_ge(zeroed, 2)
            for k in range(4):
                c = At(CH["cmp_kv"] + k)
                which, pair = k // 2, k % 2
                split_lo(c + 2)
                here = slice(2 * pair * FPAD, 2 * (pair + 1) * FPAD)
                low = f_lo[which][0:64, here].rearrange("p (g c) -> p g c", g=2)
                high = f_lo[which][64:P, here].rearrange("p (g c) -> p g c", g=2)
                part = f_hi[which][0:64, here].bitcast(f32).rearrange("p (g c) -> p g c", g=2)
                dve.wait_ge(f_hi_ready, k + 1)
                link(nc.vector.tensor_tensor(low[:, :, 0:S], fraw[0:64, :].rearrange("p (g c) -> p g c", g=2),
                                             part[:, :, 0:S], ALU.subtract))
                dve.wait_ge(f_hi_done, k + 1)
                nc.vector.tensor_copy(high[:, :, 0:S - 1],
                                      f_lo[which][0:64, here].bitcast(f32).rearrange("p (g c) -> p g c", g=2)[:, :, 1:S]
                                      ).then_inc(f_ready, 1)
            for k in range(4):
                c, t = At(CH["cmp"] + 2 * k), At(TL["cmp"] + k)
                split_lo(c + 2)
                split_lo(c + 3)
                complete(c + 1)
                link(nc.vector.tensor_copy(hb[:, 0:1], po[:, 0:1]))
                nc.vector.tensor_scalar(hidx[:, :], pj[t.par][:, 0:P], hb[:, 0:1], None, ALU.add).then_inc(pj_free[t.par], 1)
                dve.wait_ge(pj_free[t.par], t.half + 2)
                link(nc.vector.tensor_tensor(hidt[:, :], hidx[:, :], hidx[:, :], ALU.mult))
                link(nc.vector.tensor_scalar(hidt[:, :], hidt[:, :], 0.044715, 1.0, ALU.mult, ALU.add))
                nc.vector.tensor_tensor(hidt[:, :], hidt[:, :], hidx[:, :], ALU.mult).then_inc(hid_x, 1)
                dve.wait_ge(hid_th, k + 1)
                link(nc.vector.tensor_scalar(hidt[:, :], hidt[:, :], 0.5, 0.5, ALU.mult, ALU.add))
                nc.vector.tensor_tensor(hidf[:, k * P:(k + 1) * P], hidt[:, :], hidx[:, :], ALU.mult).then_inc(hid_f, 1)
                dve.wait_ge(hid_hi_ready, k + 1)
                nc.vector.tensor_tensor(hid_lo[:, k * P:(k + 1) * P], hidf[:, k * P:(k + 1) * P],
                                        hid_hi[:, k * P:(k + 1) * P].bitcast(f32), ALU.subtract).then_inc(hid_ready, 1)
            c, t = At(CH["cmp"] + 8), At(TL["cmp"] + 4)
            split_lo(c + 2)
            complete(c)
            for hh in range(2):
                last = nc.vector.tensor_scalar(
                    cmp_k[:, :].rearrange("p (g h n) -> p g h n", g=4, h=2)[:, :, hh, :],
                    pj[t.par][:, 0:P].rearrange("p (g n) -> p g n", g=4), C("half", hh), None, ALU.mult)
            last.then_inc(pj_free[t.par], 1)
            dve.wait_ge(ld["tab2"], 16)
            for s, (kn, branch) in enumerate((("nk_s", "slc"), ("nk_w", "win"))):
                for k in range(4):
                    c, t = At(CH["nkv"] + 4 * s + k), At(TL["nkv"] + 4 * s + k)
                    split_lo(c + 2)
                    if k < 2:
                        link(rope(ktmp[:, 0:S], qraw[:, :], tab64, SHUF64, t))
                        spread_keys(n_k[branch], k).then_inc(roped, 1)
            norm("q2")
            split_lo(At(CH["gates"] + 2))
            dve.wait_ge(gate_done, 1)
            early = gate[:, 0:48].rearrange("p (h r) -> p h r", r=3)[:, :, 0]
            link(nc.vector.tensor_scalar(early, early, C("rowvalid"), None, ALU.mult))
            with dve.Fori(0, 4) as i:
                for k in range(2):
                    split_lo(At(CH["nz"] + k + 2, i, 2))
            attention("nq")
            residual("nout", 1)
            norm("final2")

        @block.tensor
        def _(pe):
            pe.sem_inc(chunk_used, 2)
            pe.sem_inc(exp_done, 2)
            pe.sem_inc(p_turned, 2)
            pe.sem_inc(pT_ready, 2)
            pe.sem_inc(pv_done, 2)
            pe.sem_inc(o_copied, 1)
            pe.sem_inc(o_turned, 1)
            pe.wait_ge(setup, 1)
            pe.wait_ge(ld["cst"], 16)

            def product(acc, w0, cpar, x, first, last):
                col = cpar * CW + w0 * P
                passes = ((w_hi, 0), (w_hi, 1), (w_lo, 0))
                for k, (w, part) in enumerate(passes):
                    mm = nc.tensor.matmul(acc, w[:, col:col + P], x[part], start=first and k == 0, stop=last and k == 2)
                return mm

            def arrived(c):
                pe.wait_ge(lo_ready, c.v + 3)

            def free(t):
                pe.wait_ge(pj_free[t.par], t.half + 1)

            def project(c, t, hi, lo, n=S, norm=None):
                arrived(c)
                free(t)
                for k in range(CB):
                    if norm:
                        pe.wait_ge(h_ready, NBASE[NQ[norm]] + k + 1)
                    mm = product(pj[t.par][:, 0:n], k, c.par, (hi[:, k * n:(k + 1) * n], lo[:, k * n:(k + 1) * n]),
                                 k == 0, k == CB - 1)
                mm.then_inc(chunk_used, 1)

            def norm(name):
                _, n, _, _, _, _ = NORM[name]
                q = NQ[name]
                k = NORMS[q][1]
                for m in range(k):
                    s = NBASE[q] + m
                    pe.wait_ge(sq_ready, s + 1)
                    for b in range(n // P):
                        mm = nc.tensor.matmul(SUMS[b][:, 0:1], sq[:, (s % 2) * S + b * P:(s % 2) * S + (b + 1) * P],
                                              ones[:, 0:1], start=m == 0, stop=m == k - 1)
                    mm.then_inc(sq_used, 1)
                pe.wait_ge(diag_ready, q + 1)
                for b in range(n // P):
                    mm = nc.tensor.matmul(px[:, b * P:(b + 1) * P], ones[:, :], diag[:, b * P:(b + 1) * P],
                                          start=True, stop=True)
                mm.then_inc(factor_ready, 1)

            def turn(t, number, src=None, width=P, blocks=NB):
                pe.wait_ge(pj_free[t.par], t.half + 2)
                src = vraw if src is None else src
                for b in range(blocks):
                    mm = nc.tensor.transpose(pt[number % 2][0:width, b * P:(b + 1) * P], src[:, b * width:(b + 1) * width],
                                             ident)
                mm.then_inc(v_turned, 1)

            def query(ph, i, j, normed=None):
                c, t = next_chunk(ph, i, j, 0), next_tile(ph, i, j, 0)
                project(c, t, h_hi, h_lo, norm=normed)

            def keys_values(ph, i, j):
                c, t = next_chunk(ph, i, j, 0), next_tile(ph, i, j, 0)
                if ph.name == "aq":
                    arrived(c + 1)
                    free(t + 1)
                    for k in range(2):
                        product(pj[(t + 1).par][:, :], k, (c + 1).par,
                                (c_hi[:, k * S:(k + 1) * S], c_lo[:, k * S:(k + 1) * S]), k == 0, k == 1)
                    free(t + 2)
                    acc = pj[(t + 2).par]
                    for b in range(NB):
                        for k in range(2):
                            col = (c + 1).par * CW + (2 + k) * P
                            here = slice(k * S + b * P, k * S + (b + 1) * P)
                            for n, (x, w) in enumerate(((c_hi, w_hi), (c_hi, w_lo), (c_lo, w_hi))):
                                mm = nc.tensor.matmul(acc[:, b * P:(b + 1) * P], x[:, here], w[:, col:col + P],
                                                      start=k == 0 and n == 0, stop=k == 1 and n == 2)
                    mm.then_inc(chunk_used, 1)

            def tile(ph, i, j, more):
                t = i * 2 + j
                g = i

                def score_(u):
                    hh, b, branch = ph.units[u]
                    s = ph.first_score + t * ph.n + u
                    k0, w = ph.keys(u)
                    q = qn if branch == "cmp" else qs
                    if branch == "topk":
                        keys = a_k[:, j * S:j * S + w]
                    elif branch == "mem":
                        k_at = (2 * t + hh) * MEM
                        keys = mem_k[0 if ph.name == "amem" else 1][:, k_at:k_at + MEM]
                    elif branch == "band":
                        keys = b_k[:, sl(g * 2 * S + hh * S + k0, w)]
                    elif branch == "cmp":
                        keys = cmp_k[:, sl(g * 2 * NCMP + hh * NCMP, NCMP)]
                    else:
                        keys = n_k[branch][:, sl(g * 2 * S + hh * S, w)]
                    pe.wait_ge(score_taken, s + 1)
                    nc.tensor.matmul(ps[u % 2][:, 0:w], q[:, j * S + b * P:j * S + (b + 1) * P], keys,
                                     start=True, stop=True).then_inc(score_done, 1)

                def turn_p(u):
                    a = ph.first_unit + t * ph.n + u
                    par = u % 2
                    w = ph.keys(u)[1]
                    pe.wait_ge(p_ready, a + 1)
                    pe.wait_ge(pT_ready, a + 1)
                    wide = min(w, P)
                    for k in range(w // wide):
                        mm = nc.tensor.transpose(pt[par][0:wide, k * P:(k + 1) * P],
                                                 p_sb[:, par * S + k * wide:par * S + (k + 1) * wide], ident)
                    mm.then_inc(p_turned, 1)

                def values(u):
                    hh, b, branch = ph.units[u]
                    a = ph.first_unit + t * ph.n + u
                    par = u % 2
                    k0, w = ph.keys(u)
                    dv = ph.dv
                    acc = po[:, b * P + hh * dv:b * P + (hh + 1) * dv]
                    if u == 0:
                        pe.wait_ge(o_copied, ph.first_tile + t + 1)
                    pe.wait_ge(pT_ready, a + 3)
                    first, last = branch not in ("slc", "win"), branch not in ("cmp", "slc")
                    if branch == "cmp":
                        settle(pe)
                        nc.tensor.matmul(acc, pT[0:NCMP, par * S:par * S + P], cmp_v[0:NCMP, sl(g * 64, 64)],
                                         start=True, stop=False).then_inc(pv_done, 1)
                        return
                    kbs = w // P
                    for k in range(kbs):
                        kb = k0 // P + k
                        if branch == "topk":
                            v = a_v[:, j * S + kb * P:j * S + (kb + 1) * P]
                        elif branch == "mem":
                            v_at = kb * 256 + (2 * t + hh) * 64
                            v = mem_v[0 if ph.name == "amem" else 1][:, v_at:v_at + 64]
                        elif branch == "band":
                            v = b_v[:, sl(g * 64 + kb * 256, 64)]
                        else:
                            v = n_v[branch][:, sl(g * 64 + kb * 256, 64)]
                        mm = nc.tensor.matmul(acc, pT[:, par * S + k * P:par * S + (k + 1) * P], v,
                                              start=first and k == 0, stop=last and k == kbs - 1)
                    mm.then_inc(pv_done, 1)

                if ph.units[0][2] == "mem" or ph.name == "aq":
                    q = At(TL[ph.name] + j * (3 if ph.name == "aq" else 1) + (2 if ph.name == "aq" else 0), i,
                           2 * (3 if ph.name == "aq" else 1))
                    pe.wait_ge(pj_free[q.par], q.half + 2)
                if ph.units[0][2] != "mem":
                    pe.wait_ge(roped, RP[ph.name] + t + 2)
                score_(0)
                score_(1)
                if more:
                    query(ph, i, j)
                for u in range(ph.n):
                    if u + 2 < ph.n:
                        score_(u + 2)
                    turn_p(u)
                    if u:
                        values(u - 1)
                    if u == 1 and more:
                        keys_values(ph, i, j)
                values(ph.n - 1)
                k = ph.first_tile + t
                pe.wait_ge(o_copied, k + 2)
                pe.wait_ge(out_ready, k + 1)
                for b in range(NB):
                    mm = nc.tensor.transpose(px[:, b * P:(b + 1) * P], o_sb[:, b * P:(b + 1) * P], ident)
                mm.then_inc(o_turned, 1)

            def attention(name, normed=None):
                ph = ATT[name]
                query(ph, 0, -1, normed)
                keys_values(ph, 0, -1)
                attention_tiles(pe, ph, tile)

            def down(stage, per, kt, trips=DT // 2):
                def two(i):
                    for j in range(2):
                        t = At(TL[stage] + j, i, 2)
                        free(t)
                        for n in range(per):
                            c = At(CH[stage] + j * per + n, i, 2 * per)
                            arrived(c)
                            for k in range(n * CB, min(kt, (n + 1) * CB)):
                                here = slice(k * S, (k + 1) * S)
                                mm = product(pj[t.par][:, :], k % CB, c.par, (G_hi[:, here], G_lo[:, here]),
                                             k == 0, k == kt - 1)
                            mm.then_inc(chunk_used, 1)

                with pe.Fori(0, trips) as i:
                    two(i)

            def feed_forward(l):
                up, base = CH[f"up{l}"], TL[f"up{l}"]
                pe.wait_ge(h_ready, NBASE[NQ["affn" if l == 0 else "bffn"] + 1])
                with pe.Fori(0, FT) as i:
                    for k in range(2):
                        project(At(up + k, i, 2), At(base + k, i, 2), h_hi, h_lo)
                pe.wait_ge(g_ready, (l + 1) * FT + 1)
                down(f"down{l}", DOWN_CHUNKS, FT)

            norm("mem")
            number = TN["memv"]
            for k in range(8):
                c, t = At(CH["mem"] + k), At(TL["mem"] + k)
                project(c, t, memn_hi, memn_lo, n=MEM, norm="mem" if k == 0 else None)
                if k % 4 >= 2:
                    turn(t, number, blocks=MEM // P)
                    number += 1
            norm("amix")
            for k in range(4):
                c, t = At(CH["afront"] + k), At(TL["afront"] + k)
                project(c, t, h_hi, h_lo, norm="amix" if k == 0 else None)
                if k == 2:
                    turn(t, TN["widx"], qraw)
            norm("ckv")

            def idx_query(i, j):
                project(At(CH["idx"] + 1 + j, i, 2), At(TL["idx"] + 1 + j, i, 2), h_hi, h_lo)

            def idx_tile(i, j, more):
                t = i * 2 + j
                pe.wait_ge(roped, RP["idx"] + t + 2)
                for u, (hh, b) in enumerate(IDX_UNITS):
                    w = (b + 1) * P
                    pe.wait_ge(score_taken, t * len(IDX_UNITS) + u + 1)
                    nc.tensor.matmul(ps[u % 2][:, 0:w], qs[:, j * S + b * P:j * S + (b + 1) * P],
                                     kidx[:, hh * S:hh * S + w], start=True, stop=True).then_inc(score_done, 1)
                    if u == 1 and more:
                        idx_query(i, j)

            idx_query(0, -1)
            with pe.Fori(0, 3) as i:
                idx_tile(i, 0, True)
                idx_tile(i, 1, True)
            idx_tile(3, 0, True)
            idx_tile(3, 1, False)
            pe.wait_ge(h_ready, NBASE[NQ["ckv"] + 1])
            attention("aq")
            attention("amem")
            pe.wait_ge(out_ready, ATT["amem"].first_tile + 2 + 1)
            down("aout", 2, 10)
            norm("affn")
            feed_forward(0)

            norm("bmix")
            for k in range(4):
                c, t = At(CH["bfront"] + k), At(TL["bfront"] + k)
                project(c, t, h_hi, h_lo, norm="bmix" if k == 0 else None)
                if k >= 2:
                    turn(t, TN["bv"] + k - 2)
            attention("bq")
            attention("bmem")
            pe.wait_ge(out_ready, ATT["bmem"].first_tile + 2 + 1)
            down("bout", 2, 10)
            norm("bffn")
            feed_forward(1)
            norm("final1")

            norm("conv")
            pe.wait_ge(h_ready, NBASE[NQ["conv"] + 1])
            with pe.Fori(0, CT) as i:
                for k in range(4):
                    project(At(CH["conv"] + k, i, 4), At(TL["conv"] + k, i, 4), h_hi, h_lo)
            pe.wait_ge(g_ready, 2 * FT + CT + 1)
            down("cout", 2, CT)
            norm("kv2")
            for k in range(4):
                project(At(CH["cmp_kv"] + k), At(TL["cmp_kv"] + k), h_hi, h_lo, norm="kv2" if k == 0 else None)
            pe.wait_ge(pos_ready, 1)
            for k in range(4):
                which, m = k // 2, k % 2
                pe.wait_ge(f_ready, 2 * which + 2)
                t = At(TL["cmp"] + k)
                free(t)
                if k:
                    before = At(TL["cmp"] + k - 1)
                    pe.wait_ge(pj_free[before.par], before.half + 2)
                for n in range(2):
                    c = At(CH["cmp"] + 2 * k + n)
                    arrived(c)
                    for w0 in range(CB):
                        l = n * CB + w0
                        rhs = [f[which][:, :].rearrange("p (g c) -> p g c", g=4)[:, :, 2 * l:2 * l + 16 * (NCMP - 1) + 1:16]
                               for f in (f_hi, f_lo)]
                        at = which * 18 + l
                        product(po[:, 0:2], w0, c.par, (pos_hi[:, at:at + 2], pos_lo[:, at:at + 2]), l == 0, l == 15)
                        mm = product(pj[t.par][:, 0:P], w0, c.par, rhs, l == 0, l == 15)
                    mm.then_inc(chunk_used, 1)
            c = At(CH["cmp"] + 8)
            arrived(c)
            for which in range(2):
                t = At(TL["cmp"] + 4 + which)
                free(t)
                pe.wait_ge(hid_ready, 2 * which + 2)
                for m in range(2):
                    here = slice((2 * which + m) * P, (2 * which + m + 1) * P)
                    mm = product(pj[t.par][:, 0:P], 2 * which + m, c.par, (hid_hi[:, here], hid_lo[:, here]), m == 0, m == 1)
            mm.then_inc(chunk_used, 1)
            turn(At(TL["cmp"] + 5), TN["cmpv"], width=NCMP)
            for s, vn in enumerate(("nv_s", "nv_w")):
                for k in range(4):
                    c, t = At(CH["nkv"] + 4 * s + k), At(TL["nkv"] + 4 * s + k)
                    project(c, t, h_hi, h_lo)
                    if k >= 2:
                        turn(t, TN[vn] + k - 2)
            norm("q2")
            project(At(CH["gates"]), At(TL["gates"]), h_hi, h_lo, norm="q2")
            turn(At(TL["gates"]), TN["gates"])
            with pe.Fori(0, 4) as i:
                for k in range(2):
                    project(At(CH["nz"] + k, i, 2), At(TL["nz"] + k, i, 2), h_hi, h_lo)
            attention("nq")
            pe.wait_ge(out_ready, ATT["nq"].first_tile + 8 + 1)
            down("nout", 1, DT)
            norm("final2")


def kernel(**inputs):
    import numpy as np
    import concourse.bacc as bacc
    from concourse.bass_utils import run_bass_kernel_spmd as run

    a = {k: np.asarray(v) for k, v in inputs.items()}
    f = np.float32

    def cols(w, k, c0, n=P):
        b = np.zeros((P, P), f)
        b[:, 0:n] = w[k * P:(k + 1) * P, c0:c0 + n]
        return b

    def picked(w, k, index):
        return w[k * P:(k + 1) * P][:, index]

    zero = np.zeros((P, P), f)
    chunks = []

    def chunk(blocks):
        chunks.append(np.stack(list(blocks) + [zero] * (CB - len(blocks)), axis=1))

    def plain(w, c0, count, kt=CB):
        for m in range(count):
            blocks = [cols(w, k, c0 + m * P) for k in range(kt)]
            for n in range(0, kt, CB):
                chunk(blocks[n:n + CB])

    wa, wb, wn, wkv = a["a_w_in"][0], a["b_w_in"][0], a["b_w_in_2"][0], a["w_kv_2"]
    uk = a["a_w_uk"][0]
    uv = a["a_w_uv"][0].reshape(256, 1024)
    for l in range(2):
        plain(a["w_mem_kv"][l], 0, 4)
    plain(wa, 1024, 2)
    chunk([np.concatenate([wa[k * P:(k + 1) * P, 2400:2416], np.zeros((P, 80), f), wa[k * P:(k + 1) * P, 1280:1312]], 1)
           for k in range(DT)])
    chunk([np.concatenate([wa[k * P:(k + 1) * P, 2336:2400]] * 2, 1) for k in range(DT)])
    plain(wa, 1312, 8)
    for h in range(8):
        order = h * P + np.concatenate([np.arange(32, P), np.arange(32)])
        chunk([picked(wa, k, order) for k in range(DT)])
        blocks = []
        for k in range(2):
            b = np.zeros((P, P), f)
            b[:, 0:96] = uk[k * P:(k + 1) * P, h, :]
            blocks.append(b)
        chunk(blocks + [cols(uv, k, h * P) for k in range(2)])
    plain(wa, 2416, 2)
    plain(a["a_w_out"][0], 0, DT, 10)

    def feed_forward(l):
        for m in range(FT):
            plain(a["f_w_up"][l], m * P, 1)
            plain(a["f_w_up"][l], FT * P + m * P, 1)
        plain(a["f_w_down"][l], 0, DT, FT)

    feed_forward(0)
    plain(wb, 1024, 4)
    plain(wb, 0, 8)
    plain(wb, 1536, 2)
    plain(a["b_w_out"][0], 0, DT, 10)
    feed_forward(1)
    for m in range(CT):
        for part in (1, 2, 3, 0):
            plain(a["a_w_in_2"][0], part * CT * P + m * P, 1)
    plain(a["a_w_out_2"][0], 0, DT, CT)
    plain(wkv, 0, 4)
    for which in ("k", "v"):
        plain(a[f"cmp_w1_{which}_2"], 0, 2, 16)
    w2k, w2v = a["cmp_w2_k_2"], a["cmp_w2_v_2"]
    chunk([np.concatenate([w2k[k * P:(k + 1) * P]] * 2, 1) for k in range(2)] + [cols(w2v, k, 0, 64) for k in range(2)])
    for s in (2, 3, 4, 5):
        plain(wkv, s * 256, 2)
    chunk([cols(wn, k, 1024, 48) for k in range(DT)])
    plain(wn, 1072, 8)
    plain(wn, 0, 8)
    plain(a["b_w_out_2"][0], 0, DT)
    assert len(chunks) == NCHUNKS, (len(chunks), NCHUNKS)
    stream = np.stack(chunks).reshape(NCHUNKS, P, CW)

    def tiles(v):
        return np.ascontiguousarray(v.reshape(-1, P).T)

    def positions(e):
        return np.concatenate([tiles(e.reshape(-1)), np.zeros((P, 2), f)], 1)

    vec = np.concatenate([
        tiles(a["g_mix"].reshape(-1)), tiles(a["g_ffn"].reshape(-1)), tiles(a["g_mem"]), tiles(a["g_final"]),
        tiles(a["a_norm_2"][0]), tiles(a["kv_norm_2"]), tiles(a["b_norm_2"][0]), tiles(a["final_norm_2"]),
        tiles(a["a_kv_norm"][0]), tiles(a["f_conv_w"].reshape(-1)), tiles(a["f_conv_b"].reshape(-1)),
        tiles(a["a_conv_w_2"][0].reshape(-1)), np.broadcast_to(a["b_sinks"][0], (P, 16)),
        positions(a["cmp_pos_k_2"]), positions(a["cmp_pos_v_2"])], 1)
    assert vec.shape[1] == NVEC

    q, k = np.arange(P)[:, None], np.arange(P)[None, :]
    hide_later = np.where(k > q, NEG, 0.0)
    hide_far = np.where(k <= q, NEG, 0.0)
    n = np.arange(NCMP)[None, :]
    cmp = [np.where((n < NCMP - 1) & (16 * n + 31 <= b * P + q), 0.0, NEG) for b in range(NB)]

    def rotation(dim, at):
        rot = dim // 4
        freq = (np.float64(500000.0) ** (-np.arange(0, rot, 2) / rot)).astype(f)
        inv, sgn = np.zeros(P, f), np.zeros(P, f)
        for h in range(0, P, dim):
            inv[h + at:h + at + rot] = np.concatenate([freq, freq])
            sgn[h + at:h + at + rot] = np.concatenate([-np.ones(rot // 2), np.ones(rot // 2)])
        return inv[:, None], sgn[:, None]

    inv128, sgn128 = rotation(128, 96)
    inv64, sgn64 = rotation(64, 0)
    cst = np.concatenate([np.eye(P), np.zeros((P, S - P)), hide_later, hide_far, hide_later, *cmp,
                          (q < 64), (q >= 64), inv128, sgn128, inv64, sgn64, (q >= 31)], 1).astype(f)
    assert cst.shape[1] == NCONST
    angle = (inv64 * np.arange(S, dtype=f)[None, :]).astype(np.float64)
    tab2 = np.concatenate([np.cos(angle), np.sin(angle) * sgn64], 1).astype(f)

    def feature_major(x, n):
        return np.ascontiguousarray(x.T.reshape(DT, P, n).transpose(1, 0, 2).reshape(P, DT * n))

    arrays = {
        "wstream": stream, "x": feature_major(a["x"][0], S), "mem": feature_major(a["mem"][0], MEM),
        "pos": np.ascontiguousarray(np.broadcast_to(a["positions"], (P, S))).astype(np.int32),
        "vec": np.ascontiguousarray(vec), "cst": cst, "tab2": tab2}
    nc = bacc.Bacc("TRN2", target_bir_lowering=False, num_devices=1)
    args = [nc.dram_tensor(f"in_{n}", v.shape, mybir.dt.from_np(v.dtype), kind="ExternalInput").ap()
            for n, v in arrays.items()]
    args.append(nc.dram_tensor("out_x", (P, DT * S), mybir.dt.float32, kind="ExternalOutput").ap())
    build(nc, *args)
    got = run(nc, [{f"in_{n}": v for n, v in arrays.items()}], core_ids=[0]).results[0]["out_x"]
    return np.ascontiguousarray(got.reshape(P, DT, S).transpose(1, 0, 2).reshape(D, S).T)[None]
```

```python
import concourse.bass as bass
from concourse import mybir
from contextlib import ExitStack

P = 128
S = 512
D = 1024
DT = D // P
NB = S // P
CB = 8
CW = CB * P
MEM = 256
FT = 2816 // P
CT = 2048 // P
DOWN_CHUNKS = -(-FT // CB)
EPS = 1e-6
NEG = -1e30
TAKEN = -3e38
TOPK = 128
NCMP = 32
FPAD = 544
TWO_PI = 6.283185307179586
PI_HI = 6.28125
PI_LO = TWO_PI - PI_HI
ROUNDER = 12582912.0

STAGES = [("mem", 8), ("afront", 4), ("idx", 8), ("aq", 16), ("amem", 2), ("aout", 16), ("up0", 2 * FT),
          ("down0", DT * DOWN_CHUNKS), ("bfront", 4), ("bq", 8), ("bmem", 2), ("bout", 16), ("up1", 2 * FT),
          ("down1", DT * DOWN_CHUNKS), ("conv", 4 * CT), ("cout", 2 * DT), ("cmp_kv", 4), ("cmp", 8), ("nkv_s", 4), ("cmp2", 1),
          ("nkv_w", 4), ("gates", 1), ("nz", 8), ("nq", 8), ("nout", DT)]
CH, NCHUNKS = {}, 0
for _name, _count in STAGES:
    CH[_name] = NCHUNKS
    NCHUNKS += _count

TILES = [("mem", 8), ("afront", 4), ("idx", 8), ("aq", 24), ("amem", 2), ("aout", 8), ("up0", 2 * FT), ("down0", 8),
         ("bfront", 4), ("bq", 8), ("bmem", 2), ("bout", 8), ("up1", 2 * FT), ("down1", 8), ("conv", 4 * CT),
         ("cout", 8), ("cmp_kv", 4), ("cmp", 4), ("nkv_s", 4), ("cmp2", 2),
         ("nkv_w", 4), ("gates", 1), ("nz", 8), ("nq", 8), ("nout", 8)]
TL, _t = {}, 0
for _name, _count in TILES:
    TL[_name] = _t
    _t += _count

ROPES = [("krope", 1), ("kidx", 1), ("idx", 8), ("aq", 8), ("bk", 2), ("bq", 8), ("nk_s", 2), ("nk_w", 2),
         ("nq", 8)]
RP, _t = {}, 0
for _name, _count in ROPES:
    RP[_name] = _t
    _t += _count

NORMS = [("mem", 8), ("amix", 8), ("ckv", 2), ("affn", 8), ("bmix", 8), ("bffn", 8), ("final1", 8), ("conv", 8),
         ("kv2", 8), ("q2", 8), ("final2", 8)]
NQ = {name: q for q, (name, _) in enumerate(NORMS)}
PLAIN = ("final1", "final2")
SBASE = [sum(k for n, k in NORMS[:q] if n not in PLAIN) for q in range(len(NORMS) + 1)]
RESIDUALS = {name: DT * k for k, name in enumerate(("aout", "down0", "bout", "down1", "cout", "nout"))}
NBASE = [sum(k for _, k in NORMS[:q]) for q in range(len(NORMS) + 1)]

TURNS = [("memv", 4), ("widx", 1), ("bv", 2), ("nv_s", 2), ("cmpv", 1), ("nv_w", 2), ("gates", 1)]
TN, _t = {}, 0
for _name, _count in TURNS:
    TN[_name] = _t
    _t += _count


class Attention:

    def __init__(self, name, tiles, units, branches, chunks, dv, scale, first_score, first_unit, first_tile, first_pass,
                 out0):
        self.name, self.tiles, self.chunks, self.dv, self.scale = name, tiles, chunks, dv, scale
        self.units = [(hh, b, branch) for branch in branches for hh, b in units]
        self.first_score, self.first_unit, self.first_tile, self.out0 = first_score, first_unit, first_tile, out0
        self.first_pass, self.passes, self.m, self.n = first_pass, len(branches), len(units), len(self.units)
        self.ahead = 3 if self.m == 8 else 2
        self.at_scale, self.at_turn, self.at_gate, self.at_hi, self.at_lo = (1, 2, 3, 4, 5) if self.m == 8 else (
            0, 1, 1, 2, 3)
        self.at_query = {"aq": 1, "nq": 10}.get(name, 2)
        self.at_refill = {"aq": 2, "nq": 13}.get(name, 6)

    def split(self, u):
        return u // self.m, u % self.m

    def region(self, u):
        hh, b, _ = self.units[u]
        return b * (P // self.dv) + hh

    def keys(self, j):
        _, b, branch = self.units[j]
        if branch == "mem":
            return 0, MEM
        if branch == "band":
            return (0, P) if b == 0 else ((b - 1) * P, 2 * P)
        if branch == "cmp":
            return 0, NCMP
        return 0, (b + 1) * P


IDX_UNITS = [(hh, b) for hh in range(2) for b in range(1, NB)]
IDX_SCORES = 8 * len(IDX_UNITS)


def _attentions():
    made, score, unit, tile, done = {}, IDX_SCORES, 0, 0, 0
    pair = [(hh, b) for hh in range(2) for b in range(NB)]
    for name, tiles, units, branches, chunks, dv, dim, out0 in (
            ("aq", 8, [(0, b) for b in range(NB)], ["topk"], 2, 128, 128, 0),
            ("amem", 2, pair, ["mem"], 1, 64, 64, 8), ("bq", 8, pair, ["band"], 1, 64, 64, 0),
            ("bmem", 2, pair, ["mem"], 1, 64, 64, 8), ("nq", 8, pair, ["cmp", "slc", "win"], 1, 64, 64, 0)):
        made[name] = Attention(name, tiles, units, branches, chunks, dv, float(dim) ** -0.5, score, unit, tile, done,
                               out0)
        n = tiles * len(units) * len(branches)
        score, unit, tile, done = score + n, unit + n, tile + tiles, done + tiles * len(branches)
    return made


ATT = _attentions()

VECS = [("g_mix", 16), ("g_ffn", 16), ("g_mem", 8), ("g_final", 8), ("a_norm", 8), ("kv_norm", 8), ("b_norm", 8),
        ("final_norm", 8), ("a_kv_norm", 2), ("f_conv_w", 2 * 3 * FT), ("f_conv_b", 2 * FT), ("a_conv_w", 3 * CT),
        ("sinks", 16), ("pos_k", 18), ("pos_v", 18)]
VC, NVEC = {}, 0
for _name, _count in VECS:
    VC[_name] = NVEC
    NVEC += _count
CONSTS = [("ident", P), ("causal", S), ("band", 2 * P), ("cmp", NB * NCMP), ("half", 2), ("inv128", 1), ("sgn128", 1),
          ("inv64", 1), ("sgn64", 1), ("rowvalid", 1)]
CC, NCONST = {}, 0
for _name, _count in CONSTS:
    CC[_name] = NCONST
    NCONST += _count

SHUF128 = [(i + 16) % 32 for i in range(32)]
SHUF64 = [(i + 8) % 16 if i < 16 else i for i in range(32)]


class At:

    def __init__(self, base, i=0, per=0):
        assert per % 2 == 0
        self.v = base + i * per if per else base
        self.par = base % 2
        self.half = base // 2 + i * (per // 2) if per else base // 2
        self.args = (base, i, per)

    def __add__(self, k):
        return At(self.args[0] + k, *self.args[1:])


class Links:

    def __init__(self, eng, sem):
        self.eng, self.sem, self.n, self.shift = eng, sem, 0, 0

    def mark(self, instruction):
        self.n += 1
        instruction.then_inc(self.sem, 1)

    def catch(self):
        self.eng.wait_ge(self.sem, self.shift + self.n)

    def __call__(self, instruction):
        self.mark(instruction)
        self.catch()

    def begin(self, i, per):
        self.shift, self.at = i * per, self.n

    def end(self, per, trips):
        assert self.n - self.at == per, (self.n - self.at, per)
        self.n, self.shift = self.at + per * trips, 0



def build(nc, wstream, xin, memin, posin, vecin, cstin, tab2in, out):
    f32, f32r, i32 = mybir.dt.float32, mybir.dt.float32r, mybir.dt.int32
    ALU, ACT = mybir.AluOpType, mybir.ActivationFunctionType
    ds = bass.ds
    place = [-(-nc.sbuf_base // 32) * 32]

    def put(name, cols, dt=f32, at=None):
        if at is None:
            at, place[0] = place[0], place[0] + -(-4 * cols // 32) * 32
            assert place[0] <= nc.sbuf_top, (name, place[0] - nc.sbuf_top)
        return nc.alloc_sbuf_tensor_at(name, [P, cols], dt, offset=at)

    xT = put("xT", DT * S)
    h_hi, h_lo = put("h_hi", DT * S, f32r), put("h_lo", DT * S, f32r)
    raw = put("raw", 2 * CW)
    w_hi, w_lo = put("w_hi", 2 * CW, f32r), put("w_lo", 2 * CW, f32r)
    vec, cst, ones = put("vec", NVEC), put("cst", NCONST), put("ones", P)
    tab64 = put("tab64", 2 * S)
    v4, r4, mhalf = put("v4", 8), put("r4", 8), put("mhalf", 8)
    stats = put("stats", 8)
    lsum, esink, coef = put("lsum", 16), put("esink", 16), put("coef", 16)
    m8 = put("m8", 24)
    widx = put("widx", NB * 16)
    KB = 1024
    mem1 = place[0]
    place[0] += 6 * KB
    mem_k1, mem_v1 = put("mem_k1", 4 * MEM, at=mem1), put("mem_v1", 2 * MEM, at=mem1 + 4 * KB)

    sc0 = place[0]
    place[0] += 30 * KB
    s_sb, p_sb, pT = put("s_sb", 2 * S, at=sc0), put("p_sb", 2 * S, at=sc0 + 4 * KB), put("pT", 2 * S, at=sc0 + 8 * KB)
    o_sb, qraw, rtmp = put("o_sb", S, at=sc0 + 12 * KB), put("qraw", S, at=sc0 + 14 * KB), put("rtmp", S, at=sc0 + 16 * KB)
    qs, qn = put("qs", 2 * S, at=sc0 + 18 * KB), put("qn", 2 * S, at=sc0 + 22 * KB)
    vraw, ysb = put("vraw", S, at=sc0 + 26 * KB), put("ysb", S, at=sc0 + 28 * KB)
    om = put("om", S, at=sc0 + 26 * KB)
    ktmp = put("ktmp", 2 * S, at=sc0 + 4 * KB)
    nsink = put("nsink", 16)
    fa, fb, fc = put("fa", S, at=sc0), put("fb", S, at=sc0 + 2 * KB), put("fc", S, at=sc0 + 4 * KB)
    fd, fe, fg = put("fd", S, at=sc0 + 6 * KB), put("fe", S, at=sc0 + 8 * KB), put("fg", S, at=sc0 + 10 * KB)
    sq, hf, diag = put("sq", 2 * S, at=sc0 + 12 * KB), put("hf", 2 * S, at=sc0 + 16 * KB), put("diag", S, at=sc0 + 20 * KB)

    g0 = place[0]
    half = FT * S * 4
    place[0] += 2 * half
    assert place[0] <= nc.sbuf_top, place[0] - nc.sbuf_top
    g1 = g0 + half
    G_hi, G_lo = put("G_hi", FT * S, f32r, at=g0), put("G_lo", FT * S, f32r, at=g1)
    memn_hi, memn_lo = put("memn_hi", DT * MEM, f32r, at=g0), put("memn_lo", DT * MEM, f32r, at=g0 + 8 * KB)
    memT = put("memT", DT * MEM, at=g1)
    a_k, a_v = put("a_k", 2 * S, at=g0 + 20 * KB), put("a_v", 2 * S, at=g0 + 24 * KB)
    c_hi, c_lo = put("c_hi", 2 * S, f32r, at=g0 + 28 * KB), put("c_lo", 2 * S, f32r, at=g0 + 32 * KB)
    kidx, tab128 = put("kidx", 2 * S, at=g0 + 36 * KB), put("tab128", 2 * S, at=g0 + 40 * KB)
    bias_a, score = put("bias_a", 3 * S, at=g1 + 20 * KB), put("score", 3 * S, at=g1 + 26 * KB)
    mem_k0, mem_v0 = put("mem_k0", 4 * MEM, at=g1 + 32 * KB), put("mem_v0", 2 * MEM, at=g1 + 36 * KB)
    ckv = put("ckv", 2 * S, at=g1 + 38 * KB)
    posi, posf = put("posi", S, i32, at=g1 + 8 * KB), put("posf", S, at=g1 + 10 * KB)
    ang, turns = put("ang", S, at=g1 + 12 * KB), put("turns", S, at=g1 + 14 * KB)
    b_k, b_v = put("b_k", 8 * S, at=g0 + 20 * KB), put("b_v", NB * 256, at=g0 + 36 * KB)
    fold = [put("fold_k", 4 * FPAD, at=g0), put("fold_v", 4 * FPAD, at=g0 + 16 * FPAD)]
    win = put("win", 2 * CW, at=sc0 + 16 * KB)
    win_hi = [put("win_k_hi", 2 * CW, f32r, at=g1), put("win_v_hi", 2 * CW, f32r, at=sc0)]
    win_lo = [put("win_k_lo", 2 * CW, f32r, at=g1 + 8 * KB), put("win_v_lo", 2 * CW, f32r, at=sc0 + 8 * KB)]
    n_k = {"slc": put("n_ks", 8 * S, at=g0 + 18 * KB), "win": put("n_kw", 8 * S, at=g1 + 18 * KB)}
    n_v = {"slc": put("n_vs", NB * 256, at=g0 + 34 * KB), "win": put("n_vw", NB * 256, at=g0 + 38 * KB)}
    cmp_k, cmp_v = put("cmp_k", 2 * 4 * NCMP, at=g0 + 42 * KB), put("cmp_v", 4 * 64, at=g0 + 43 * KB)
    gate = put("gate", NB * 48, at=g1 + 34 * KB)
    hidx, hidt = put("hidx", P, at=g1 + 36 * KB), put("hidt", P, at=g1 + 36 * KB + 512)
    hidf = put("hidf", 4 * P, at=g1 + 37 * KB)
    hid_hi, hid_lo = put("hid_hi", 4 * P, f32r, at=g1 + 39 * KB), put("hid_lo", 4 * P, f32r, at=g1 + 41 * KB)
    zsil = put("zsil", 8 * S, at=g1)
    mem_k, mem_v = [mem_k0, mem_k1], [mem_v0, mem_v1]

    ident = cst[:, CC["ident"]:CC["ident"] + P]

    def V(name, k=0):
        return vec[:, VC[name] + k:VC[name] + k + 1]

    def VD(name, k):
        return vec[:, ds(k + VC[name], 1)]

    def C(name, k=0, n=1):
        return cst[:, CC[name] + k:CC[name] + k + n]

    def causal(b):
        return C("causal", (NB - 1 - b) * P, (b + 1) * P)

    def ST(k, par):
        return stats[:, 2 * k + par:2 * k + par + 1]

    MX, NEGM = range(2)

    def of_pass(tile, g, r, n=1):
        return tile[:, (g % 2) * 8 + r:(g % 2) * 8 + r + n]

    with ExitStack() as ctx:
        def sem(name):
            return ctx.enter_context(nc.semaphore(name))

        def bank(name):
            return ctx.enter_context(nc.psum_tensor(name, [P, 512], f32))

        pj = [bank("pj0"), bank("pj1")]
        ps = [bank("ps0"), bank("ps1")]
        pt = [bank("pt0"), bank("pt1")]
        po = [bank("po0"), bank("po1")]
        px = po[1]

        ld = {n: sem(f"loaded_{n}") for n in ("mem", "x", "vec", "cst", "pos", "tab2")}
        chunk_loaded = [sem("chunk_loaded0"), sem("chunk_loaded1")]
        hi_ready = sem("hi_ready")
        lo_ready = sem("lo_ready")
        chunk_used = sem("chunk_used")
        pj_free = [sem("pj_free0"), sem("pj_free1")]
        setup = sem("setup")
        x_ready = sem("x_ready")
        sq_ready, sq_used = sem("sq_ready"), sem("sq_used")
        var_ready, rs_ready = sem("var_ready"), sem("rs_ready")
        diag_ready, factor_ready = sem("diag_ready"), sem("factor_ready")
        hf_ready, hhi_ready, h_ready = sem("hf_ready"), sem("hhi_ready"), sem("h_ready")
        score_done, score_taken = sem("score_done"), sem("score_taken")
        idx_added = sem("idx_added")
        max_ready, exp_done = sem("max_ready"), sem("exp_done")
        p_turned, pT_ready, pv_done = sem("p_turned"), sem("pT_ready"), sem("pv_done")
        o_scaled, o_turned = sem("o_scaled"), sem("o_turned")
        out_hi, out_ready = sem("out_hi"), sem("out_ready")
        y_ready = sem("y_ready")
        roped = sem("roped")
        v_turned = sem("v_turned")
        act_ready, g_hi_ready, g_ready = sem("act_ready"), sem("g_hi_ready"), sem("g_ready")
        win_summed, win_hi_ready, win_ready = sem("win_summed"), sem("win_hi_ready"), sem("win_ready")
        hid_x, hid_th, hid_f, hid_hi_ready, hid_ready = (
            sem(n) for n in ("hid_x", "hid_th", "hid_f", "hid_hi_ready", "hid_ready"))
        gate_done = sem("gate_done")
        zeroed = sem("zeroed")
        dve_step = sem("dve_step")
        angle_ready, sin_ready = sem("angle_ready"), sem("sin_ready")
        settled = sem("settled")
        stored = sem("stored")

        block = ctx.enter_context(nc.Block())

        @block.sync
        def _(sp):
            sp.dma_start(memT[:, :], memin).then_inc(ld["mem"], 16)
            sp.dma_start(vec[:, :], vecin).then_inc(ld["vec"], 16)
            sp.dma_start(cst[:, :], cstin).then_inc(ld["cst"], 16)
            sp.dma_start(posi[:, :], posin).then_inc(ld["pos"], 16)
            sp.dma_start(xT[:, :], xin).then_inc(ld["x"], 16)
            with sp.Fori(0, NCHUNKS // 2) as i:
                for par in range(2):
                    c = At(par, i, 2)
                    sp.wait_ge(lo_ready, c.v + 1)
                    sp.dma_start(raw[:, par * CW:(par + 1) * CW],
                                 wstream[ds(c.v, 1), :, :].rearrange("a p c -> p (a c)")).then_inc(chunk_loaded[par], 16)
            sp.wait_ge(h_ready, NBASE[-1])
            sp.dma_start(out, xT[:, :]).then_inc(stored, 16)
            sp.wait_ge(stored, 16)

        NORM = {
            "mem": (memT, MEM, "g_mem", 0, memn_hi, memn_lo), "amix": (xT, S, "g_mix", 0, h_hi, h_lo),
            "ckv": (ckv, S, "a_kv_norm", 0, c_hi, c_lo), "affn": (xT, S, "g_ffn", 0, h_hi, h_lo),
            "bmix": (xT, S, "g_mix", DT, h_hi, h_lo), "bffn": (xT, S, "g_ffn", DT, h_hi, h_lo),
            "final1": (xT, S, "g_final", 0, None, None), "conv": (xT, S, "a_norm", 0, h_hi, h_lo),
            "kv2": (xT, S, "kv_norm", 0, h_hi, h_lo), "q2": (xT, S, "b_norm", 0, h_hi, h_lo),
            "final2": (xT, S, "final_norm", 0, None, None)}
        SUMS = [ps[0], ps[1], pt[0], pt[1]]

        def settle(eng):
            eng.sem_inc(settled, 1)

        def sl(start, n):
            return slice(start, start + n) if isinstance(start, int) else ds(start, n)

        def attention_tiles(eng, ph, tile, links=None, per=0):
            tile(ph, 0, 0)
            trips = ph.tiles // 2 - 1
            if trips:
                with eng.Fori(0, trips) as i:
                    if links:
                        links.begin(i, per)
                    tile(ph, i, 1)
                    tile(ph, i, 2)
                if links:
                    links.end(per, trips)
            tile(ph, 0, ph.tiles - 1)

        def later(ph, i, j, u):
            if u < ph.n:
                return i, j, u
            if isinstance(i, int) and j == ph.tiles - 1:
                return None
            return i, j + 1, u - ph.n

        def before(ph, i, j, p):
            if p:
                return i, j, p - 1
            if isinstance(i, int) and j == 0:
                return None
            return i, j - 1, ph.passes - 1

        def unit_of(ph, i, j, u):
            return ph.first_unit + (i * 2 + j) * ph.n + u

        def pass_of(ph, i, j, p):
            return ph.first_pass + (i * 2 + j) * ph.passes + p

        def bank_of(ph, j, p):
            return (j * ph.passes + p) % 2

        def more(ph, i, j):
            return not (isinstance(i, int) and j == ph.tiles - 1)

        def next_chunk(ph, i, j, c):
            return At(CH[ph.name] + (j + 1) * ph.chunks + c, i, 2 * ph.chunks)

        def next_tile(ph, i, j, k):
            per = 3 if ph.name == "aq" else ph.chunks
            return At(TL[ph.name] + (j + 1) * per + k, i, 2 * per)

        @block.gpsimd
        def _(pool):
            nc.gpsimd.memset(ones[:, :], 1.0)
            nc.gpsimd.memset(mhalf[:, :], -0.5)
            nc.gpsimd.memset(score[:, :], 0.0)
            nc.gpsimd.memset(v4[:, :], 1.0).then_inc(setup, 1)

            def inverse_root(name):
                q = NQ[name]
                pool.wait_ge(var_ready, q + 1)
                nc.gpsimd.tensor_tensor(r4[:, :], v4[:, :], mhalf[:, :], ALU.pow).then_inc(rs_ready, 1)

            pool.wait_ge(setup, 1)
            for name in ("mem", "amix", "ckv", "affn"):
                inverse_root(name)
            pool.wait_ge(x_ready, RESIDUALS["down0"] + DT)
            nc.gpsimd.memset(b_k[:, :], 0.0).then_inc(zeroed, 1)
            inverse_root("bmix")
            pool.wait_ge(roped, RP["nk_s"] + 1)
            pool.dma_start(tab64[:, :], tab2in).then_inc(ld["tab2"], 16)
            for name in ("bffn", "final1", "conv"):
                inverse_root(name)
            pool.wait_ge(x_ready, RESIDUALS["cout"] + DT)
            for tile in fold:
                pad = tile[:, :].rearrange("p (g c) -> p g c", g=4)[:, :, S - 1:FPAD]
                last = nc.gpsimd.memset(pad, 0.0)
            last.then_inc(zeroed, 1)
            inverse_root("kv2")
            nc.gpsimd.memset(n_k["win"][:, :], 0.0)
            nc.gpsimd.memset(n_k["slc"][:, :], 0.0).then_inc(zeroed, 1)
            for name in ("q2", "final2"):
                inverse_root(name)

        @block.scalar
        def _(act):
            act.sem_inc(sq_used, 2)

            def split_hi(c):
                if isinstance(c.v, int) and c.v >= NCHUNKS:
                    return
                act.wait_ge(chunk_loaded[c.par], c.half * 16 + 16)
                act.wait_ge(chunk_used, c.v + 1)
                nc.scalar.activation(w_hi[:, c.par * CW:(c.par + 1) * CW], raw[:, c.par * CW:(c.par + 1) * CW],
                                     ACT.Copy).then_inc(hi_ready, 1)

            def take(dst, t, c, n=S, func=ACT.Copy, scale=1.0, rows=slice(0, P)):
                act.wait_ge(chunk_used, c.v + 3)
                nc.scalar.activation(dst, pj[t.par][rows, 0:n], func, scale=scale).then_inc(pj_free[t.par], 1)

            def norm(name, waits):
                src, n, _, _, hi, _ = NORM[name]
                q = NQ[name]
                k = NORMS[q][1]
                for m in range(k):
                    s = NBASE[q] + m
                    sem_, value = waits(m)
                    act.wait_ge(sem_, value)
                    act.wait_ge(sq_used, s + 1)
                    nc.scalar.activation(sq[:, (s % 2) * S:(s % 2) * S + n], src[:, m * n:(m + 1) * n],
                                         ACT.Square).then_inc(sq_ready, 1)
                if hi is None:
                    return
                for m in range(k):
                    s = SBASE[q] + m
                    act.wait_ge(hf_ready, s + 1)
                    nc.scalar.activation(hi[:, m * n:(m + 1) * n], hf[:, (s % 2) * S:(s % 2) * S + n],
                                         ACT.Copy).then_inc(hhi_ready, 1)

            def after(name):
                return lambda m: (x_ready, RESIDUALS[name] + m + 1)

            def turn(t, c, number, dst, src, n=S, func=ACT.Copy, scale=1.0):
                take(vraw[:, 0:n], t, c, n)
                act.wait_ge(v_turned, number + 1)
                return nc.scalar.activation(dst, src, func, scale=scale)

            def bank3(number, lo, n):
                return pt[number % 2][:, :].rearrange("p (b c) -> p b c", b=NB)[:, :, lo:lo + n]

            def query(ph, i, j, first=False):
                c, t = next_chunk(ph, i, j, 0), next_tile(ph, i, j, 0)
                par = (j + 1) % 2
                if ph.units[0][2] == "mem":
                    take(qs[:, par * S:(par + 1) * S], t, c)
                else:
                    r = RP[ph.name] + 1 + j + i * 2
                    act.wait_ge(roped, r + 1)
                    dst = qn[:, par * S:(par + 1) * S] if ph.name == "nq" else qraw[:, :]
                    take(dst, t, c)

            def keys_values(ph, i, j):
                c, t = next_chunk(ph, i, j, 0), next_tile(ph, i, j, 0)
                par = (j + 1) % 2
                take(a_k[0:96, par * S:(par + 1) * S], t + 1, c + 1, rows=slice(0, 96))
                take(a_v[:, par * S:(par + 1) * S], t + 2, c + 1)

            def refill(ph, i, j, k=0):
                split_hi(next_chunk(ph, i, j, k) + 2)

            def softmax(ph, i, j, u):
                at = later(ph, i, j, u)
                if at is None:
                    return
                i, j, u = at
                a = unit_of(ph, i, j, u)
                par = u % 2
                w = ph.keys(u)[1]
                p, _ = ph.split(u)
                g, r = bank_of(ph, j, p), ph.region(u)
                act.wait_ge(max_ready, a + 1)
                act.wait_ge(p_turned, a + 1)
                if ph.name == "bq":
                    h = (i * 2 + j) * 2 + ph.units[u][0]
                    settle(act)
                    nc.scalar.activation(of_pass(esink, g, r), nsink[:, sl(h, 1)], ACT.Exp, scale=-1.0,
                                         bias=ST(NEGM, par))
                nc.scalar.activation(p_sb[:, par * S:par * S + w], s_sb[:, par * S:par * S + w], ACT.Exp,
                                     scale=ph.scale, bias=ST(NEGM, par),
                                     accum_out=of_pass(lsum, g, r)).then_inc(exp_done, 1)

            def bring(ph, i, j, u):
                a = unit_of(ph, i, j, u)
                par = u % 2
                w = ph.keys(u)[1]
                act.wait_ge(p_turned, a + 3)
                act.wait_ge(pv_done, a + 1)
                rows = slice(0, min(w, P))
                n = max(w, P)
                nc.scalar.activation(pT[rows, par * S:par * S + n], pt[par][rows, 0:n],
                                     ACT.Copy).then_inc(pT_ready, 1)

            def output_hi(ph, i, j):
                t = i * 2 + j
                o = (ph.out0 + t) * S
                if ph.name == "nq":
                    act.wait_ge(y_ready, t + 1)
                    src = ysb
                else:
                    act.wait_ge(o_turned, ph.first_tile + t + 1)
                    src = po[bank_of(ph, j, ph.passes - 1)]
                settle(act)
                nc.scalar.activation(G_hi[:, sl(o, S)], src[:, :], ACT.Copy).then_inc(out_hi, 1)

            def tile(ph, i, j):
                for u in range(ph.n):
                    p, v = ph.split(u)
                    bring(ph, i, j, u)
                    if more(ph, i, j):
                        if u == ph.at_query:
                            query(ph, i, j)
                        if u == ph.at_refill:
                            refill(ph, i, j)
                        if u == 2 and ph.name == "aq":
                            keys_values(ph, i, j)
                        if u == 3 and ph.name == "aq":
                            refill(ph, i, j, 1)
                    softmax(ph, i, j, u + 2)
                    last = before(ph, i, j, p)
                    if v == ph.at_hi and p == 0 and last:
                        output_hi(ph, *last[:2])

            def attention(name):
                ph = ATT[name]
                query(ph, 0, -1)
                refill(ph, 0, -1)
                if name == "aq":
                    keys_values(ph, 0, -1)
                    refill(ph, 0, -1, 1)
                softmax(ph, 0, 0, 0)
                softmax(ph, 0, 0, 1)
                attention_tiles(act, ph, tile)
                output_hi(ph, 0, ph.tiles - 1)

            def splits(stage, per, trips):
                with act.Fori(0, trips) as i:
                    for k in range(per):
                        split_hi(At(CH[stage] + k + 2, i, per))

            def feed_forward(l):
                up, base = CH[f"up{l}"], TL[f"up{l}"]
                with act.Fori(0, FT) as i:
                    split_hi(At(up + 2, i, 2))
                    t = At(base, i, 2)
                    act.wait_ge(pj_free[t.par], t.half + 2)
                    nc.scalar.activation(fb[:, :], fa[:, :], ACT.Silu).then_inc(act_ready, 1)
                    split_hi(At(up + 3, i, 2))
                    t = At(base + 1, i, 2)
                    act.wait_ge(pj_free[t.par], t.half + 2)
                    settle(act)
                    nc.scalar.activation(G_hi[:, ds(i * S, S)], fc[:, :], ACT.Copy).then_inc(g_hi_ready, 1)
                splits(f"down{l}", 2 * DOWN_CHUNKS, DT // 2)

            split_hi(At(0))
            split_hi(At(1))
            norm("mem", lambda m: (ld["mem"], 16))
            number = TN["memv"]
            for l in range(2):
                for k in range(4):
                    c, t = At(CH["mem"] + 4 * l + k), At(TL["mem"] + 4 * l + k)
                    split_hi(c + 2)
                    if k >= 2:
                        turn(t, c, number, mem_v[l][:, :].rearrange("p (b c) -> p b c", b=2)[:, :, (k - 2) * P:(k - 1) * P],
                             pt[number % 2][:, 0:MEM].rearrange("p (b c) -> p b c", b=2), n=MEM)
                        number += 1
            for k, tab in enumerate((tab64, tab128)):
                act.wait_ge(angle_ready, k + 1)
                nc.scalar.activation(tab[:, S:2 * S], ang[:, :], ACT.Sin)
                nc.scalar.activation(tab[:, 0:S], turns[:, :], ACT.Sin).then_inc(sin_ready, 1)
            norm("amix", lambda m: (ld["x"], 16))
            for k in range(4):
                c, t = At(CH["afront"] + k), At(TL["afront"] + k)
                split_hi(c + 2)
                if k < 2:
                    take(ckv[:, k * S:(k + 1) * S], t, c)
                elif k == 2:
                    act.wait_ge(roped, RP["krope"] + 1)
                    take(qraw[:, :], t, c)
                    act.wait_ge(v_turned, TN["widx"] + 1)
                    nc.scalar.activation(widx[:, :].rearrange("p (b c) -> p b c", b=NB), bank3(TN["widx"], 0, 16),
                                         ACT.Copy, scale=1024.0 ** -0.5)
                else:
                    act.wait_ge(roped, RP["kidx"] + 1)
                    take(qraw[:, :], t, c)
            tk = TL["afront"]
            act.wait_ge(roped, RP["idx"] + 1)
            norm("ckv", lambda m: (pj_free[(tk + m) % 2], (tk + m) // 2 + 2))

            def idx_query(i, j):
                c, t = At(CH["idx"] + 1 + j, i, 2), At(TL["idx"] + 1 + j, i, 2)
                split_hi(c + 2)
                act.wait_ge(roped, RP["idx"] + 1 + j + i * 2 + 1)
                take(qraw[:, :], t, c)

            def idx_tile(i, j, more):
                t = i * 2 + j
                for u, (hh, b) in enumerate(IDX_UNITS):
                    s = t * len(IDX_UNITS) + u
                    w = (b + 1) * P
                    act.wait_ge(score_done, s + 1)
                    act.wait_ge(idx_added, s + 1)
                    nc.scalar.activation(s_sb[:, (u % 2) * S:(u % 2) * S + w], ps[u % 2][:, 0:w],
                                         ACT.Relu).then_inc(score_taken, 1)
                    if u == 1 and more:
                        idx_query(i, j)

            idx_query(0, -1)
            with act.Fori(0, 3) as i:
                idx_tile(i, 0, True)
                idx_tile(i, 1, True)
            idx_tile(3, 0, True)
            idx_tile(3, 1, False)
            attention("aq")
            attention("amem")
            splits("aout", 4, DT // 2)
            norm("affn", after("aout"))
            feed_forward(0)

            norm("bmix", after("down0"))
            for k in range(2):
                c, t = At(CH["bfront"] + k), At(TL["bfront"] + k)
                split_hi(c + 2)
                act.wait_ge(roped, RP["bk"] + k + 1)
                take(qraw[:, :], t, c)
            for k in range(2):
                c, t = At(CH["bfront"] + 2 + k), At(TL["bfront"] + 2 + k)
                split_hi(c + 2)
                turn(t, c, TN["bv"] + k, b_v[:, :].rearrange("p (b c) -> p b c", b=NB)[:, :, k * P:(k + 1) * P],
                     bank3(TN["bv"] + k, 0, P))
            attention("bq")
            attention("bmem")
            splits("bout", 4, DT // 2)
            norm("bffn", after("bout"))
            feed_forward(1)
            norm("final1", after("down1"))

            norm("conv", lambda m: (h_ready, NBASE[NQ["final1"]] + m + 1))
            with act.Fori(0, CT) as i:
                c, t = At(CH["conv"], i, 4), At(TL["conv"], i, 4)
                split_hi(c + 2)
                take(fa[:, :], t, c)
                split_hi(c + 3)
                split_hi(c + 4)
                take(fd[:, :], t + 2, c + 2, func=ACT.Silu)
                split_hi(c + 5)
                act.wait_ge(pj_free[(t + 3).par], (t + 3).half + 2)
                settle(act)
                nc.scalar.activation(G_hi[:, ds(i * S, S)], fg[:, :], ACT.Copy).then_inc(g_hi_ready, 1)
            splits("cout", 4, DT // 2)
            norm("kv2", after("cout"))

            dve_pieces = [(which, part) for which in range(2) for part in range(2)]
            act.wait_ge(zeroed, 2)

            def window_hi(k):
                which, part = dve_pieces[k]
                act.wait_ge(win_summed, k + 1)
                nc.scalar.activation(win_hi[which][:, part * CW:(part + 1) * CW], win[:, part * CW:(part + 1) * CW],
                                     ACT.Copy).then_inc(win_hi_ready, 1)

            for k in range(4):
                c, t = At(CH["cmp_kv"] + k), At(TL["cmp_kv"] + k)
                which, pair = k // 2, k % 2
                split_hi(c + 2)
                act.wait_ge(chunk_used, c.v + 3)
                for g in range(2):
                    at, rows = (2 * pair + g) * FPAD, slice(g * 64, g * 64 + 64)
                    nc.scalar.activation(fold[which][0:64, at:at + S], pj[t.par][rows, :], ACT.Copy)
                    last = nc.scalar.activation(fold[which][64:P, at:at + S - 1], pj[t.par][rows, 1:S], ACT.Copy)
                last.then_inc(pj_free[t.par], 1)
                if k >= 2:
                    window_hi(k - 2)
            window_hi(2)
            window_hi(3)
            for k in range(4):
                c = At(CH["cmp"] + 2 * k)
                split_hi(c + 2)
                split_hi(c + 3)
                act.wait_ge(hid_x, k + 1)
                nc.scalar.activation(hidt[:, :], hidt[:, :], ACT.Tanh, scale=0.7978845608028654).then_inc(hid_th, 1)
                act.wait_ge(hid_f, k + 1)
                nc.scalar.activation(hid_hi[:, k * P:(k + 1) * P], hidf[:, k * P:(k + 1) * P],
                                     ACT.Copy).then_inc(hid_hi_ready, 1)
            for s, (kn, vn, branch) in enumerate((("nk_s", "nv_s", "slc"), ("nk_w", "nv_w", "win"))):
                if s:
                    c, t = At(CH["cmp2"]), At(TL["cmp2"] + 1)
                    split_hi(c + 2)
                    turn(t, c, TN["cmpv"], cmp_v[0:NCMP, :].rearrange("p (g c) -> p g c", g=4),
                         pt[TN["cmpv"] % 2][0:NCMP, :].rearrange("p (g c) -> p g c", g=4)[:, :, 0:64], n=P)
                stage = ("nkv_s", "nkv_w")[s]
                for k in range(2):
                    c, t = At(CH[stage] + k), At(TL[stage] + k)
                    split_hi(c + 2)
                    act.wait_ge(roped, RP[kn] + k + 1)
                    take(qraw[:, :], t, c)
                for k in range(2):
                    c, t = At(CH[stage] + 2 + k), At(TL[stage] + 2 + k)
                    split_hi(c + 2)
                    turn(t, c, TN[vn] + k,
                         n_v[branch][:, :].rearrange("p (b c) -> p b c", b=NB)[:, :, k * P:(k + 1) * P],
                         bank3(TN[vn] + k, 0, P))
            act.wait_ge(roped, RP["nq"] + 1)
            norm("q2", after("cout"))
            c, t = At(CH["gates"]), At(TL["gates"])
            split_hi(c + 2)
            turn(t, c, TN["gates"], gate[:, :].rearrange("p (b c) -> p b c", b=NB), bank3(TN["gates"], 0, 48),
                 func=ACT.Sigmoid).then_inc(gate_done, 1)
            with act.Fori(0, 4) as i:
                for k in range(2):
                    c, t = At(CH["nz"] + k, i, 2), At(TL["nz"] + k, i, 2)
                    split_hi(c + 2)
                    take(zsil[:, ds((i * 2 + k) * S, S)], t, c, func=ACT.Silu)
            attention("nq")
            with act.Fori(0, DT // 2 - 1) as i:
                for k in range(2):
                    split_hi(At(CH["nout"] + k + 2, i, 2))
            norm("final2", after("nout"))

        @block.vector
        def _(dve):
            link = Links(dve, dve_step)
            for b in range(2):
                dve.sem_inc(pj_free[b], 1)
            dve.sem_inc(lo_ready, 2)
            dve.sem_inc(score_taken, 2)
            dve.sem_inc(idx_added, 2)
            dve.sem_inc(roped, 1)
            dve.sem_inc(out_ready, 1)
            dve.sem_inc(g_ready, 1)
            dve.wait_ge(setup, 1)

            def split_lo(c):
                if isinstance(c.v, int) and c.v >= NCHUNKS:
                    return
                dve.wait_ge(hi_ready, c.v + 1)
                here = slice(c.par * CW, (c.par + 1) * CW)
                nc.vector.tensor_tensor(w_lo[:, here], raw[:, here], w_hi[:, here].bitcast(f32),
                                        ALU.subtract).then_inc(lo_ready, 1)

            def complete(c):
                dve.wait_ge(chunk_used, c.v + 3)

            def norm(name):
                src, n, gain, first, hi, lo = NORM[name]
                q = NQ[name]
                k = NORMS[q][1]
                blocks = n // P
                dve.wait_ge(sq_used, NBASE[q + 1] + 2)
                for b in range(blocks):
                    last = nc.vector.tensor_scalar(v4[:, b:b + 1], SUMS[b][:, 0:1], 1.0 / (k * P), EPS, ALU.mult, ALU.add)
                last.then_inc(var_ready, 1)
                dve.wait_ge(rs_ready, q + 1)
                for b in range(blocks):
                    last = nc.vector.tensor_scalar(diag[:, b * P:(b + 1) * P], ident, r4[:, b:b + 1], None, ALU.mult)
                last.then_inc(diag_ready, 1)
                dve.wait_ge(factor_ready, q + 1)

                def low(m):
                    s = SBASE[q] + m
                    dve.wait_ge(hhi_ready, s + 1)
                    here = slice(m * n, (m + 1) * n)
                    nc.vector.tensor_tensor(lo[:, here], hf[:, (s % 2) * S:(s % 2) * S + n], hi[:, here].bitcast(f32),
                                            ALU.subtract).then_inc(h_ready, 1)

                for m in range(k):
                    here = slice(m * n, (m + 1) * n)
                    if hi is None:
                        nc.vector.scalar_tensor_tensor(out=src[:, here], in0=src[:, here], scalar=V(gain, first + m),
                                                       in1=px[:, 0:n], op0=ALU.mult, op1=ALU.mult).then_inc(h_ready, 1)
                        continue
                    s = SBASE[q] + m
                    if m >= 2:
                        dve.wait_ge(h_ready, NBASE[q] + m - 1)
                    nc.vector.scalar_tensor_tensor(out=hf[:, (s % 2) * S:(s % 2) * S + n], in0=src[:, here],
                                                   scalar=V(gain, first + m), in1=px[:, 0:n],
                                                   op0=ALU.mult, op1=ALU.mult).then_inc(hf_ready, 1)
                    if m:
                        low(m - 1)
                if hi is not None:
                    low(k - 1)
                dve.wait_ge(h_ready, NBASE[q + 1])

            def rope(dst, src, tab, mask, t):
                rope_start(dst, src, tab, mask, t)
                return rope_end(dst, tab)

            def rope_start(dst, src, tab, mask, t):
                dve.wait_ge(pj_free[t.par], t.half + 2)
                nc.vector.tensor_tensor(dst, src, tab[:, 0:S], ALU.mult)
                link(nc.vector.stream_shuffle(rtmp[:, :], src, mask))

            def rope_end(dst, tab):
                link(nc.vector.tensor_tensor(rtmp[:, :], rtmp[:, :], tab[:, S:2 * S], ALU.mult))
                return nc.vector.tensor_tensor(dst, dst, rtmp[:, :], ALU.add)

            def spread_keys(dst, pair):
                for g in range(2):
                    for hh in range(2):
                        col = ((2 * pair + g) * 2 + hh) * S
                        last = nc.vector.tensor_copy(dst[hh * 64:hh * 64 + 64, col:col + S], ktmp[g * 64:g * 64 + 64, 0:S])
                return last

            def query(ph, i, j, half):
                t = next_tile(ph, i, j, 0)
                par = (j + 1) % 2
                if ph.units[0][2] == "mem":
                    return
                dst = qs[:, par * S:(par + 1) * S]
                src = qn[:, par * S:(par + 1) * S] if ph.name == "nq" else qraw[:, :]
                tab, mask = (tab128, SHUF128) if ph.name == "aq" else (tab64, SHUF64)
                if half == 0:
                    rope_start(dst, src, tab, mask, t)
                else:
                    rope_end(dst, tab).then_inc(roped, 1)

            def refill(ph, i, j, k=0):
                split_lo(next_chunk(ph, i, j, k) + 2)

            def bias(ph, u):
                _, b, branch = ph.units[u]
                if branch == "topk" and b:
                    return bias_a[:, (b - 1) * S:(b - 1) * S + (b + 1) * P]
                if branch == "mem":
                    return C("causal", 0, MEM)
                if branch == "band":
                    return C("band", P, P) if b == 0 else C("band", 0, 2 * P)
                if branch == "cmp":
                    return C("cmp", b * NCMP, NCMP)
                return causal(b)

            def maximum(ph, i, j, u):
                at = later(ph, i, j, u)
                if at is None:
                    return
                i, j, u = at
                s, a = ph.first_score + (i * 2 + j) * ph.n + u, unit_of(ph, i, j, u)
                par = u % 2
                w = ph.keys(u)[1]
                dve.wait_ge(score_done, s + 1)
                dve.wait_ge(exp_done, a + 1)
                settle(dve)
                nc.vector.tensor_tensor_reduce(out=s_sb[:, par * S:par * S + w], in0=ps[par][:, 0:w], in1=bias(ph, u),
                                               scale=1.0, scalar=-3.0e38, op0=ALU.add, op1=ALU.max,
                                               accum_out=ST(MX, par)).then_inc(score_taken, 1)
                dve.wait_ge(score_taken, s + 3)
                if ph.name == "bq":
                    h = (i * 2 + j) * 2 + ph.units[u][0]
                    nc.vector.tensor_scalar(ST(NEGM, par), ST(MX, par), -ph.scale, nsink[:, sl(h, 1)],
                                            ALU.mult, ALU.min).then_inc(max_ready, 1)
                else:
                    nc.vector.tensor_scalar(ST(NEGM, par), ST(MX, par), -ph.scale, None, ALU.mult).then_inc(max_ready, 1)

            def scale_pass(ph, i, j, p):
                t, g = i * 2 + j, bank_of(ph, j, p)
                end = unit_of(ph, i, j, (p + 1) * ph.m - 1)
                n = ph.m
                dve.wait_ge(exp_done, end + 3)
                total, c = of_pass(lsum, g, 0, n), of_pass(coef, g, 0, n)
                if ph.name == "bq":
                    link(nc.vector.tensor_tensor(c, total, of_pass(esink, g, 0, n), ALU.add))
                    total = c
                link(nc.vector.reciprocal(c, total))
                if ph.name == "nq":
                    gates = gate[:, :].rearrange("p (b c) -> p b c", b=NB)[:, :, sl(t * 2 + p * 16, 2)]
                    c3 = c.rearrange("p (b h) -> p b h", b=NB)
                    link(nc.vector.tensor_tensor(c3, c3, gates, ALU.mult))
                dve.wait_ge(pv_done, end + 3)
                if ph.first_tile or not (isinstance(i, int) and j == 0):
                    dve.wait_ge(o_turned, ph.first_tile + t)
                settle(dve)
                dst = o_sb if p == 0 else om
                scaled = nc.vector.tensor_tensor(dst[:, :].rearrange("p (r c) -> p r c", r=n),
                                                 po[g][:, :].rearrange("p (r c) -> p r c", r=n),
                                                 c.unsqueeze(2).broadcast_to([P, n, ph.dv]), ALU.mult)
                if p:
                    link(scaled)
                    scaled = nc.vector.tensor_tensor(o_sb[:, :], o_sb[:, :], om[:, :], ALU.add)
                scaled.then_inc(o_scaled, 1)
                dve.wait_ge(o_scaled, pass_of(ph, i, j, p) + 1)

            def gate_output(ph, i, j):
                t = i * 2 + j
                dve.wait_ge(o_turned, ph.first_tile + t + 1)
                dve.wait_ge(out_ready, ph.first_tile + t + 1)
                nc.vector.tensor_tensor(ysb[:, :], po[bank_of(ph, j, ph.passes - 1)][:, :], zsil[:, sl(t * S, S)],
                                        ALU.mult).then_inc(y_ready, 1)

            def output_lo(ph, i, j):
                t = i * 2 + j
                o = (ph.out0 + t) * S
                src = ysb if ph.name == "nq" else po[bank_of(ph, j, ph.passes - 1)]
                dve.wait_ge(out_hi, ph.first_tile + t + 1)
                nc.vector.tensor_tensor(G_lo[:, sl(o, S)], src[:, :], G_hi[:, sl(o, S)].bitcast(f32),
                                        ALU.subtract).then_inc(out_ready, 1)

            def tile(ph, i, j):
                for u in range(ph.n):
                    p, v = ph.split(u)
                    maximum(ph, i, j, u + 2)
                    last = before(ph, i, j, p)
                    if last and v == ph.at_scale:
                        scale_pass(ph, *last)
                    if more(ph, i, j):
                        if u == ph.at_query:
                            query(ph, i, j, 0)
                        if u == ph.at_query + (0 if ph.name == "aq" else 1):
                            query(ph, i, j, 1)
                        if u == ph.at_refill:
                            refill(ph, i, j)
                        if u == 3 and ph.name == "aq":
                            refill(ph, i, j, 1)
                    if last and p == 0:
                        if v == ph.at_gate and ph.name == "nq":
                            gate_output(ph, *last[:2])
                        if v == ph.at_lo:
                            output_lo(ph, *last[:2])

            LINKS = {"aq": 2 * (2 + 1), "amem": 0, "bq": 2 * (2 + 2), "bmem": 0, "nq": 2 * (2 + 8)}

            def attention(name):
                ph = ATT[name]
                query(ph, 0, -1, 0)
                query(ph, 0, -1, 1)
                refill(ph, 0, -1)
                if name == "aq":
                    refill(ph, 0, -1, 1)
                maximum(ph, 0, 0, 0)
                maximum(ph, 0, 0, 1)
                attention_tiles(dve, ph, tile, link, LINKS[name])
                end = ph.tiles - 1
                scale_pass(ph, 0, end, ph.passes - 1)
                if ph.name == "nq":
                    gate_output(ph, 0, end)
                output_lo(ph, 0, end)

            def residual(stage, per):
                def two(i, last=False):
                    for j in range(2):
                        for k in range(per):
                            split_lo(At(CH[stage] + j * per + k + 2, i, 2 * per))
                        c, t = At(CH[stage] + (j + 1) * per - 1, i, 2 * per), At(TL[stage] + j, i, 2)
                        complete(c)
                        here = xT[:, sl((i * 2 + j) * S, S)]
                        nc.vector.tensor_tensor(here, here, pj[t.par][:, :], ALU.add).then_inc(pj_free[t.par], 1)
                        dve.wait_ge(pj_free[t.par], t.half + 2)
                        dve.sem_inc(x_ready, 1)

                trips = DT // 2 - (1 if stage == "nout" else 0)
                with dve.Fori(0, trips) as i:
                    two(i)
                if stage == "nout":
                    two(trips)

            def feed_forward(l):
                up, base = CH[f"up{l}"], TL[f"up{l}"]
                with dve.Fori(0, FT) as i:
                    link.begin(i, 2)
                    c, t = At(up, i, 2), At(base, i, 2)
                    split_lo(c + 2)
                    complete(c)
                    w = [VD("f_conv_w", i + (l * 3 + j) * FT) for j in range(3)]
                    a = pj[t.par]
                    link(nc.vector.tensor_scalar(fa[:, :], a[:, :], w[2], VD("f_conv_b", i + l * FT), ALU.mult, ALU.add))
                    link(nc.vector.scalar_tensor_tensor(out=fa[:, 1:S], in0=a[:, 0:S - 1], scalar=w[1], in1=fa[:, 1:S],
                                                        op0=ALU.mult, op1=ALU.add))
                    nc.vector.scalar_tensor_tensor(out=fa[:, 2:S], in0=a[:, 0:S - 2], scalar=w[0], in1=fa[:, 2:S],
                                                   op0=ALU.mult, op1=ALU.add).then_inc(pj_free[t.par], 1)
                    split_lo(c + 3)
                    complete(c + 1)
                    dve.wait_ge(act_ready, i + (l * FT + 1))
                    dve.wait_ge(g_ready, i + (l * FT + 1))
                    nc.vector.tensor_tensor(fc[:, :], fb[:, :], pj[(t + 1).par][:, :],
                                            ALU.mult).then_inc(pj_free[(t + 1).par], 1)
                    dve.wait_ge(g_hi_ready, i + (l * FT + 1))
                    nc.vector.tensor_tensor(G_lo[:, ds(i * S, S)], fc[:, :], G_hi[:, ds(i * S, S)].bitcast(f32),
                                            ALU.subtract).then_inc(g_ready, 1)
                link.end(2, FT)
                residual(f"down{l}", DOWN_CHUNKS)

            split_lo(At(0))
            split_lo(At(1))
            dve.wait_ge(ld["cst"], 16)
            dve.wait_ge(ld["vec"], 16)
            nc.vector.tensor_scalar(nsink[:, :], vec[:, VC["sinks"]:VC["sinks"] + 16], -1.0, None, ALU.mult)
            norm("mem")
            for l in range(2):
                for k in range(4):
                    c, t = At(CH["mem"] + 4 * l + k), At(TL["mem"] + 4 * l + k)
                    split_lo(c + 2)
                    if k < 2:
                        complete(c)
                        for hh in range(2):
                            last = nc.vector.tensor_scalar(mem_k[l][:, (2 * k + hh) * MEM:(2 * k + hh + 1) * MEM],
                                                           pj[t.par][:, 0:MEM], C("half", hh), None, ALU.mult)
                        last.then_inc(pj_free[t.par], 1)
            dve.wait_ge(ld["pos"], 16)
            link(nc.vector.tensor_copy(posf[:, :], posi[:, :]))
            for k, (width, tab) in enumerate((("64", tab64), ("128", tab128))):
                if k:
                    dve.wait_ge(sin_ready, k)
                link(nc.vector.tensor_scalar(ang[:, :], posf[:, :], C("inv" + width), None, ALU.mult))
                link(nc.vector.tensor_scalar(turns[:, :], ang[:, :], 1.0 / TWO_PI, ROUNDER, ALU.mult, ALU.add))
                link(nc.vector.tensor_scalar(turns[:, :], turns[:, :], ROUNDER, None, ALU.subtract))
                for part in (PI_HI, PI_LO):
                    link(nc.vector.scalar_tensor_tensor(out=ang[:, :], in0=turns[:, :], scalar=-part, in1=ang[:, :],
                                                        op0=ALU.mult, op1=ALU.add))
                link(nc.vector.tensor_scalar(ang[:, :], ang[:, :], 3.1415925, -3.1415925, ALU.min, ALU.max))
                link(nc.vector.scalar_tensor_tensor(out=turns[:, :], in0=ang[:, :], scalar=-1.0, in1=ang[:, :],
                                                    op0=ALU.mult, op1=ALU.max))
                nc.vector.tensor_scalar(turns[:, :], turns[:, :], -1.0, TWO_PI / 4, ALU.mult,
                                        ALU.add).then_inc(angle_ready, 1)
            for k, (width, tab) in enumerate((("64", tab64), ("128", tab128))):
                dve.wait_ge(sin_ready, k + 1)
                link(nc.vector.tensor_scalar(tab[:, S:2 * S], tab[:, S:2 * S], C("sgn" + width), None, ALU.mult))
            norm("amix")
            for k in range(4):
                c, t = At(CH["afront"] + k), At(TL["afront"] + k)
                split_lo(c + 2)
                if k == 2:
                    link(rope(ktmp[:, 0:S], qraw[:, :], tab128, SHUF128, t))
                    for par in range(2):
                        last = nc.vector.tensor_copy(a_k[96:P, par * S:(par + 1) * S], ktmp[96:P, 0:S])
                    last.then_inc(roped, 1)
                if k == 3:
                    link(rope(ktmp[:, S:2 * S], qraw[:, :], tab64, SHUF64, t))
                    for hh in range(2):
                        last = nc.vector.tensor_scalar(kidx[:, hh * S:(hh + 1) * S], ktmp[:, S:2 * S], C("half", hh), None,
                                                       ALU.mult)
                    last.then_inc(roped, 1)
            norm("ckv")

            def idx_query(i, j):
                c, t = At(CH["idx"] + 1 + j, i, 2), At(TL["idx"] + 1 + j, i, 2)
                par = (j + 1) % 2
                split_lo(c + 2)
                rope(qs[:, par * S:(par + 1) * S], qraw[:, :], tab64, SHUF64, t).then_inc(roped, 1)

            def idx_tile(i, j, more):
                t = i * 2 + j
                for u, (hh, b) in enumerate(IDX_UNITS):
                    s = t * len(IDX_UNITS) + u
                    w = (b + 1) * P
                    here = score[:, (b - 1) * S:(b - 1) * S + w]
                    dve.wait_ge(score_taken, s + 3)
                    dve.wait_ge(idx_added, s + 1)
                    nc.vector.scalar_tensor_tensor(out=here, in0=s_sb[:, (u % 2) * S:(u % 2) * S + w],
                                                   scalar=widx[:, sl(b * 16 + t * 2 + hh, 1)], in1=here,
                                                   op0=ALU.mult, op1=ALU.add).then_inc(idx_added, 1)
                    if u == 1 and more:
                        idx_query(i, j)

            idx_query(0, -1)
            with dve.Fori(0, 3) as i:
                link.begin(i, 4)
                idx_tile(i, 0, True)
                idx_tile(i, 1, True)
            link.end(4, 3)
            idx_tile(3, 0, True)
            idx_tile(3, 1, False)
            rows = [(b, score[:, (b - 1) * S:(b - 1) * S + (b + 1) * P], m8[:, (b - 1) * 8:b * 8]) for b in range(1, NB)]
            dve.wait_ge(idx_added, IDX_SCORES + 2)
            for b, here, _ in rows:
                link.mark(nc.vector.tensor_tensor(here, here, causal(b), ALU.add))
            link.catch()
            with dve.Fori(0, TOPK // 8) as i:
                link.begin(i, 6)
                for b, here, best in rows:
                    link.mark(nc.vector.max(best, here))
                link.catch()
                settle(dve)
                for b, here, best in rows:
                    link.mark(nc.vector.match_replace(here, best, here, TAKEN))
                link.catch()
            link.end(6, TOPK // 8)
            for b, here, _ in rows:
                link.mark(nc.vector.tensor_scalar(bias_a[:, (b - 1) * S:(b - 1) * S + (b + 1) * P], here, -2e38, NEG,
                                                  ALU.is_gt, ALU.mult))
            link.catch()
            attention("aq")
            attention("amem")
            residual("aout", 2)
            norm("affn")
            feed_forward(0)

            norm("bmix")
            dve.wait_ge(zeroed, 1)
            for k in range(4):
                c, t = At(CH["bfront"] + k), At(TL["bfront"] + k)
                split_lo(c + 2)
                if k < 2:
                    link(rope(ktmp[:, 0:S], qraw[:, :], tab64, SHUF64, t))
                    spread_keys(b_k, k).then_inc(roped, 1)
            attention("bq")
            attention("bmem")
            residual("bout", 2)
            norm("bffn")
            feed_forward(1)
            norm("final1")

            norm("conv")
            with dve.Fori(0, CT) as i:
                link.begin(i, 4)
                c, t = At(CH["conv"], i, 4), At(TL["conv"], i, 4)
                split_lo(c + 2)
                split_lo(c + 3)
                dve.wait_ge(pj_free[t.par], t.half + 2)
                complete(c + 1)
                nc.vector.tensor_tensor(fb[:, :], fa[:, :], pj[(t + 1).par][:, :],
                                        ALU.mult).then_inc(pj_free[(t + 1).par], 1)
                dve.wait_ge(pj_free[(t + 1).par], (t + 1).half + 2)
                w = [VD("a_conv_w", i + j * CT) for j in range(3)]
                link(nc.vector.tensor_scalar(fc[:, :], fb[:, :], w[2], None, ALU.mult))
                link(nc.vector.scalar_tensor_tensor(out=fc[:, 1:S], in0=fb[:, 0:S - 1], scalar=w[1], in1=fc[:, 1:S],
                                                    op0=ALU.mult, op1=ALU.add))
                link(nc.vector.scalar_tensor_tensor(out=fc[:, 2:S], in0=fb[:, 0:S - 2], scalar=w[0], in1=fc[:, 2:S],
                                                    op0=ALU.mult, op1=ALU.add))
                split_lo(c + 4)
                dve.wait_ge(pj_free[t.par], t.half + 1 + 2)
                link(nc.vector.tensor_tensor(fe[:, :], fc[:, :], fd[:, :], ALU.mult))
                split_lo(c + 5)
                complete(c + 3)
                dve.wait_ge(g_ready, i + (2 * FT + 1))
                nc.vector.tensor_tensor(fg[:, :], fe[:, :], pj[(t + 3).par][:, :],
                                        ALU.mult).then_inc(pj_free[(t + 3).par], 1)
                dve.wait_ge(g_hi_ready, i + (2 * FT + 1))
                nc.vector.tensor_tensor(G_lo[:, ds(i * S, S)], fg[:, :], G_hi[:, ds(i * S, S)].bitcast(f32),
                                        ALU.subtract).then_inc(g_ready, 1)
            link.end(4, CT)
            residual("cout", 2)
            norm("kv2")

            for k in range(2):
                split_lo(At(CH["cmp_kv"] + k + 2))
            for which in range(2):
                for k in range(2):
                    split_lo(At(CH["cmp_kv"] + 2 * which + k + 2)) if which else None
                t = At(TL["cmp_kv"] + 2 * which + 1)
                dve.wait_ge(pj_free[t.par], t.half + 2)
                for part in range(2):
                    n = which * 2 + part
                    here = slice(part * CW, (part + 1) * CW)
                    tokens = fold[which][:, :].rearrange("p (g c) -> p g c", g=4)[:, :, 16 * part:16 * (part + NCMP)]
                    tokens = tokens.rearrange("p g (n l t) -> p l g n t", l=CB, t=2)[:, :, :, :, 0]
                    at = VC["pos_v" if which else "pos_k"] + part * CB
                    positions = vec[:, at:at + CB].unsqueeze(2).unsqueeze(3).broadcast_to([P, CB, 4, NCMP])
                    if which:
                        dve.wait_ge(win_ready, n - 1)
                    nc.vector.tensor_tensor(win[:, here].rearrange("p (l g n) -> p l g n", l=CB, g=4), tokens, positions,
                                            ALU.add).then_inc(win_summed, 1)
                for part in range(2):
                    n = which * 2 + part
                    here = slice(part * CW, (part + 1) * CW)
                    dve.wait_ge(win_hi_ready, n + 1)
                    nc.vector.tensor_tensor(win_lo[which][:, here], win[:, here], win_hi[which][:, here].bitcast(f32),
                                            ALU.subtract).then_inc(win_ready, 1)
            for k in range(4):
                c, t = At(CH["cmp"] + 2 * k), At(TL["cmp"] + k)
                split_lo(c + 2)
                split_lo(c + 3)
                complete(c + 1)
                nc.vector.tensor_copy(hidx[:, :], pj[t.par][:, 0:P]).then_inc(pj_free[t.par], 1)
                dve.wait_ge(pj_free[t.par], t.half + 2)
                link(nc.vector.tensor_tensor(hidt[:, :], hidx[:, :], hidx[:, :], ALU.mult))
                link(nc.vector.tensor_scalar(hidt[:, :], hidt[:, :], 0.044715, 1.0, ALU.mult, ALU.add))
                nc.vector.tensor_tensor(hidt[:, :], hidt[:, :], hidx[:, :], ALU.mult).then_inc(hid_x, 1)
                dve.wait_ge(hid_th, k + 1)
                link(nc.vector.tensor_scalar(hidt[:, :], hidt[:, :], 0.5, 0.5, ALU.mult, ALU.add))
                nc.vector.tensor_tensor(hidf[:, k * P:(k + 1) * P], hidt[:, :], hidx[:, :], ALU.mult).then_inc(hid_f, 1)
                dve.wait_ge(hid_hi_ready, k + 1)
                nc.vector.tensor_tensor(hid_lo[:, k * P:(k + 1) * P], hidf[:, k * P:(k + 1) * P],
                                        hid_hi[:, k * P:(k + 1) * P].bitcast(f32), ALU.subtract).then_inc(hid_ready, 1)
            dve.wait_ge(ld["tab2"], 16)
            dve.wait_ge(zeroed, 3)
            for s, (kn, branch) in enumerate((("nk_s", "slc"), ("nk_w", "win"))):
                if s:
                    c, t = At(CH["cmp2"]), At(TL["cmp2"])
                    split_lo(c + 2)
                    complete(c)
                    for hh in range(2):
                        last = nc.vector.tensor_scalar(
                            cmp_k[:, :].rearrange("p (g h n) -> p g h n", g=4, h=2)[:, :, hh, :],
                            pj[t.par][:, 0:P].rearrange("p (g n) -> p g n", g=4), C("half", hh), None, ALU.mult)
                    last.then_inc(pj_free[t.par], 1)
                stage = ("nkv_s", "nkv_w")[s]
                for k in range(4):
                    c, t = At(CH[stage] + k), At(TL[stage] + k)
                    split_lo(c + 2)
                    if k < 2:
                        link(rope(ktmp[:, 0:S], qraw[:, :], tab64, SHUF64, t))
                        spread_keys(n_k[branch], k).then_inc(roped, 1)
            norm("q2")
            split_lo(At(CH["gates"] + 2))
            dve.wait_ge(gate_done, 1)
            early = gate[:, 0:16]
            link(nc.vector.tensor_scalar(early, early, C("rowvalid"), None, ALU.mult))
            with dve.Fori(0, 4) as i:
                for k in range(2):
                    split_lo(At(CH["nz"] + k + 2, i, 2))
            attention("nq")
            residual("nout", 1)
            norm("final2")

        @block.tensor
        def _(pe):
            pe.sem_inc(chunk_used, 2)
            pe.sem_inc(exp_done, 2)
            pe.sem_inc(p_turned, 2)
            pe.sem_inc(pT_ready, 2)
            pe.sem_inc(pv_done, 2)
            pe.wait_ge(setup, 1)
            pe.wait_ge(ld["cst"], 16)

            def product(acc, w0, cpar, x, first, last):
                col = cpar * CW + w0 * P
                passes = ((w_hi, 0), (w_hi, 1), (w_lo, 0))
                for k, (w, part) in enumerate(passes):
                    mm = nc.tensor.matmul(acc, w[:, col:col + P], x[part], start=first and k == 0, stop=last and k == 2)
                return mm

            def arrived(c):
                pe.wait_ge(lo_ready, c.v + 3)

            def free(t):
                pe.wait_ge(pj_free[t.par], t.half + 1)

            def project(c, t, hi, lo, n=S, norm=None, some=range(CB)):
                if 0 in some:
                    arrived(c)
                    free(t)
                for k in some:
                    if norm:
                        pe.wait_ge(h_ready, NBASE[NQ[norm]] + k + 1)
                    mm = product(pj[t.par][:, 0:n], k, c.par, (hi[:, k * n:(k + 1) * n], lo[:, k * n:(k + 1) * n]),
                                 k == 0, k == CB - 1)
                if CB - 1 in some:
                    mm.then_inc(chunk_used, 1)

            def norm(name):
                _, n, _, _, _, _ = NORM[name]
                q = NQ[name]
                k = NORMS[q][1]
                for m in range(k):
                    s = NBASE[q] + m
                    pe.wait_ge(sq_ready, s + 1)
                    for b in range(n // P):
                        mm = nc.tensor.matmul(SUMS[b][:, 0:1], sq[:, (s % 2) * S + b * P:(s % 2) * S + (b + 1) * P],
                                              ones[:, 0:1], start=m == 0, stop=m == k - 1)
                    mm.then_inc(sq_used, 1)
                pe.wait_ge(diag_ready, q + 1)
                for b in range(n // P):
                    mm = nc.tensor.matmul(px[:, b * P:(b + 1) * P], ones[:, :], diag[:, b * P:(b + 1) * P],
                                          start=True, stop=True)
                mm.then_inc(factor_ready, 1)

            def turn(t, number, src=None, width=P, blocks=NB):
                pe.wait_ge(pj_free[t.par], t.half + 2)
                src = vraw if src is None else src
                for b in range(blocks):
                    mm = nc.tensor.transpose(pt[number % 2][0:width, b * P:(b + 1) * P], src[:, b * width:(b + 1) * width],
                                             ident)
                mm.then_inc(v_turned, 1)

            def query(ph, i, j, normed=None, some=range(CB)):
                c, t = next_chunk(ph, i, j, 0), next_tile(ph, i, j, 0)
                project(c, t, h_hi, h_lo, norm=normed, some=some)

            def keys_values(ph, i, j):
                c, t = next_chunk(ph, i, j, 0), next_tile(ph, i, j, 0)
                if ph.name == "aq":
                    arrived(c + 1)
                    free(t + 1)
                    for k in range(2):
                        product(pj[(t + 1).par][:, :], k, (c + 1).par,
                                (c_hi[:, k * S:(k + 1) * S], c_lo[:, k * S:(k + 1) * S]), k == 0, k == 1)
                    free(t + 2)
                    acc = pj[(t + 2).par]
                    for b in range(NB):
                        for k in range(2):
                            col = (c + 1).par * CW + (2 + k) * P
                            here = slice(k * S + b * P, k * S + (b + 1) * P)
                            for n, (x, w) in enumerate(((c_hi, w_hi), (c_hi, w_lo), (c_lo, w_hi))):
                                mm = nc.tensor.matmul(acc[:, b * P:(b + 1) * P], x[:, here], w[:, col:col + P],
                                                      start=k == 0 and n == 0, stop=k == 1 and n == 2)
                    mm.then_inc(chunk_used, 1)

            def score_(ph, i, j, u):
                at = later(ph, i, j, u)
                if at is None:
                    return
                i, j, u = at
                hh, b, branch = ph.units[u]
                t, g, par = i * 2 + j, i + j // 2, j % 2
                k0, w = ph.keys(u)
                if u == 0:
                    if branch in ("mem", "topk"):
                        per = 3 if branch == "topk" else 1
                        q = At(TL[ph.name] + j * per + per - 1, i, 2 * per)
                        pe.wait_ge(pj_free[q.par], q.half + 2)
                    if branch != "mem":
                        pe.wait_ge(roped, RP[ph.name] + t + 2)
                q = qn if branch == "cmp" else qs
                if branch == "topk":
                    keys = a_k[:, par * S:par * S + w]
                elif branch == "mem":
                    k_at = (2 * t + hh) * MEM
                    keys = mem_k[0 if ph.name == "amem" else 1][:, k_at:k_at + MEM]
                elif branch == "band":
                    keys = b_k[:, sl(g * 2 * S + hh * S + k0, w)]
                elif branch == "cmp":
                    keys = cmp_k[:, sl(g * 2 * NCMP + hh * NCMP, NCMP)]
                else:
                    keys = n_k[branch][:, sl(g * 2 * S + hh * S, w)]
                pe.wait_ge(score_taken, ph.first_score + t * ph.n + u + 1)
                nc.tensor.matmul(ps[u % 2][:, 0:w], q[:, par * S + b * P:par * S + (b + 1) * P], keys,
                                 start=True, stop=True).then_inc(score_done, 1)

            def turn_p(ph, i, j, u):
                at = later(ph, i, j, u)
                if at is None:
                    return
                i, j, u = at
                a = unit_of(ph, i, j, u)
                par = u % 2
                w = ph.keys(u)[1]
                pe.wait_ge(exp_done, a + 3)
                pe.wait_ge(pT_ready, a + 1)
                wide = min(w, P)
                for k in range(w // wide):
                    mm = nc.tensor.transpose(pt[par][0:wide, k * P:(k + 1) * P],
                                             p_sb[:, par * S + k * wide:par * S + (k + 1) * wide], ident)
                mm.then_inc(p_turned, 1)

            def values(ph, i, j, u):
                hh, b, branch = ph.units[u]
                t, g = i * 2 + j, i + j // 2
                a = unit_of(ph, i, j, u)
                par = u % 2
                k0, w = ph.keys(u)
                p, v = ph.split(u)
                r = ph.region(u)
                acc = po[bank_of(ph, j, p)][:, r * ph.dv:(r + 1) * ph.dv]
                if v == 0:
                    if p == (ph.passes + 1) % 3 if ph.passes == 3 else True:
                        n = ph.first_tile + t + (1 if ph.passes == 3 else 0)
                        if not isinstance(n, int) or n > 0:
                            pe.wait_ge(out_ready, n)
                    else:
                        pe.wait_ge(o_scaled, pass_of(ph, i, j, p) - 1)
                pe.wait_ge(pT_ready, a + 3)
                if branch == "cmp":
                    settle(pe)
                    nc.tensor.matmul(acc, pT[0:NCMP, par * S:par * S + P], cmp_v[0:NCMP, sl(g * 64, 64)],
                                     start=True, stop=True).then_inc(pv_done, 1)
                    return
                kbs = w // P
                for k in range(kbs):
                    kb = k0 // P + k
                    if branch == "topk":
                        val = a_v[:, j % 2 * S + kb * P:j % 2 * S + (kb + 1) * P]
                    elif branch == "mem":
                        v_at = kb * 256 + (2 * t + hh) * 64
                        val = mem_v[0 if ph.name == "amem" else 1][:, v_at:v_at + 64]
                    elif branch == "band":
                        val = b_v[:, sl(g * 64 + kb * 256, 64)]
                    else:
                        val = n_v[branch][:, sl(g * 64 + kb * 256, 64)]
                    mm = nc.tensor.matmul(acc, pT[:, par * S + k * P:par * S + (k + 1) * P], val,
                                          start=k == 0, stop=k == kbs - 1)
                mm.then_inc(pv_done, 1)

            def turn_output(ph, i, j):
                pe.wait_ge(o_scaled, pass_of(ph, i, j, ph.passes - 1) + 1)
                out_bank = po[bank_of(ph, j, ph.passes - 1)]
                for b in range(NB):
                    mm = nc.tensor.transpose(out_bank[:, b * P:(b + 1) * P], o_sb[:, b * P:(b + 1) * P], ident)
                mm.then_inc(o_turned, 1)

            def tile(ph, i, j):
                for u in range(ph.n):
                    p, v = ph.split(u)
                    score_(ph, i, j, u + ph.ahead)
                    turn_p(ph, i, j, u + 1)
                    values(ph, i, j, u)
                    last = before(ph, i, j, p)
                    if last and p == 0 and v == ph.at_turn:
                        turn_output(ph, *last[:2])
                    if more(ph, i, j):
                        if ph.name == "aq":
                            if u == 0:
                                query(ph, i, j)
                            if u == 1:
                                keys_values(ph, i, j)
                        elif ph.name == "nq":
                            if u < 8:
                                query(ph, i, j, some=range(u, u + 1))
                        elif u < 3:
                            query(ph, i, j, some=(range(0, 3), range(3, 6), range(6, CB))[u])

            def attention(name, normed=None):
                ph = ATT[name]
                query(ph, 0, -1, normed)
                keys_values(ph, 0, -1)
                for u in range(ph.ahead):
                    score_(ph, 0, 0, u)
                turn_p(ph, 0, 0, 0)
                attention_tiles(pe, ph, tile)
                turn_output(ph, 0, ph.tiles - 1)

            def down(stage, per, kt, trips=DT // 2):
                def two(i):
                    for j in range(2):
                        t = At(TL[stage] + j, i, 2)
                        free(t)
                        for n in range(per):
                            c = At(CH[stage] + j * per + n, i, 2 * per)
                            arrived(c)
                            for k in range(n * CB, min(kt, (n + 1) * CB)):
                                here = slice(k * S, (k + 1) * S)
                                mm = product(pj[t.par][:, :], k % CB, c.par, (G_hi[:, here], G_lo[:, here]),
                                             k == 0, k == kt - 1)
                            mm.then_inc(chunk_used, 1)

                with pe.Fori(0, trips) as i:
                    two(i)

            def feed_forward(l):
                up, base = CH[f"up{l}"], TL[f"up{l}"]
                pe.wait_ge(h_ready, NBASE[NQ["affn" if l == 0 else "bffn"] + 1])
                with pe.Fori(0, FT) as i:
                    for k in range(2):
                        project(At(up + k, i, 2), At(base + k, i, 2), h_hi, h_lo)
                pe.wait_ge(g_ready, (l + 1) * FT + 1)
                down(f"down{l}", DOWN_CHUNKS, FT)

            norm("mem")
            number = TN["memv"]
            for k in range(8):
                c, t = At(CH["mem"] + k), At(TL["mem"] + k)
                project(c, t, memn_hi, memn_lo, n=MEM, norm="mem" if k == 0 else None)
                if k % 4 >= 2:
                    turn(t, number, blocks=MEM // P)
                    number += 1
            norm("amix")
            for k in range(4):
                c, t = At(CH["afront"] + k), At(TL["afront"] + k)
                project(c, t, h_hi, h_lo, norm="amix" if k == 0 else None)
                if k == 2:
                    turn(t, TN["widx"], qraw)
            norm("ckv")

            def idx_query(i, j):
                project(At(CH["idx"] + 1 + j, i, 2), At(TL["idx"] + 1 + j, i, 2), h_hi, h_lo)

            def idx_tile(i, j, more):
                t = i * 2 + j
                pe.wait_ge(roped, RP["idx"] + t + 2)
                for u, (hh, b) in enumerate(IDX_UNITS):
                    w = (b + 1) * P
                    pe.wait_ge(score_taken, t * len(IDX_UNITS) + u + 1)
                    nc.tensor.matmul(ps[u % 2][:, 0:w], qs[:, j * S + b * P:j * S + (b + 1) * P],
                                     kidx[:, hh * S:hh * S + w], start=True, stop=True).then_inc(score_done, 1)
                    if u == 1 and more:
                        idx_query(i, j)

            idx_query(0, -1)
            with pe.Fori(0, 3) as i:
                idx_tile(i, 0, True)
                idx_tile(i, 1, True)
            idx_tile(3, 0, True)
            idx_tile(3, 1, False)
            pe.wait_ge(h_ready, NBASE[NQ["ckv"] + 1])
            attention("aq")
            attention("amem")
            pe.wait_ge(out_ready, ATT["amem"].first_tile + 2 + 1)
            down("aout", 2, 10)
            norm("affn")
            feed_forward(0)

            norm("bmix")
            for k in range(4):
                c, t = At(CH["bfront"] + k), At(TL["bfront"] + k)
                project(c, t, h_hi, h_lo, norm="bmix" if k == 0 else None)
                if k >= 2:
                    turn(t, TN["bv"] + k - 2)
            attention("bq")
            attention("bmem")
            pe.wait_ge(out_ready, ATT["bmem"].first_tile + 2 + 1)
            down("bout", 2, 10)
            norm("bffn")
            feed_forward(1)
            norm("final1")

            norm("conv")
            pe.wait_ge(h_ready, NBASE[NQ["conv"] + 1])
            with pe.Fori(0, CT) as i:
                for k in range(4):
                    project(At(CH["conv"] + k, i, 4), At(TL["conv"] + k, i, 4), h_hi, h_lo)
            pe.wait_ge(g_ready, 2 * FT + CT + 1)
            down("cout", 2, CT)
            norm("kv2")
            for k in range(4):
                project(At(CH["cmp_kv"] + k), At(TL["cmp_kv"] + k), h_hi, h_lo, norm="kv2" if k == 0 else None)
            for k in range(4):
                which = k // 2
                t = At(TL["cmp"] + k)
                free(t)
                for n in range(2):
                    c = At(CH["cmp"] + 2 * k + n)
                    arrived(c)
                    pe.wait_ge(win_ready, 2 * which + n + 1)
                    for w0 in range(CB):
                        l = n * CB + w0
                        here = slice(l * P, (l + 1) * P)
                        mm = product(pj[t.par][:, 0:P], w0, c.par, (win_hi[which][:, here], win_lo[which][:, here]),
                                     l == 0, l == 15)
                    mm.then_inc(chunk_used, 1)

            def kv_tiles(stage, vn):
                for k in range(4):
                    c, t = At(CH[stage] + k), At(TL[stage] + k)
                    project(c, t, h_hi, h_lo)
                    if k == 3:
                        turn(At(TL[stage] + 2), TN[vn])
                turn(At(TL[stage] + 3), TN[vn] + 1)

            kv_tiles("nkv_s", "nv_s")
            c = At(CH["cmp2"])
            arrived(c)
            for which in range(2):
                t = At(TL["cmp2"] + which)
                free(t)
                pe.wait_ge(hid_ready, 2 * which + 2)
                for m in range(2):
                    here = slice((2 * which + m) * P, (2 * which + m + 1) * P)
                    mm = product(pj[t.par][:, 0:P], 2 * which + m, c.par, (hid_hi[:, here], hid_lo[:, here]), m == 0, m == 1)
            mm.then_inc(chunk_used, 1)
            turn(At(TL["cmp2"] + 1), TN["cmpv"], width=NCMP)
            kv_tiles("nkv_w", "nv_w")
            norm("q2")
            project(At(CH["gates"]), At(TL["gates"]), h_hi, h_lo, norm="q2")
            turn(At(TL["gates"]), TN["gates"])
            with pe.Fori(0, 4) as i:
                for k in range(2):
                    project(At(CH["nz"] + k, i, 2), At(TL["nz"] + k, i, 2), h_hi, h_lo)
            attention("nq")
            pe.wait_ge(out_ready, ATT["nq"].first_tile + 8 + 1)
            down("nout", 1, DT)
            norm("final2")


def kernel(**inputs):
    import numpy as np
    import concourse.bacc as bacc
    from concourse.bass_utils import run_bass_kernel_spmd as run

    a = {k: np.asarray(v) for k, v in inputs.items()}
    f = np.float32

    def cols(w, k, c0, n=P):
        b = np.zeros((P, P), f)
        b[:, 0:n] = w[k * P:(k + 1) * P, c0:c0 + n]
        return b

    def picked(w, k, index):
        return w[k * P:(k + 1) * P][:, index]

    zero = np.zeros((P, P), f)
    chunks = []

    def chunk(blocks):
        chunks.append(np.stack(list(blocks) + [zero] * (CB - len(blocks)), axis=1))

    def plain(w, c0, count, kt=CB):
        for m in range(count):
            blocks = [cols(w, k, c0 + m * P) for k in range(kt)]
            for n in range(0, kt, CB):
                chunk(blocks[n:n + CB])

    wa, wb, wn, wkv = a["a_w_in"][0], a["b_w_in"][0], a["b_w_in_2"][0], a["w_kv_2"]
    uk = a["a_w_uk"][0]
    uv = a["a_w_uv"][0].reshape(256, 1024)
    for l in range(2):
        plain(a["w_mem_kv"][l], 0, 4)
    plain(wa, 1024, 2)
    chunk([np.concatenate([wa[k * P:(k + 1) * P, 2400:2416], np.zeros((P, 80), f), wa[k * P:(k + 1) * P, 1280:1312]], 1)
           for k in range(DT)])
    chunk([np.concatenate([wa[k * P:(k + 1) * P, 2336:2400]] * 2, 1) for k in range(DT)])
    plain(wa, 1312, 8)
    for h in range(8):
        order = h * P + np.concatenate([np.arange(32, P), np.arange(32)])
        chunk([picked(wa, k, order) for k in range(DT)])
        blocks = []
        for k in range(2):
            b = np.zeros((P, P), f)
            b[:, 0:96] = uk[k * P:(k + 1) * P, h, :]
            blocks.append(b)
        chunk(blocks + [cols(uv, k, h * P) for k in range(2)])
    plain(wa, 2416, 2)
    plain(a["a_w_out"][0], 0, DT, 10)

    def feed_forward(l):
        for m in range(FT):
            plain(a["f_w_up"][l], m * P, 1)
            plain(a["f_w_up"][l], FT * P + m * P, 1)
        plain(a["f_w_down"][l], 0, DT, FT)

    feed_forward(0)
    plain(wb, 1024, 4)
    plain(wb, 0, 8)
    plain(wb, 1536, 2)
    plain(a["b_w_out"][0], 0, DT, 10)
    feed_forward(1)
    for m in range(CT):
        for part in (1, 2, 3, 0):
            plain(a["a_w_in_2"][0], part * CT * P + m * P, 1)
    plain(a["a_w_out_2"][0], 0, DT, CT)
    plain(wkv, 0, 4)
    for which in ("k", "v"):
        plain(a[f"cmp_w1_{which}_2"], 0, 2, 16)
    plain(wkv, 2 * 256, 4)
    w2k, w2v = a["cmp_w2_k_2"], a["cmp_w2_v_2"]
    chunk([np.concatenate([w2k[k * P:(k + 1) * P]] * 2, 1) for k in range(2)] + [cols(w2v, k, 0, 64) for k in range(2)])
    plain(wkv, 4 * 256, 4)
    branchwise = 1024 + np.arange(48).reshape(16, 3).T.reshape(-1)
    chunk([np.concatenate([picked(wn, k, branchwise), np.zeros((P, P - 48), f)], 1) for k in range(DT)])
    plain(wn, 1072, 8)
    plain(wn, 0, 8)
    plain(a["b_w_out_2"][0], 0, DT)
    assert len(chunks) == NCHUNKS, (len(chunks), NCHUNKS)
    stream = np.stack(chunks).reshape(NCHUNKS, P, CW)

    def tiles(v):
        return np.ascontiguousarray(v.reshape(-1, P).T)

    def positions(e):
        return np.concatenate([tiles(e.reshape(-1)), np.zeros((P, 2), f)], 1)

    vec = np.concatenate([
        tiles(a["g_mix"].reshape(-1)), tiles(a["g_ffn"].reshape(-1)), tiles(a["g_mem"]), tiles(a["g_final"]),
        tiles(a["a_norm_2"][0]), tiles(a["kv_norm_2"]), tiles(a["b_norm_2"][0]), tiles(a["final_norm_2"]),
        tiles(a["a_kv_norm"][0]), tiles(a["f_conv_w"].reshape(-1)), tiles(a["f_conv_b"].reshape(-1)),
        tiles(a["a_conv_w_2"][0].reshape(-1)), np.broadcast_to(a["b_sinks"][0], (P, 16)),
        positions(a["cmp_pos_k_2"]), positions(a["cmp_pos_v_2"])], 1)
    assert vec.shape[1] == NVEC

    q, k = np.arange(P)[:, None], np.arange(P)[None, :]
    hide_later = np.where(k > q, NEG, 0.0)
    hide_far = np.where(k <= q, NEG, 0.0)
    n = np.arange(NCMP)[None, :]
    cmp = [np.where((n < NCMP - 1) & (16 * n + 31 <= b * P + q), 0.0, NEG) for b in range(NB)]

    def rotation(dim, at):
        rot = dim // 4
        freq = (np.float64(500000.0) ** (-np.arange(0, rot, 2) / rot)).astype(f)
        inv, sgn = np.zeros(P, f), np.zeros(P, f)
        for h in range(0, P, dim):
            inv[h + at:h + at + rot] = np.concatenate([freq, freq])
            sgn[h + at:h + at + rot] = np.concatenate([-np.ones(rot // 2), np.ones(rot // 2)])
        return inv[:, None], sgn[:, None]

    inv128, sgn128 = rotation(128, 96)
    inv64, sgn64 = rotation(64, 0)
    cst = np.concatenate([np.eye(P), np.zeros((P, S - P)), hide_later, hide_far, hide_later, *cmp,
                          (q < 64), (q >= 64), inv128, sgn128, inv64, sgn64, (q >= 31)], 1).astype(f)
    assert cst.shape[1] == NCONST
    angle = (inv64 * np.arange(S, dtype=f)[None, :]).astype(np.float64)
    tab2 = np.concatenate([np.cos(angle), np.sin(angle) * sgn64], 1).astype(f)

    def feature_major(x, n):
        return np.ascontiguousarray(x.T.reshape(DT, P, n).transpose(1, 0, 2).reshape(P, DT * n))

    arrays = {
        "wstream": stream, "x": feature_major(a["x"][0], S), "mem": feature_major(a["mem"][0], MEM),
        "pos": np.ascontiguousarray(np.broadcast_to(a["positions"], (P, S))).astype(np.int32),
        "vec": np.ascontiguousarray(vec), "cst": cst, "tab2": tab2}
    nc = bacc.Bacc("TRN2", target_bir_lowering=False, num_devices=1)
    args = [nc.dram_tensor(f"in_{n}", v.shape, mybir.dt.from_np(v.dtype), kind="ExternalInput").ap()
            for n, v in arrays.items()]
    args.append(nc.dram_tensor("out_x", (P, DT * S), mybir.dt.float32, kind="ExternalOutput").ap())
    build(nc, *args)
    got = run(nc, [{f"in_{n}": v for n, v in arrays.items()}], core_ids=[0]).results[0]["out_x"]
    return np.ascontiguousarray(got.reshape(P, DT, S).transpose(1, 0, 2).reshape(D, S).T)[None]
```

```python
import concourse.bass as bass
from concourse import mybir
from contextlib import ExitStack

P = 128
S = 512
D = 1024
DT = D // P
NB = S // P
CB = 8
CW = CB * P
MEM = 256
FT = 2816 // P
CT = 2048 // P
DOWN_CHUNKS = -(-FT // CB)
OT = 10
OUT_CHUNKS = DT * OT // CB
EPS = 1e-6
NEG = -1e30
TAKEN = -3e38
TOPK = 128
NCMP = 32
FPAD = 544
TWO_PI = 6.283185307179586
PI_HI = 6.28125
PI_LO = TWO_PI - PI_HI
ROUNDER = 12582912.0

STAGES = [("afront", 2), ("idx", 8), ("ckv", 2), ("mem", 8), ("aq", 18), ("aout", OUT_CHUNKS), ("up0", 2 * FT),
          ("down0", DT * DOWN_CHUNKS), ("bfront", 4), ("bq", 8), ("bmem", 2), ("bout", OUT_CHUNKS), ("up1", 2 * FT),
          ("down1", DT * DOWN_CHUNKS), ("conv", 4 * CT), ("cout", 2 * DT), ("cmp_kv", 4), ("cmp", 8), ("nkv_s", 4), ("cmp2", 1),
          ("nkv_w", 4), ("gates", 1), ("nz", 8), ("nq", 8), ("nout", DT)]
CH, NCHUNKS = {}, 0
for _name, _count in STAGES:
    CH[_name] = NCHUNKS
    NCHUNKS += _count

TILES = [("afront", 2), ("idx", 8), ("ckv", 2), ("mem", 8), ("aq", 26), ("aout", 8), ("up0", 2 * FT), ("down0", 8),
         ("bfront", 4), ("bq", 8), ("bmem", 2), ("bout", 8), ("up1", 2 * FT), ("down1", 8), ("conv", 4 * CT),
         ("cout", 8), ("cmp_kv", 4), ("cmp", 2), ("nkv_s", 4), ("cmp2", 2),
         ("nkv_w", 4), ("gates", 1), ("nz", 8), ("nq", 8), ("nout", 8)]
TL, _t = {}, 0
for _name, _count in TILES:
    TL[_name] = _t
    _t += _count

ROPES = [("kidx", 1), ("krope", 1), ("idx", 8), ("aq", 8), ("bk", 2), ("bq", 8), ("nk_s", 2), ("nk_w", 2),
         ("nq", 8)]
RP, _t = {}, 0
for _name, _count in ROPES:
    RP[_name] = _t
    _t += _count

NORMS = [("amix", 8), ("mem", 8), ("ckv", 2), ("affn", 8), ("bmix", 8), ("bffn", 8), ("conv", 8), ("final1", 8),
         ("kv2", 8), ("q2", 8), ("final2", 8)]
NQ = {name: q for q, (name, _) in enumerate(NORMS)}
PLAIN = ("final1", "final2")
BEHIND = {"amix": None, "affn": "aout", "bmix": "down0", "bffn": "bout", "final1": "down1", "kv2": "cout",
          "final2": "nout"}
STATS = [name for name, _ in NORMS if name != "q2"]
SUMMED = [name for name in STATS if name != "conv"]
QUEUE = [name for name in SUMMED if name not in BEHIND]
SQBASE = {name: sum(dict(NORMS)[n] for n in SUMMED[:k]) for k, name in enumerate(SUMMED)}
USED = {name: sum(dict(NORMS)[n] for n in QUEUE[:k]) for k, name in enumerate(QUEUE)}
SBASE = [sum(k for n, k in NORMS[:q] if n not in PLAIN) for q in range(len(NORMS) + 1)]
RESIDUALS = {name: DT * k for k, name in enumerate(("aout", "down0", "bout", "down1", "cout", "nout"))}
NBASE = [sum(k for _, k in NORMS[:q]) for q in range(len(NORMS) + 1)]

TURNS = [("widx", 1), ("memv", 4), ("bv", 2), ("nv_s", 2), ("cmpv", 1), ("nv_w", 2), ("gates", 1)]
TN, _t = {}, 0
for _name, _count in TURNS:
    TN[_name] = _t
    _t += _count


POOL_CHUNKS = {"mem": (CH["mem"], CH["aq"] + 2), "aq": (CH["aq"] + 2, CH["aout"] + 2), "bq": (CH["bq"] + 2, CH["bout"] + 2),
               "nq": (CH["nq"] + 2, CH["nout"] + 2)}


class Attention:

    def __init__(self, name, tiles, units, branches, chunks, dv, scale, first_score, first_unit, first_tile, first_pass,
                 out0):
        self.name, self.tiles, self.chunks, self.dv, self.scale = name, tiles, chunks, dv, scale
        self.units = [(hh, b, branch) for branch in branches for hh, b in units]
        self.first_score, self.first_unit, self.first_tile, self.out0 = first_score, first_unit, first_tile, out0
        self.first_pass, self.passes, self.m, self.n = first_pass, len(branches), len(units), len(self.units)
        self.ahead = 3 if self.m == 8 else 2
        self.at_scale, self.at_turn, self.at_gate, self.at_hi, self.at_lo = (1, 2, 3, 4, 5) if self.m == 8 else (
            0, 1, 1, 2, 3)
        self.beside = (0, 1, 3, 5, 7, 8, 12, 16)
        self.at_query = {"aq": 3, "bq": 7, "nq": 17}.get(name)
        self.at_rope = {"aq": 0, "bq": 2, "nq": 10}.get(name)
        self.at_refill = {"aq": 2, "bq": 2, "nq": 19}.get(name, 6)

    def split(self, u):
        return u // self.m, u % self.m

    def region(self, u):
        hh, b, _ = self.units[u]
        return b * (P // self.dv) + hh

    def keys(self, j):
        _, b, branch = self.units[j]
        if branch == "mem":
            return 0, MEM
        if branch == "band":
            return (0, P) if b == 0 else ((b - 1) * P, 2 * P)
        if branch == "cmp":
            return 0, NCMP
        return 0, (b + 1) * P


IDX_UNITS = [(hh, b) for hh in range(2) for b in range(1, NB)]
IDX_SCORES = 8 * len(IDX_UNITS)


def _attentions():
    made, score, unit, tile, done = {}, IDX_SCORES, 0, 0, 0
    pair = [(hh, b) for hh in range(2) for b in range(NB)]
    for name, tiles, units, branches, chunks, dv, dim, out0 in (
            ("aq", 8, [(0, b) for b in range(NB)], ["topk"], 2, 128, 128, 0),
            ("amem", 2, pair, ["mem"], 1, 64, 64, 8), ("bq", 8, pair, ["band"], 1, 64, 64, 0),
            ("bmem", 2, pair, ["mem"], 1, 64, 64, 8), ("nq", 8, pair, ["cmp", "slc", "win"], 1, 64, 64, 0)):
        made[name] = Attention(name, tiles, units, branches, chunks, dv, float(dim) ** -0.5, score, unit, tile, done,
                               out0)
        n = tiles * len(units) * len(branches)
        score, unit, tile, done = score + n, unit + n, tile + tiles, done + tiles * len(branches)
    return made


ATT = _attentions()

VECS = [("g_mix", 16), ("g_ffn", 16), ("g_mem", 8), ("g_final", 8), ("a_norm", 8), ("kv_norm", 8), ("b_norm", 8),
        ("final_norm", 8), ("a_kv_norm", 2), ("f_conv_w", 2 * 3 * FT), ("f_conv_b", 2 * FT), ("a_conv_w", 3 * CT),
        ("sinks", 16), ("pos_k", 18), ("pos_v", 18)]
VC, NVEC = {}, 0
for _name, _count in VECS:
    VC[_name] = NVEC
    NVEC += _count
CONSTS = [("ident", P), ("causal", S), ("band", 2 * P), ("cmp", NB * NCMP), ("half", 2), ("inv128", 1), ("sgn128", 1),
          ("inv64", 1), ("sgn64", 1), ("rowvalid", 1)]
CC, NCONST = {}, 0
for _name, _count in CONSTS:
    CC[_name] = NCONST
    NCONST += _count

SHUF128 = [(i + 16) % 32 for i in range(32)]
SHUF64 = [(i + 8) % 16 if i < 16 else i for i in range(32)]


class At:

    def __init__(self, base, i=0, per=0):
        assert per % 2 == 0
        self.v = base + i * per if per else base
        self.par = base % 2
        self.half = base // 2 + i * (per // 2) if per else base // 2
        self.args = (base, i, per)

    def __add__(self, k):
        return At(self.args[0] + k, *self.args[1:])


class Links:

    def __init__(self, eng, sem):
        self.eng, self.sem, self.n, self.shift = eng, sem, 0, 0

    def mark(self, instruction):
        self.n += 1
        instruction.then_inc(self.sem, 1)

    def catch(self):
        self.eng.wait_ge(self.sem, self.shift + self.n)

    def __call__(self, instruction):
        self.mark(instruction)
        self.catch()

    def begin(self, i, per):
        self.shift, self.at = i * per, self.n

    def end(self, per, trips):
        assert self.n - self.at == per, (self.n - self.at, per)
        self.n, self.shift = self.at + per * trips, 0



def build(nc, wstream, xin, memin, posin, vecin, cstin, tab2in, out):
    f32, f32r, i32 = mybir.dt.float32, mybir.dt.float32r, mybir.dt.int32
    ALU, ACT = mybir.AluOpType, mybir.ActivationFunctionType
    ds = bass.ds
    place = [-(-nc.sbuf_base // 32) * 32]

    def put(name, cols, dt=f32, at=None):
        if at is None:
            at, place[0] = place[0], place[0] + -(-4 * cols // 32) * 32
            assert place[0] <= nc.sbuf_top, (name, place[0] - nc.sbuf_top)
        return nc.alloc_sbuf_tensor_at(name, [P, cols], dt, offset=at)

    xT = put("xT", DT * S)
    h_hi, h_lo = put("h_hi", DT * S, f32r), put("h_lo", DT * S, f32r)
    raw = put("raw", 2 * CW)
    w_hi, w_lo = put("w_hi", 2 * CW, f32r), put("w_lo", 2 * CW, f32r)
    vec, cst, ones = put("vec", NVEC), put("cst", NCONST), put("ones", P)
    tab64 = put("tab64", 2 * S)
    v4, r4, mhalf = put("v4", 8), put("r4", 8), put("mhalf", 8)
    stats = put("stats", 8)
    lsum, esink, coef = put("lsum", 16), put("esink", 16), put("coef", 16)
    m8 = put("m8", 24)
    widx = put("widx", NB * 16)
    KB = 1024
    mem1 = place[0]
    place[0] += 6 * KB
    mem_k1, mem_v1 = put("mem_k1", 4 * MEM, at=mem1), put("mem_v1", 2 * MEM, at=mem1 + 4 * KB)

    sc0 = place[0]
    place[0] += 30 * KB
    s_sb, p_sb, pT = put("s_sb", 2 * S, at=sc0), put("p_sb", 2 * S, at=sc0 + 4 * KB), put("pT", 2 * S, at=sc0 + 8 * KB)
    o_sb, qraw, rtmp = put("o_sb", S, at=sc0 + 12 * KB), put("qraw", S, at=sc0 + 14 * KB), put("rtmp", S, at=sc0 + 16 * KB)
    qs, qn = put("qs", 2 * S, at=sc0 + 18 * KB), put("qn", 2 * S, at=sc0 + 22 * KB)
    vraw, ysb = put("vraw", S, at=sc0 + 26 * KB), put("ysb", S, at=sc0 + 28 * KB)
    om = put("om", S, at=sc0 + 26 * KB)
    ktmp = put("ktmp", 2 * S, at=sc0 + 4 * KB)
    nsink = put("nsink", 16)
    fa, fb, fc = put("fa", S, at=sc0), put("fb", S, at=sc0 + 2 * KB), put("fc", S, at=sc0 + 4 * KB)
    ssum = put("ssum", S, at=sc0 + 22 * KB)
    gsq, gsum = put("gsq", 2 * S, at=sc0), put("gsum", S, at=sc0 + 4 * KB)
    gg, vg, r1, r12 = put("gg", 8), put("vg", 8), put("r1", 8), put("r12", 8)
    fd, fe, fg = put("fd", S, at=sc0 + 6 * KB), put("fe", S, at=sc0 + 8 * KB), put("fg", S, at=sc0 + 10 * KB)
    sq, hf = put("sq", 2 * S, at=sc0 + 12 * KB), put("hf", 4 * S, at=sc0 + 16 * KB)

    g0 = place[0]
    half = FT * S * 4
    place[0] += 2 * half
    assert place[0] <= nc.sbuf_top, place[0] - nc.sbuf_top
    g1 = g0 + half
    G_hi, G_lo = put("G_hi", FT * S, f32r, at=g0), put("G_lo", FT * S, f32r, at=g1)
    memn_hi, memn_lo = put("memn_hi", DT * MEM, f32r, at=g0), put("memn_lo", DT * MEM, f32r, at=g0 + 8 * KB)
    memT = put("memT", DT * MEM, at=g1)
    a_k, a_v = put("a_k", 2 * S, at=g0 + 20 * KB), put("a_v", 2 * S, at=g0 + 24 * KB)
    c_hi, c_lo = put("c_hi", 2 * S, f32r, at=g0 + 28 * KB), put("c_lo", 2 * S, f32r, at=g0 + 32 * KB)
    kidx, tab128 = put("kidx", 2 * S, at=g0 + 36 * KB), put("tab128", 2 * S, at=g0 + 40 * KB)
    bias_a, score = put("bias_a", 3 * S, at=g1 + 20 * KB), put("score", 3 * S, at=g1 + 26 * KB)
    mem_k0, mem_v0 = put("mem_k0", 4 * MEM, at=g1 + 32 * KB), put("mem_v0", 2 * MEM, at=g1 + 36 * KB)
    ckv = put("ckv", 2 * S, at=g1 + 38 * KB)
    posi, posf = put("posi", S, i32, at=g1 + 8 * KB), put("posf", S, at=g1 + 10 * KB)
    ang, turns = put("ang", S, at=g1 + 12 * KB), put("turns", S, at=g1 + 14 * KB)
    b_k, b_v = put("b_k", 8 * S, at=g0 + 20 * KB), put("b_v", NB * 256, at=g0 + 36 * KB)
    fold = [put("fold_k", 4 * FPAD, at=g0), put("fold_v", 4 * FPAD, at=g0 + 16 * FPAD)]
    win = put("win", 2 * CW, at=sc0 + 16 * KB)
    win_hi = [put("win_k_hi", 2 * CW, f32r, at=g1), put("win_v_hi", 2 * CW, f32r, at=sc0)]
    win_lo = [put("win_k_lo", 2 * CW, f32r, at=g1 + 8 * KB), put("win_v_lo", 2 * CW, f32r, at=sc0 + 8 * KB)]
    n_k = {"slc": put("n_ks", 8 * S, at=g0 + 18 * KB), "win": put("n_kw", 8 * S, at=g1 + 18 * KB)}
    n_v = {"slc": put("n_vs", NB * 256, at=g0 + 34 * KB), "win": put("n_vw", NB * 256, at=g0 + 38 * KB)}
    cmp_k, cmp_v = put("cmp_k", 2 * 4 * NCMP, at=g0 + 42 * KB), put("cmp_v", 4 * 64, at=g0 + 43 * KB)
    gate = put("gate", NB * 48, at=g1 + 34 * KB)
    hidx, hidt = put("hidx", 2 * P, at=g1 + 36 * KB), put("hidt", 2 * P, at=g1 + 37 * KB)
    hidf = [put("hidf_k", 2 * P, at=g1 + 38 * KB), put("hidf_v", 2 * P, at=g1 + 43 * KB)]
    hid_hi, hid_lo = put("hid_hi", 4 * P, f32r, at=g1 + 39 * KB), put("hid_lo", 4 * P, f32r, at=g1 + 41 * KB)
    zsil = put("zsil", 8 * S, at=g1)
    mem_k, mem_v = [mem_k0, mem_k1], [mem_v0, mem_v1]

    ident = cst[:, CC["ident"]:CC["ident"] + P]

    def V(name, k=0):
        return vec[:, VC[name] + k:VC[name] + k + 1]

    def VD(name, k):
        return vec[:, ds(k + VC[name], 1)]

    def C(name, k=0, n=1):
        return cst[:, CC[name] + k:CC[name] + k + n]

    def causal(b):
        return C("causal", (NB - 1 - b) * P, (b + 1) * P)

    def ST(k, par):
        return stats[:, 2 * k + par:2 * k + par + 1]

    MX, NEGM = range(2)

    def of_pass(tile, g, r, n=1):
        return tile[:, (g % 2) * 8 + r:(g % 2) * 8 + r + n]

    with ExitStack() as ctx:
        def sem(name):
            return ctx.enter_context(nc.semaphore(name))

        def bank(name):
            return ctx.enter_context(nc.psum_tensor(name, [P, 512], f32))

        pj = [bank("pj0"), bank("pj1")]
        ps = [bank("ps0"), bank("ps1")]
        pt = [bank("pt0"), bank("pt1")]
        po = [bank("po0"), bank("po1")]
        px = po[1]

        ld = {n: sem(f"loaded_{n}") for n in ("mem", "vec", "cst", "pos", "tab2")}
        x_loaded = [sem(f"x_loaded{k}") for k in range(DT // 2)]
        chunk_loaded = [sem("chunk_loaded0"), sem("chunk_loaded1")]
        hi_ready = sem("hi_ready")
        lo_ready = sem("lo_ready")
        chunk_used = sem("chunk_used")
        pj_free = [sem("pj_free0"), sem("pj_free1")]
        setup = sem("setup")
        x_ready = sem("x_ready")
        sq_ready, sq_used = sem("sq_ready"), sem("sq_used")
        var_ready, rs_ready = sem("var_ready"), sem("rs_ready")
        factor_ready = sem("factor_ready")
        gsq_ready, gsum_ready, g_used = sem("gsq_ready"), sem("gsum_ready"), sem("g_used")
        r12_ready = sem("r12_ready")
        rest_summed, rest_used = sem("rest_summed"), sem("rest_used")
        hf_ready, hhi_ready = sem("hf_ready"), sem("hhi_ready")
        h_ready = [sem("h_ready0"), sem("h_ready1")]
        score_done, score_taken = sem("score_done"), sem("score_taken")
        idx_added = sem("idx_added")
        max_ready, exp_done = sem("max_ready"), sem("exp_done")
        p_turned, pT_ready, pv_done = sem("p_turned"), sem("pT_ready"), sem("pv_done")
        om_ready = sem("om_ready")
        o_scaled, o_turned = sem("o_scaled"), sem("o_turned")
        out_hi, out_ready = sem("out_hi"), sem("out_ready")
        y_ready = sem("y_ready")
        roped = sem("roped")
        v_turned = sem("v_turned")
        act_ready, g_hi_ready, g_ready = sem("act_ready"), sem("g_hi_ready"), sem("g_ready")
        win_summed, win_hi_ready, win_ready = sem("win_summed"), sem("win_hi_ready"), sem("win_ready")
        hid_x, hid_th, hid_f, hid_turned, hid_hi_ready, hid_ready = (
            sem(n) for n in ("hid_x", "hid_th", "hid_f", "hid_turned", "hid_hi_ready", "hid_ready"))
        gate_done = sem("gate_done")
        zeroed = sem("zeroed")
        dve_step = sem("dve_step")
        angle_ready, sin_ready = sem("angle_ready"), sem("sin_ready")
        settled = sem("settled")
        stored = sem("stored")

        block = ctx.enter_context(nc.Block())

        def normed(name, m):
            return h_ready[m % 2], (NBASE[NQ[name]] + m) // 2 + 1

        def all_normed(eng, name):
            for m in (-2, -1):
                eng.wait_ge(*normed(name, dict(NORMS)[name] + m))

        @block.sync
        def _(sp):
            sp.dma_start(posi[:, :], posin).then_inc(ld["pos"], 16)
            sp.dma_start(cst[:, :], cstin).then_inc(ld["cst"], 16)
            for m in range(0, DT, 2):
                here = slice(m * S, (m + 2) * S)
                sp.dma_start(xT[:, here], xin[:, here]).then_inc(x_loaded[m // 2], 16)
            sp.dma_start(vec[:, :], vecin).then_inc(ld["vec"], 16)
            sp.dma_start(memT[:, :], memin).then_inc(ld["mem"], 16)
            with sp.Fori(0, NCHUNKS // 2) as i:
                for par in range(2):
                    c = At(par, i, 2)
                    sp.wait_ge(lo_ready, c.v + 1)
                    sp.dma_start(raw[:, par * CW:(par + 1) * CW],
                                 wstream[ds(c.v, 1), :, :].rearrange("a p c -> p (a c)")).then_inc(chunk_loaded[par], 16)
            for m in range(0, DT, 2):
                sp.wait_ge(*normed("final2", m + 1))
                here = slice(m * S, (m + 2) * S)
                sp.dma_start(out[:, here], xT[:, here]).then_inc(stored, 16)
            sp.wait_ge(stored, 16 * DT // 2)

        NORM = {
            "mem": (memT, MEM, "g_mem", 0, memn_hi, memn_lo), "amix": (xT, S, "g_mix", 0, h_hi, h_lo),
            "ckv": (ckv, S, "a_kv_norm", 0, c_hi, c_lo), "affn": (xT, S, "g_ffn", 0, h_hi, h_lo),
            "bmix": (xT, S, "g_mix", DT, h_hi, h_lo), "bffn": (xT, S, "g_ffn", DT, h_hi, h_lo),
            "final1": (xT, S, "g_final", 0, None, None), "conv": (xT, S, "a_norm", 0, h_hi, h_lo),
            "kv2": (xT, S, "kv_norm", 0, h_hi, h_lo), "q2": (xT, S, "b_norm", 0, h_hi, h_lo),
            "final2": (xT, S, "final_norm", 0, None, None)}

        HIDDEN = [po[0], ps[0]]

        def sum_banks(name):
            return (*ps, *po) if name == "ckv" else (*ps, *pt)

        def settle(eng):
            eng.sem_inc(settled, 1)

        def chunks_of(j):
            def last(m):
                return (OT * (m + 1) - 1) // CB
            return range(last(j - 1) + 1 if j else 0, last(j) + 1)

        def sl(start, n):
            return slice(start, start + n) if isinstance(start, int) else ds(start, n)

        def attention_tiles(eng, ph, tile, links=None, per=0):
            tile(ph, 0, 0)
            tail = 3 if ph.name == "nq" else 1
            trips = (ph.tiles - 1 - tail) // 2
            if trips:
                with eng.Fori(0, trips) as i:
                    if links:
                        links.begin(i, per)
                    tile(ph, i, 1)
                    tile(ph, i, 2)
                if links:
                    links.end(per, trips)
            for j in range(ph.tiles - tail, ph.tiles):
                tile(ph, 0, j)

        def later(ph, i, j, u):
            if u < ph.n:
                return i, j, u
            if isinstance(i, int) and j == ph.tiles - 1:
                return None
            return i, j + 1, u - ph.n

        def before(ph, i, j, p):
            if p:
                return i, j, p - 1
            if isinstance(i, int) and j == 0:
                return None
            return i, j - 1, ph.passes - 1

        def unit_of(ph, i, j, u):
            return ph.first_unit + (i * 2 + j) * ph.n + u

        def pass_of(ph, i, j, p):
            return ph.first_pass + (i * 2 + j) * ph.passes + p

        def bank_of(ph, j, p):
            return (j * ph.passes + p) % 2

        def more(ph, i, j):
            return not (isinstance(i, int) and j == ph.tiles - 1)

        def ahead(ph, i, j):
            return ph.name in ("aq", "bq") or ph.name == "nq" and not (isinstance(i, int) and j >= ph.tiles - 2)

        def query_at(ph, i, j):
            if ph.name == "amem":
                return query_at(ATT["aq"], i, j + ATT["aq"].tiles)
            if ph.name != "aq":
                return At(CH[ph.name] + j, i, 2), At(TL[ph.name] + j, i, 2)
            if isinstance(i, int) and j < 2:
                return At(CH["aq"] + j), At(TL["aq"] + j)
            if isinstance(i, int) and j == ph.tiles + 1:
                return At(CH["aq"] + 17), At(TL["aq"] + 25)
            return At(CH["aq"] + 2 * j, i, 4), At(TL["aq"] + 3 * j, i, 6)

        def keys_values_at(i, j):
            if isinstance(i, int) and j == 0:
                return At(CH["aq"] + 2), At(TL["aq"] + 2)
            return At(CH["aq"] + 1 + 2 * j, i, 4), At(TL["aq"] + 1 + 3 * j, i, 6)

        @block.gpsimd
        def _(pool):
            nc.gpsimd.memset(ones[:, :], 1.0)
            nc.gpsimd.memset(mhalf[:, :], -0.5)
            nc.gpsimd.memset(score[:, :], 0.0)
            nc.gpsimd.memset(v4[:, :], 1.0).then_inc(setup, 1)

            def add_squares(name):
                k = list(BEHIND).index(name)
                for m in range(1, DT - 1):
                    pool.wait_ge(sq_ready, SQBASE[name] + m + 1)
                    if m > 1:
                        pool.wait_ge(rest_summed, (DT - 2) * k + m - 1)
                    before = sq[:, 0:S] if m == 1 else ssum[:, :]
                    nc.gpsimd.tensor_tensor(ssum[:, :], before, sq[:, (m % 2) * S:(m % 2 + 1) * S],
                                            ALU.add).then_inc(rest_summed, 1)
                    if name == "final1":
                        pool.wait_ge(gsq_ready, m + 1)
                        if m > 1:
                            pool.wait_ge(gsum_ready, m - 1)
                        before = gsq[:, 0:S] if m == 1 else gsum[:, :]
                        nc.gpsimd.tensor_tensor(gsum[:, :], before, gsq[:, (m % 2) * S:(m % 2 + 1) * S],
                                                ALU.add).then_inc(gsum_ready, 1)

            def inverse_root(name):
                pool.wait_ge(var_ready, STATS.index(name) + 1)
                nc.gpsimd.tensor_tensor(r4[:, :], v4[:, :], mhalf[:, :], ALU.pow).then_inc(rs_ready, 1)

            def low(name):
                src, n, _, _, hi, lo = NORM[name]
                for m in range(1, dict(NORMS)[name], 2):
                    s = SBASE[NQ[name]] + m
                    pool.wait_ge(hhi_ready, s + 1)
                    here = slice(m * n, (m + 1) * n)
                    nc.gpsimd.tensor_tensor(lo[:, here], hf[:, (s % 4) * S:(s % 4) * S + n], hi[:, here].bitcast(f32),
                                            ALU.subtract).then_inc(h_ready[1], 1)

            pool.wait_ge(setup, 1)
            add_squares("amix")
            for name in ("amix", "mem"):
                inverse_root(name)
                low(name)
            def split_lo(c):
                pool.wait_ge(hi_ready, c.v + 1)
                pool.wait_ge(lo_ready, c.v + 2)
                here = slice(c.par * CW, (c.par + 1) * CW)
                nc.gpsimd.tensor_tensor(w_lo[:, here], raw[:, here], w_hi[:, here].bitcast(f32),
                                        ALU.subtract).then_inc(lo_ready, 1)

            for c in range(*POOL_CHUNKS["mem"]):
                split_lo(At(c))
                if c == CH["mem"] + 5:
                    inverse_root("ckv")

            def splits(stage):
                start, stop = POOL_CHUNKS[stage]
                with pool.Fori(0, (stop - start) // 2) as i:
                    for k in range(2):
                        split_lo(At(start + k, i, 2))

            splits("aq")
            add_squares("affn")
            inverse_root("affn")
            low("affn")
            add_squares("bmix")
            inverse_root("bmix")
            low("bmix")
            pool.wait_ge(x_ready, RESIDUALS["down0"] + DT)
            nc.gpsimd.memset(b_k[:, :], 0.0).then_inc(zeroed, 1)
            splits("bq")
            pool.wait_ge(roped, RP["nk_s"] + 1)
            pool.dma_start(tab64[:, :], tab2in).then_inc(ld["tab2"], 16)
            add_squares("bffn")
            inverse_root("bffn")
            low("bffn")
            add_squares("final1")
            for name in ("conv", "final1"):
                inverse_root(name)
            low("conv")
            add_squares("kv2")
            inverse_root("kv2")
            pool.wait_ge(x_ready, RESIDUALS["cout"] + DT)
            for tile in fold:
                pad = tile[:, :].rearrange("p (g c) -> p g c", g=4)[:, :, S - 1:FPAD]
                last = nc.gpsimd.memset(pad, 0.0)
            last.then_inc(zeroed, 1)
            low("kv2")
            nc.gpsimd.memset(n_k["win"][:, :], 0.0)
            nc.gpsimd.memset(n_k["slc"][:, :], 0.0).then_inc(zeroed, 1)
            low("q2")

            def branch_sum(i, j, p):
                t = i * 2 + j
                pool.wait_ge(om_ready, t * 2 + p)
                pool.wait_ge(o_scaled, ATT["nq"].first_pass + t * 3 + p)
                settle(pool)
                nc.gpsimd.tensor_tensor(o_sb[:, :], o_sb[:, :], om[:, :], ALU.add).then_inc(o_scaled, 1)

            def output_lo(i, j):
                ph, t = ATT["nq"], i * 2 + j
                pool.wait_ge(out_hi, ph.first_tile + t + 1)
                settle(pool)
                nc.gpsimd.tensor_tensor(G_lo[:, sl(t * S, S)], ysb[:, :], G_hi[:, sl(t * S, S)].bitcast(f32),
                                        ALU.subtract).then_inc(out_ready, 1)

            def tile(i, j, before, chunk):
                if before:
                    output_lo(i, j - 1)
                branch_sum(i, j, 1)
                if chunk:
                    split_lo(At(POOL_CHUNKS["nq"][0] + 1 + j, i, 2))
                branch_sum(i, j, 2)

            for k in range(2):
                split_lo(At(POOL_CHUNKS["nq"][0] + k))
            tile(0, 0, False, False)
            with pool.Fori(0, 3) as i:
                tile(i, 1, True, True)
                tile(i, 2, True, True)
            tile(0, 7, True, False)
            output_lo(0, 7)
            add_squares("final2")
            inverse_root("final2")

        @block.scalar
        def _(act):
            act.sem_inc(sq_used, 2)

            def split_hi(c):
                if isinstance(c.v, int) and c.v >= NCHUNKS:
                    return
                act.wait_ge(chunk_loaded[c.par], c.half * 16 + 16)
                act.wait_ge(chunk_used, c.v + 1)
                nc.scalar.activation(w_hi[:, c.par * CW:(c.par + 1) * CW], raw[:, c.par * CW:(c.par + 1) * CW],
                                     ACT.Copy).then_inc(hi_ready, 1)

            def take(dst, t, c, n=S, func=ACT.Copy, scale=1.0, rows=slice(0, P)):
                act.wait_ge(chunk_used, c.v + 3)
                nc.scalar.activation(dst, pj[t.par][rows, 0:n], func, scale=scale).then_inc(pj_free[t.par], 1)

            def squares(name, waits):
                src, n, _, _, _, _ = NORM[name]
                for m in range(dict(NORMS)[name]):
                    sem_, value = waits(m)
                    act.wait_ge(sem_, value)
                    act.wait_ge(sq_used, USED[name] + m + 1)
                    nc.scalar.activation(sq[:, (m % 2) * S:(m % 2) * S + n], src[:, m * n:(m + 1) * n],
                                         ACT.Square).then_inc(sq_ready, 1)

            def squares_as_they_come(name, waits):
                for m in range(DT):
                    act.wait_ge(*waits(m))
                    if m >= 2:
                        act.wait_ge(rest_summed, (DT - 2) * list(BEHIND).index(name) + max(1, m - 2))
                    nc.scalar.activation(sq[:, (m % 2) * S:(m % 2 + 1) * S], xT[:, m * S:(m + 1) * S],
                                         ACT.Square).then_inc(sq_ready, 1)

            def norm_hi(name):
                _, n, _, _, hi, _ = NORM[name]
                for m in range(dict(NORMS)[name]):
                    s = SBASE[NQ[name]] + m
                    act.wait_ge(hf_ready, s + 1)
                    nc.scalar.activation(hi[:, m * n:(m + 1) * n], hf[:, (s % 4) * S:(s % 4) * S + n],
                                         ACT.Copy).then_inc(hhi_ready, 1)

            def turn(t, c, number, dst, src, n=S, func=ACT.Copy, scale=1.0):
                take(vraw[:, 0:n], t, c, n)
                act.wait_ge(v_turned, number + 1)
                return nc.scalar.activation(dst, src, func, scale=scale)

            def bank3(number, lo, n):
                return pt[number % 2][:, :].rearrange("p (b c) -> p b c", b=NB)[:, :, lo:lo + n]

            def query(ph, i, j):
                c, t = query_at(ph, i, j)
                if ph.name != "amem":
                    act.wait_ge(roped, RP[ph.name] + max(j, 1) if isinstance(i, int) else RP[ph.name] + i * 2 + j)
                take(qn[:, j % 2 * S:(j % 2 + 1) * S], t, c)

            def keys_values(i, j):
                c, t = keys_values_at(i, j)
                par = j % 2
                take(a_k[0:96, par * S:(par + 1) * S], t, c, rows=slice(0, 96))
                take(a_v[:, par * S:(par + 1) * S], t + 1, c)

            def softmax(ph, i, j, u):
                at = later(ph, i, j, u)
                if at is None:
                    return
                i, j, u = at
                a = unit_of(ph, i, j, u)
                par = u % 2
                w = ph.keys(u)[1]
                p, _ = ph.split(u)
                g, r = bank_of(ph, j, p), ph.region(u)
                act.wait_ge(max_ready, a + 1)
                act.wait_ge(p_turned, a + 1)
                if ph.name == "bq":
                    h = (i * 2 + j) * 2 + ph.units[u][0]
                    settle(act)
                    nc.scalar.activation(of_pass(esink, g, r), nsink[:, sl(h, 1)], ACT.Exp, scale=-1.0,
                                         bias=ST(NEGM, par))
                nc.scalar.activation(p_sb[:, par * S:par * S + w], s_sb[:, par * S:par * S + w], ACT.Exp,
                                     scale=ph.scale, bias=ST(NEGM, par),
                                     accum_out=of_pass(lsum, g, r)).then_inc(exp_done, 1)

            def bring(ph, i, j, u):
                a = unit_of(ph, i, j, u)
                par = u % 2
                w = ph.keys(u)[1]
                act.wait_ge(p_turned, a + 3)
                act.wait_ge(pv_done, a + 1)
                rows = slice(0, min(w, P))
                n = max(w, P)
                nc.scalar.activation(pT[rows, par * S:par * S + n], pt[par][rows, 0:n],
                                     ACT.Copy).then_inc(pT_ready, 1)

            def output_hi(ph, i, j):
                t = i * 2 + j
                o = (ph.out0 + t) * S
                if ph.name == "nq":
                    act.wait_ge(y_ready, t + 1)
                    src = ysb
                else:
                    act.wait_ge(o_turned, ph.first_tile + t + 1)
                    src = po[bank_of(ph, j, ph.passes - 1)]
                settle(act)
                nc.scalar.activation(G_hi[:, sl(o, S)], src[:, :], ACT.Copy).then_inc(out_hi, 1)

            def tile(ph, i, j):
                for u in range(ph.n):
                    p, v = ph.split(u)
                    bring(ph, i, j, u)
                    if u == ph.at_query and ph.m == 8 and ahead(ph, i, j):
                        query(ph, i, j + 2)
                    if ph.name == "aq" and u == 1 and more(ph, i, j):
                        keys_values(i, j + 1)
                    if u == ph.at_refill and more(ph, i, j):
                        if ph.name == "aq":
                            split_hi(keys_values_at(i, j + 1)[0] + 2)
                        elif ph.name == "bmem" or ph.name != "amem" and not (isinstance(i, int) and j == 0):
                            split_hi(query_at(ph, i, j + 1)[0] + 2)
                    softmax(ph, i, j, u + 2)
                    if u == ph.at_query and ph.name == "aq":
                        query(ph, i, j + 2)
                        split_hi(query_at(ph, i, j + 2)[0] + 2)
                    last = before(ph, i, j, p)
                    if v == ph.at_hi and p == 0 and last:
                        output_hi(ph, *last[:2])

            def attention(name):
                ph = ATT[name]
                if name in ("aq", "bq", "nq"):
                    for j in range(2):
                        query(ph, 0, j)
                        split_hi(query_at(ph, 0, j)[0] + 2)
                if name == "aq":
                    keys_values(0, 0)
                    split_hi(keys_values_at(0, 0)[0] + 2)
                if name == "bmem":
                    split_hi(query_at(ph, 0, 0)[0] + 2)
                softmax(ph, 0, 0, 0)
                softmax(ph, 0, 0, 1)
                attention_tiles(act, ph, tile)
                output_hi(ph, 0, ph.tiles - 1)

            def square(name, i, j):
                m = i * 2 + j
                act.wait_ge(x_ready, RESIDUALS[BEHIND[name]] + m + 1)
                if not isinstance(m, int) or m >= 2:
                    act.wait_ge(rest_summed, (DT - 2) * list(BEHIND).index(name) + m - 1)
                settle(act)
                nc.scalar.activation(sq[:, j * S:(j + 1) * S], xT[:, sl(m * S, S)], ACT.Square).then_inc(sq_ready, 1)
                if name == "final1":
                    if not isinstance(m, int) or m >= 2:
                        act.wait_ge(gsum_ready, m - 1)
                    settle(act)
                    nc.scalar.activation(gsq[:, j * S:(j + 1) * S], xT[:, sl(m * S, S)], ACT.Square,
                                         scale=vec[:, sl(m + VC["g_final"], 1)]).then_inc(gsq_ready, 1)

            def residual(name, per):
                stage = BEHIND[name]

                def two(i):
                    for j in range(2):
                        for k in range(per):
                            split_hi(At(CH[stage] + j * per + k + 2, i, 2 * per))
                        square(name, i, j)

                two(0)
                with act.Fori(1, DT // 2 - (1 if stage == "nout" else 0)) as i:
                    two(i)
                if stage == "nout":
                    two(DT // 2 - 1)

            def packed_residual(name):
                stage = BEHIND[name]
                for j in range(DT):
                    for c in chunks_of(j):
                        split_hi(At(CH[stage] + c + 2))
                    square(name, j // 2, j % 2)

            def feed_forward(l):
                up, base = CH[f"up{l}"], TL[f"up{l}"]
                with act.Fori(0, FT) as i:
                    split_hi(At(up + 2, i, 2))
                    t = At(base, i, 2)
                    act.wait_ge(pj_free[t.par], t.half + 2)
                    nc.scalar.activation(fb[:, :], fa[:, :], ACT.Silu).then_inc(act_ready, 1)
                    split_hi(At(up + 3, i, 2))
                    t = At(base + 1, i, 2)
                    act.wait_ge(pj_free[t.par], t.half + 2)
                    settle(act)
                    nc.scalar.activation(G_hi[:, ds(i * S, S)], fc[:, :], ACT.Copy).then_inc(g_hi_ready, 1)
                residual(("bmix", "final1")[l], DOWN_CHUNKS)

            def tables(k):
                tab = (tab64, tab128)[k]
                act.wait_ge(angle_ready, k + 1)
                nc.scalar.activation(tab[:, S:2 * S], ang[:, :], ACT.Sin)
                nc.scalar.activation(tab[:, 0:S], turns[:, :], ACT.Sin).then_inc(sin_ready, 1)

            squares_as_they_come("amix", lambda m: (x_loaded[m // 2], 16))
            tables(0)
            split_hi(At(0))
            split_hi(At(1))
            norm_hi("amix")
            c, t = At(CH["afront"]), At(TL["afront"])
            split_hi(c + 2)
            take(qn[:, 0:S], t, c)
            squares("mem", lambda m: (ld["mem"], 16))
            tables(1)
            norm_hi("mem")
            all_normed(act, "mem")
            c, t = At(CH["afront"] + 1), At(TL["afront"] + 1)
            split_hi(c + 2)
            take(qn[:, S:2 * S], t, c)
            act.wait_ge(v_turned, TN["widx"] + 1)
            nc.scalar.activation(widx[:, :].rearrange("p (b c) -> p b c", b=NB), bank3(TN["widx"], 0, 16),
                                 ACT.Copy, scale=1024.0 ** -0.5)

            def idx_query(i, j):
                c, t = At(CH["idx"] + j, i, 2), At(TL["idx"] + j, i, 2)
                act.wait_ge(roped, RP["idx"] + j + i * 2)
                take(qn[:, j % 2 * S:(j % 2 + 1) * S], t, c)

            def idx_tile(i, j, more):
                t = i * 2 + j
                for u, (hh, b) in enumerate(IDX_UNITS):
                    s = t * len(IDX_UNITS) + u
                    w = (b + 1) * P
                    act.wait_ge(score_done, s + 1)
                    act.wait_ge(idx_added, s + 1)
                    nc.scalar.activation(s_sb[:, (u % 2) * S:(u % 2) * S + w], ps[u % 2][:, 0:w],
                                         ACT.Relu).then_inc(score_taken, 1)
                    if u == 4 and more:
                        idx_query(i, j + 2)
                if more:
                    split_hi(At(CH["idx"] + j + 4, i, 2))

            for j in range(2):
                split_hi(At(CH["idx"] + j + 2))
                idx_query(0, j)
            with act.Fori(0, 3) as i:
                idx_tile(i, 0, True)
                idx_tile(i, 1, True)
            idx_tile(3, 0, False)
            idx_tile(3, 1, False)

            for k in range(2):
                c, t = At(CH["ckv"] + k), At(TL["ckv"] + k)
                split_hi(c + 2)
                take(ckv[:, k * S:(k + 1) * S], t, c)
            tk = TL["ckv"]
            squares("ckv", lambda m: (pj_free[(tk + m) % 2], (tk + m) // 2 + 2))
            number = TN["memv"]
            for l in range(2):
                for k in range(4):
                    c, t = At(CH["mem"] + 4 * l + k), At(TL["mem"] + 4 * l + k)
                    split_hi(c + 2)
                    if k < 2:
                        act.wait_ge(chunk_used, c.v + 3)
                        for hh in range(2):
                            last = nc.scalar.activation(mem_k[l][:, (2 * k + hh) * MEM:(2 * k + hh + 1) * MEM],
                                                        pj[t.par][:, 0:MEM], ACT.Copy, scale=C("half", hh))
                        last.then_inc(pj_free[t.par], 1)
                    else:
                        turn(t, c, number, mem_v[l][:, :].rearrange("p (b c) -> p b c", b=2)[:, :, (k - 2) * P:(k - 1) * P],
                             pt[number % 2][:, 0:MEM].rearrange("p (b c) -> p b c", b=2), n=MEM)
                        number += 1
            norm_hi("ckv")
            attention("aq")
            attention("amem")
            packed_residual("affn")
            norm_hi("affn")
            feed_forward(0)

            norm_hi("bmix")
            for k in range(2):
                c, t = At(CH["bfront"] + k), At(TL["bfront"] + k)
                split_hi(c + 2)
                act.wait_ge(roped, RP["bk"] + k + 1)
                take(qraw[:, :], t, c)
            for k in range(2):
                c, t = At(CH["bfront"] + 2 + k), At(TL["bfront"] + 2 + k)
                split_hi(c + 2)
                turn(t, c, TN["bv"] + k, b_v[:, :].rearrange("p (b c) -> p b c", b=NB)[:, :, k * P:(k + 1) * P],
                     bank3(TN["bv"] + k, 0, P))
            attention("bq")
            attention("bmem")
            packed_residual("bffn")
            norm_hi("bffn")
            feed_forward(1)

            norm_hi("conv")
            with act.Fori(0, CT) as i:
                c, t = At(CH["conv"], i, 4), At(TL["conv"], i, 4)
                split_hi(c + 2)
                take(fa[:, :], t, c)
                split_hi(c + 3)
                split_hi(c + 4)
                take(fd[:, :], t + 2, c + 2, func=ACT.Silu)
                split_hi(c + 5)
                act.wait_ge(pj_free[(t + 3).par], (t + 3).half + 2)
                settle(act)
                nc.scalar.activation(G_hi[:, ds(i * S, S)], fg[:, :], ACT.Copy).then_inc(g_hi_ready, 1)
            residual("kv2", 2)
            norm_hi("kv2")

            pieces = [(which, part) for which in range(2) for part in range(2)]
            act.wait_ge(zeroed, 2)

            def window_hi(k):
                which, part = pieces[k]
                act.wait_ge(win_summed, k + 1)
                nc.scalar.activation(win_hi[which][:, part * CW:(part + 1) * CW], win[:, part * CW:(part + 1) * CW],
                                     ACT.Copy).then_inc(win_hi_ready, 1)

            for k in range(4):
                c, t = At(CH["cmp_kv"] + k), At(TL["cmp_kv"] + k)
                which, pair = k // 2, k % 2
                split_hi(c + 2)
                act.wait_ge(chunk_used, c.v + 3)
                for g in range(2):
                    at, rows = (2 * pair + g) * FPAD, slice(g * 64, g * 64 + 64)
                    nc.scalar.activation(fold[which][0:64, at:at + S], pj[t.par][rows, :], ACT.Copy)
                    last = nc.scalar.activation(fold[which][64:P, at:at + S - 1], pj[t.par][rows, 1:S], ACT.Copy)
                last.then_inc(pj_free[t.par], 1)
                if k >= 2:
                    window_hi(k - 2)
            window_hi(2)
            window_hi(3)
            for which in range(2):
                for n in range(4):
                    split_hi(At(CH["cmp"] + 4 * which + n + 2))
                act.wait_ge(hid_x, which + 1)
                nc.scalar.activation(hidt[:, :], hidt[:, :], ACT.Tanh, scale=0.7978845608028654).then_inc(hid_th, 1)

            def hidden_hi(which):
                act.wait_ge(hid_turned, which + 1)
                nc.scalar.activation(hid_hi[:, 2 * which * P:2 * (which + 1) * P], HIDDEN[which][:, 0:2 * P],
                                     ACT.Copy).then_inc(hid_hi_ready, 1)

            for s, (kn, vn, branch) in enumerate((("nk_s", "nv_s", "slc"), ("nk_w", "nv_w", "win"))):
                if s:
                    c, t = At(CH["cmp2"]), At(TL["cmp2"] + 1)
                    split_hi(c + 2)
                    turn(t, c, TN["cmpv"], cmp_v[0:NCMP, :].rearrange("p (g c) -> p g c", g=4),
                         pt[TN["cmpv"] % 2][0:NCMP, :].rearrange("p (g c) -> p g c", g=4)[:, :, 0:64], n=P)
                stage = ("nkv_s", "nkv_w")[s]
                for k in range(2):
                    c, t = At(CH[stage] + k), At(TL[stage] + k)
                    split_hi(c + 2)
                    act.wait_ge(roped, RP[kn] + k + 1)
                    take(qraw[:, :], t, c)
                    if s == 0:
                        hidden_hi(k)
                for k in range(2):
                    c, t = At(CH[stage] + 2 + k), At(TL[stage] + 2 + k)
                    split_hi(c + 2)
                    turn(t, c, TN[vn] + k,
                         n_v[branch][:, :].rearrange("p (b c) -> p b c", b=NB)[:, :, k * P:(k + 1) * P],
                         bank3(TN[vn] + k, 0, P))
            act.wait_ge(roped, RP["nq"] + 1)
            norm_hi("q2")
            c, t = At(CH["gates"]), At(TL["gates"])
            split_hi(c + 2)
            turn(t, c, TN["gates"], gate[:, :].rearrange("p (b c) -> p b c", b=NB), bank3(TN["gates"], 0, 48),
                 func=ACT.Sigmoid).then_inc(gate_done, 1)
            with act.Fori(0, 4) as i:
                for k in range(2):
                    c, t = At(CH["nz"] + k, i, 2), At(TL["nz"] + k, i, 2)
                    split_hi(c + 2)
                    take(zsil[:, ds((i * 2 + k) * S, S)], t, c, func=ACT.Silu)
            attention("nq")
            residual("final2", 1)

        @block.vector
        def _(dve):
            link = Links(dve, dve_step)
            for b in range(2):
                dve.sem_inc(pj_free[b], 1)
            dve.sem_inc(lo_ready, 2)
            dve.sem_inc(score_taken, 2)
            dve.sem_inc(idx_added, 2)
            dve.sem_inc(roped, 1)
            dve.sem_inc(out_ready, 1)
            dve.sem_inc(g_ready, 1)
            dve.wait_ge(setup, 1)

            def split_lo(c):
                if isinstance(c.v, int) and c.v >= NCHUNKS:
                    return
                dve.wait_ge(hi_ready, c.v + 1)
                here = slice(c.par * CW, (c.par + 1) * CW)
                nc.vector.tensor_tensor(w_lo[:, here], raw[:, here], w_hi[:, here].bitcast(f32),
                                        ALU.subtract).then_inc(lo_ready, 1)

            def complete(c):
                dve.wait_ge(chunk_used, c.v + 3)

            def means(name):
                k = dict(NORMS)[name]
                blocks = NORM[name][1] // P
                if name in BEHIND:
                    dve.wait_ge(rest_used, list(BEHIND).index(name) + 1)
                else:
                    dve.wait_ge(sq_used, USED[name] + k + 2)
                for b in range(blocks):
                    last = nc.vector.tensor_scalar(v4[:, b:b + 1], sum_banks(name)[b][:, 0:1], 1.0 / (k * P), EPS,
                                                   ALU.mult, ALU.add)
                last.then_inc(var_ready, 1)

            def norm(name):
                means(name)
                apply(name)

            def two_norms():
                n = STATS.index("conv")
                nc.vector.tensor_tensor(gg[:, :], vec[:, VC["g_final"]:VC["g_final"] + DT],
                                        vec[:, VC["a_norm"]:VC["a_norm"] + DT], ALU.mult)
                dve.wait_ge(g_used, 1)
                means("final1")
                for b in range(NB):
                    link.mark(nc.vector.tensor_scalar(vg[:, b:b + 1], sum_banks("final1")[b][:, 1:2], 1.0 / D, None,
                                                      ALU.mult))
                dve.wait_ge(rs_ready, n + 1)
                link(nc.vector.tensor_copy(r1[:, 0:NB], r4[:, 0:NB]))
                for k in range(2):
                    link(nc.vector.tensor_tensor(vg[:, 0:NB], vg[:, 0:NB], r1[:, 0:NB], ALU.mult))
                nc.vector.tensor_scalar(v4[:, 0:NB], vg[:, 0:NB], EPS, None, ALU.add).then_inc(var_ready, 1)
                dve.wait_ge(rs_ready, n + 2)
                nc.vector.tensor_tensor(r12[:, 0:NB], r1[:, 0:NB], r4[:, 0:NB], ALU.mult).then_inc(r12_ready, 1)
                dve.wait_ge(factor_ready, n + 2)
                apply("conv")
                apply("final1")

            def apply(name):
                src, n, gain, first, hi, lo = NORM[name]
                factor = po[0] if name == "conv" else px

                def gains(m):
                    return gg[:, m:m + 1] if name == "conv" else V(gain, first + m)

                q = NQ[name]
                k = NORMS[q][1]
                if name not in ("q2", "conv", "final1"):
                    dve.wait_ge(factor_ready, STATS.index(name) + 1)

                def low(m):
                    if m % 2 == 0 or name == "ckv":
                        s = SBASE[q] + m
                        dve.wait_ge(hhi_ready, s + 1)
                        here = slice(m * n, (m + 1) * n)
                        nc.vector.tensor_tensor(lo[:, here], hf[:, (s % 4) * S:(s % 4) * S + n], hi[:, here].bitcast(f32),
                                                ALU.subtract).then_inc(h_ready[m % 2], 1)

                for m in range(k):
                    here = slice(m * n, (m + 1) * n)
                    if hi is None:
                        nc.vector.scalar_tensor_tensor(out=src[:, here], in0=src[:, here], scalar=gains(m),
                                                       in1=factor[:, 0:n], op0=ALU.mult,
                                                       op1=ALU.mult).then_inc(h_ready[m % 2], 1)
                        continue
                    s = SBASE[q] + m
                    if m >= 4:
                        dve.wait_ge(*normed(name, m - 4))
                    nc.vector.scalar_tensor_tensor(out=hf[:, (s % 4) * S:(s % 4) * S + n], in0=src[:, here],
                                                   scalar=gains(m), in1=factor[:, 0:n],
                                                   op0=ALU.mult, op1=ALU.mult).then_inc(hf_ready, 1)
                    if m:
                        low(m - 1)
                if hi is not None:
                    low(k - 1)
                all_normed(dve, name)

            def rope(dst, src, tab, mask, t):
                rope_start(dst, src, tab, mask, t)
                return rope_end(dst, tab)

            def rope_start(dst, src, tab, mask, t):
                dve.wait_ge(pj_free[t.par], t.half + 2)
                nc.vector.tensor_tensor(dst, src, tab[:, 0:S], ALU.mult)
                link(nc.vector.stream_shuffle(rtmp[:, :], src, mask))

            def rope_end(dst, tab):
                link(nc.vector.tensor_tensor(rtmp[:, :], rtmp[:, :], tab[:, S:2 * S], ALU.mult))
                return nc.vector.tensor_tensor(dst, dst, rtmp[:, :], ALU.add)

            def spread_keys(dst, pair):
                for g in range(2):
                    for hh in range(2):
                        col = ((2 * pair + g) * 2 + hh) * S
                        last = nc.vector.tensor_copy(dst[hh * 64:hh * 64 + 64, col:col + S], ktmp[g * 64:g * 64 + 64, 0:S])
                return last

            def query(ph, i, j, half):
                if ph.units[0][2] == "mem":
                    return
                t = query_at(ph, i, j)[1]
                par = j % 2
                dst, src = qs[:, par * S:(par + 1) * S], qn[:, par * S:(par + 1) * S]
                tab, mask = (tab128, SHUF128) if ph.name == "aq" else (tab64, SHUF64)
                if half == 0:
                    rope_start(dst, src, tab, mask, t)
                else:
                    rope_end(dst, tab).then_inc(roped, 1)


            def bias(ph, u):
                _, b, branch = ph.units[u]
                if branch == "topk" and b:
                    return bias_a[:, (b - 1) * S:(b - 1) * S + (b + 1) * P]
                if branch == "mem":
                    return C("causal", 0, MEM)
                if branch == "band":
                    return C("band", P, P) if b == 0 else C("band", 0, 2 * P)
                if branch == "cmp":
                    return C("cmp", b * NCMP, NCMP)
                return causal(b)

            def maximum(ph, i, j, u):
                at = later(ph, i, j, u)
                if at is None:
                    return
                i, j, u = at
                s, a = ph.first_score + (i * 2 + j) * ph.n + u, unit_of(ph, i, j, u)
                par = u % 2
                w = ph.keys(u)[1]
                dve.wait_ge(score_done, s + 1)
                dve.wait_ge(exp_done, a + 1)
                settle(dve)
                nc.vector.tensor_tensor_reduce(out=s_sb[:, par * S:par * S + w], in0=ps[par][:, 0:w], in1=bias(ph, u),
                                               scale=1.0, scalar=-3.0e38, op0=ALU.add, op1=ALU.max,
                                               accum_out=ST(MX, par)).then_inc(score_taken, 1)
                dve.wait_ge(score_taken, s + 3)
                if ph.name == "bq":
                    h = (i * 2 + j) * 2 + ph.units[u][0]
                    nc.vector.tensor_scalar(ST(NEGM, par), ST(MX, par), -ph.scale, nsink[:, sl(h, 1)],
                                            ALU.mult, ALU.min).then_inc(max_ready, 1)
                else:
                    nc.vector.tensor_scalar(ST(NEGM, par), ST(MX, par), -ph.scale, None, ALU.mult).then_inc(max_ready, 1)

            def scale_pass(ph, i, j, p):
                t, g = i * 2 + j, bank_of(ph, j, p)
                end = unit_of(ph, i, j, (p + 1) * ph.m - 1)
                n = ph.m
                dve.wait_ge(exp_done, end + 3)
                total, c = of_pass(lsum, g, 0, n), of_pass(coef, g, 0, n)
                if ph.name == "bq":
                    link(nc.vector.tensor_tensor(c, total, of_pass(esink, g, 0, n), ALU.add))
                    total = c
                link(nc.vector.reciprocal(c, total))
                if ph.name == "nq":
                    gates = gate[:, :].rearrange("p (b c) -> p b c", b=NB)[:, :, sl(t * 2 + p * 16, 2)]
                    c3 = c.rearrange("p (b h) -> p b h", b=NB)
                    link(nc.vector.tensor_tensor(c3, c3, gates, ALU.mult))
                dve.wait_ge(pv_done, end + 3)
                if ph.first_tile or not (isinstance(i, int) and j == 0):
                    dve.wait_ge(o_turned, ph.first_tile + t)
                if p > 1:
                    dve.wait_ge(o_scaled, pass_of(ph, i, j, p))
                settle(dve)
                dst = o_sb if p == 0 else om
                scaled = nc.vector.tensor_tensor(dst[:, :].rearrange("p (r c) -> p r c", r=n),
                                                 po[g][:, :].rearrange("p (r c) -> p r c", r=n),
                                                 c.unsqueeze(2).broadcast_to([P, n, ph.dv]), ALU.mult)
                scaled.then_inc(om_ready if p else o_scaled, 1)

            def gate_output(ph, i, j):
                t = i * 2 + j
                dve.wait_ge(o_turned, ph.first_tile + t + 1)
                dve.wait_ge(out_ready, ph.first_tile + t + 1)
                nc.vector.tensor_tensor(ysb[:, :], po[bank_of(ph, j, ph.passes - 1)][:, :], zsil[:, sl(t * S, S)],
                                        ALU.mult).then_inc(y_ready, 1)

            def output_lo(ph, i, j):
                if ph.name == "nq":
                    return
                t = i * 2 + j
                o = (ph.out0 + t) * S
                src = po[bank_of(ph, j, ph.passes - 1)]
                dve.wait_ge(out_hi, ph.first_tile + t + 1)
                nc.vector.tensor_tensor(G_lo[:, sl(o, S)], src[:, :], G_hi[:, sl(o, S)].bitcast(f32),
                                        ALU.subtract).then_inc(out_ready, 1)

            def tile(ph, i, j):
                for u in range(ph.n):
                    p, v = ph.split(u)
                    maximum(ph, i, j, u + 2)
                    last = before(ph, i, j, p)
                    if last and v == ph.at_scale:
                        scale_pass(ph, *last)
                    if more(ph, i, j) and ph.at_rope is not None and u in (ph.at_rope, ph.at_rope + 1):
                        query(ph, i, j + 1, u - ph.at_rope)
                    if last and p == 0:
                        if v == ph.at_gate and ph.name == "nq":
                            gate_output(ph, *last[:2])
                        if v == ph.at_lo:
                            output_lo(ph, *last[:2])

            LINKS = {"aq": 2 * (2 + 1), "amem": 0, "bq": 2 * (2 + 2), "bmem": 0, "nq": 2 * (2 + 6)}

            def attention(name, begun=False):
                ph = ATT[name]
                for part in range(0 if begun else 2):
                    query(ph, 0, 0, part)
                maximum(ph, 0, 0, 0)
                maximum(ph, 0, 0, 1)
                attention_tiles(dve, ph, tile, link, LINKS[name])
                end = ph.tiles - 1
                scale_pass(ph, 0, end, ph.passes - 1)
                if ph.name == "nq":
                    gate_output(ph, 0, end)
                output_lo(ph, 0, end)
                if name in ("amem", "bmem", "nq"):
                    dve.wait_ge(lo_ready, POOL_CHUNKS[{"amem": "aq", "bmem": "bq", "nq": "nq"}[name]][1] + 2)

            def residual(stage, per):
                def two(i, last=False):
                    for j in range(2):
                        for k in range(per):
                            split_lo(At(CH[stage] + j * per + k + 2, i, 2 * per))
                        c, t = At(CH[stage] + (j + 1) * per - 1, i, 2 * per), At(TL[stage] + j, i, 2)
                        complete(c)
                        here = xT[:, sl((i * 2 + j) * S, S)]
                        nc.vector.tensor_tensor(here, here, pj[t.par][:, :], ALU.add).then_inc(pj_free[t.par], 1)
                        dve.wait_ge(pj_free[t.par], t.half + 2)
                        dve.sem_inc(x_ready, 1)

                trips = DT // 2 - (1 if stage == "nout" else 0)
                with dve.Fori(0, trips) as i:
                    two(i)
                if stage == "nout":
                    two(trips)

            def packed_residual(stage):
                for j in range(DT):
                    for c in chunks_of(j):
                        split_lo(At(CH[stage] + c + 2))
                    t = At(TL[stage] + j)
                    complete(At(CH[stage] + chunks_of(j)[-1]))
                    here = xT[:, j * S:(j + 1) * S]
                    nc.vector.tensor_tensor(here, here, pj[t.par][:, :], ALU.add).then_inc(pj_free[t.par], 1)
                    dve.wait_ge(pj_free[t.par], t.half + 2)
                    dve.sem_inc(x_ready, 1)

            def feed_forward(l):
                up, base = CH[f"up{l}"], TL[f"up{l}"]
                with dve.Fori(0, FT) as i:
                    link.begin(i, 2)
                    c, t = At(up, i, 2), At(base, i, 2)
                    split_lo(c + 2)
                    complete(c)
                    w = [VD("f_conv_w", i + (l * 3 + j) * FT) for j in range(3)]
                    a = pj[t.par]
                    link(nc.vector.tensor_scalar(fa[:, :], a[:, :], w[2], VD("f_conv_b", i + l * FT), ALU.mult, ALU.add))
                    link(nc.vector.scalar_tensor_tensor(out=fa[:, 1:S], in0=a[:, 0:S - 1], scalar=w[1], in1=fa[:, 1:S],
                                                        op0=ALU.mult, op1=ALU.add))
                    nc.vector.scalar_tensor_tensor(out=fa[:, 2:S], in0=a[:, 0:S - 2], scalar=w[0], in1=fa[:, 2:S],
                                                   op0=ALU.mult, op1=ALU.add).then_inc(pj_free[t.par], 1)
                    split_lo(c + 3)
                    complete(c + 1)
                    dve.wait_ge(act_ready, i + (l * FT + 1))
                    dve.wait_ge(g_ready, i + (l * FT + 1))
                    nc.vector.tensor_tensor(fc[:, :], fb[:, :], pj[(t + 1).par][:, :],
                                            ALU.mult).then_inc(pj_free[(t + 1).par], 1)
                    dve.wait_ge(g_hi_ready, i + (l * FT + 1))
                    nc.vector.tensor_tensor(G_lo[:, ds(i * S, S)], fc[:, :], G_hi[:, ds(i * S, S)].bitcast(f32),
                                            ALU.subtract).then_inc(g_ready, 1)
                link.end(2, FT)
                residual(f"down{l}", DOWN_CHUNKS)

            def angles(k):
                width, tab = (("64", tab64), ("128", tab128))[k]
                if k:
                    dve.wait_ge(sin_ready, k)
                link(nc.vector.tensor_scalar(ang[:, :], posf[:, :], C("inv" + width), None, ALU.mult))
                link(nc.vector.tensor_scalar(turns[:, :], ang[:, :], 1.0 / TWO_PI, ROUNDER, ALU.mult, ALU.add))
                link(nc.vector.tensor_scalar(turns[:, :], turns[:, :], ROUNDER, None, ALU.subtract))
                for part in (PI_HI, PI_LO):
                    link(nc.vector.scalar_tensor_tensor(out=ang[:, :], in0=turns[:, :], scalar=-part, in1=ang[:, :],
                                                        op0=ALU.mult, op1=ALU.add))
                link(nc.vector.tensor_scalar(ang[:, :], ang[:, :], 3.1415925, -3.1415925, ALU.min, ALU.max))
                link(nc.vector.scalar_tensor_tensor(out=turns[:, :], in0=ang[:, :], scalar=-1.0, in1=ang[:, :],
                                                    op0=ALU.mult, op1=ALU.max))
                nc.vector.tensor_scalar(turns[:, :], turns[:, :], -1.0, TWO_PI / 4, ALU.mult,
                                        ALU.add).then_inc(angle_ready, 1)

            def sines(k):
                width, tab = (("64", tab64), ("128", tab128))[k]
                dve.wait_ge(sin_ready, k + 1)
                link(nc.vector.tensor_scalar(tab[:, S:2 * S], tab[:, S:2 * S], C("sgn" + width), None, ALU.mult))

            dve.wait_ge(ld["pos"], 16)
            link(nc.vector.tensor_copy(posf[:, :], posi[:, :]))
            dve.wait_ge(ld["cst"], 16)
            angles(0)
            means("amix")
            dve.wait_ge(ld["vec"], 16)
            nc.vector.tensor_scalar(nsink[:, :], vec[:, VC["sinks"]:VC["sinks"] + 16], -1.0, None, ALU.mult)
            split_lo(At(0))
            apply("amix")
            split_lo(At(1))
            sines(0)
            c, t = At(CH["afront"]), At(TL["afront"])
            split_lo(c + 2)
            link(rope(ktmp[:, S:2 * S], qn[:, 0:S], tab64, SHUF64, t))
            for hh in range(2):
                last = nc.vector.tensor_scalar(kidx[:, hh * S:(hh + 1) * S], ktmp[:, S:2 * S], C("half", hh), None,
                                               ALU.mult)
            last.then_inc(roped, 1)
            means("mem")
            angles(1)
            apply("mem")
            sines(1)
            split_lo(At(CH["afront"] + 3))
            t = At(TL["afront"] + 1)
            link(rope(ktmp[:, 0:S], qn[:, S:2 * S], tab128, SHUF128, t))
            for par in range(2):
                last = nc.vector.tensor_copy(a_k[96:P, par * S:(par + 1) * S], ktmp[96:P, 0:S])
            last.then_inc(roped, 1)

            def idx_query(i, j, half):
                par = j % 2
                dst = qs[:, par * S:(par + 1) * S]
                if half == 0:
                    rope_start(dst, qn[:, par * S:(par + 1) * S], tab64, SHUF64, At(TL["idx"] + j, i, 2))
                else:
                    rope_end(dst, tab64).then_inc(roped, 1)

            def idx_tile(i, j, more):
                t = i * 2 + j
                for u, (hh, b) in enumerate(IDX_UNITS):
                    s = t * len(IDX_UNITS) + u
                    w = (b + 1) * P
                    here = score[:, (b - 1) * S:(b - 1) * S + w]
                    dve.wait_ge(score_taken, s + 3)
                    dve.wait_ge(idx_added, s + 1)
                    nc.vector.scalar_tensor_tensor(out=here, in0=s_sb[:, (u % 2) * S:(u % 2) * S + w],
                                                   scalar=widx[:, sl(b * 16 + t * 2 + hh, 1)], in1=here,
                                                   op0=ALU.mult, op1=ALU.add).then_inc(idx_added, 1)
                    if u < 2 and (more or j == 0):
                        idx_query(i, j + 1, u)
                if more:
                    split_lo(At(CH["idx"] + j + 4, i, 2))

            for j in range(2):
                split_lo(At(CH["idx"] + j + 2))
                if j == 0:
                    idx_query(0, 0, 0)
                    idx_query(0, 0, 1)
            with dve.Fori(0, 3) as i:
                link.begin(i, 4)
                idx_tile(i, 0, True)
                idx_tile(i, 1, True)
            link.end(4, 3)
            idx_tile(3, 0, False)
            idx_tile(3, 1, False)
            rows = [(b, score[:, (b - 1) * S:(b - 1) * S + (b + 1) * P], m8[:, (b - 1) * 8:b * 8]) for b in range(1, NB)]
            dve.wait_ge(idx_added, IDX_SCORES + 2)
            for b, here, _ in rows:
                link.mark(nc.vector.tensor_tensor(here, here, causal(b), ALU.add))
            link.catch()

            def rounds(n):
                with dve.Fori(0, n) as i:
                    link.begin(i, 6)
                    for b, here, best in rows:
                        link.mark(nc.vector.max(best, here))
                    link.catch()
                    settle(dve)
                    for b, here, best in rows:
                        link.mark(nc.vector.match_replace(here, best, here, TAKEN))
                    link.catch()
                link.end(6, n)

            rounds(6)
            means("ckv")
            rounds(4)
            apply("ckv")
            rounds(2)
            for part in range(2):
                query(ATT["aq"], 0, 0, part)
            rounds(TOPK // 8 - 12)
            for b, here, _ in rows:
                link.mark(nc.vector.tensor_scalar(bias_a[:, (b - 1) * S:(b - 1) * S + (b + 1) * P], here, -2e38, NEG,
                                                  ALU.is_gt, ALU.mult))
            link.catch()
            attention("aq", begun=True)
            attention("amem")
            packed_residual("aout")
            norm("affn")
            feed_forward(0)

            norm("bmix")
            dve.wait_ge(zeroed, 1)
            for k in range(4):
                c, t = At(CH["bfront"] + k), At(TL["bfront"] + k)
                split_lo(c + 2)
                if k < 2:
                    link(rope(ktmp[:, 0:S], qraw[:, :], tab64, SHUF64, t))
                    spread_keys(b_k, k).then_inc(roped, 1)
            attention("bq")
            attention("bmem")
            packed_residual("bout")
            norm("bffn")
            feed_forward(1)
            two_norms()

            with dve.Fori(0, CT) as i:
                link.begin(i, 4)
                c, t = At(CH["conv"], i, 4), At(TL["conv"], i, 4)
                split_lo(c + 2)
                split_lo(c + 3)
                dve.wait_ge(pj_free[t.par], t.half + 2)
                complete(c + 1)
                nc.vector.tensor_tensor(fb[:, :], fa[:, :], pj[(t + 1).par][:, :],
                                        ALU.mult).then_inc(pj_free[(t + 1).par], 1)
                dve.wait_ge(pj_free[(t + 1).par], (t + 1).half + 2)
                w = [VD("a_conv_w", i + j * CT) for j in range(3)]
                link(nc.vector.tensor_scalar(fc[:, :], fb[:, :], w[2], None, ALU.mult))
                link(nc.vector.scalar_tensor_tensor(out=fc[:, 1:S], in0=fb[:, 0:S - 1], scalar=w[1], in1=fc[:, 1:S],
                                                    op0=ALU.mult, op1=ALU.add))
                link(nc.vector.scalar_tensor_tensor(out=fc[:, 2:S], in0=fb[:, 0:S - 2], scalar=w[0], in1=fc[:, 2:S],
                                                    op0=ALU.mult, op1=ALU.add))
                split_lo(c + 4)
                dve.wait_ge(pj_free[t.par], t.half + 1 + 2)
                link(nc.vector.tensor_tensor(fe[:, :], fc[:, :], fd[:, :], ALU.mult))
                split_lo(c + 5)
                complete(c + 3)
                dve.wait_ge(g_ready, i + (2 * FT + 1))
                nc.vector.tensor_tensor(fg[:, :], fe[:, :], pj[(t + 3).par][:, :],
                                        ALU.mult).then_inc(pj_free[(t + 3).par], 1)
                dve.wait_ge(g_hi_ready, i + (2 * FT + 1))
                nc.vector.tensor_tensor(G_lo[:, ds(i * S, S)], fg[:, :], G_hi[:, ds(i * S, S)].bitcast(f32),
                                        ALU.subtract).then_inc(g_ready, 1)
            link.end(4, CT)
            residual("cout", 2)
            norm("kv2")

            for k in range(2):
                split_lo(At(CH["cmp_kv"] + k + 2))
            for which in range(2):
                for k in range(2 if which else 0):
                    split_lo(At(CH["cmp_kv"] + 2 * which + k + 2))
                t = At(TL["cmp_kv"] + 2 * which + 1)
                dve.wait_ge(pj_free[t.par], t.half + 2)
                for part in range(2):
                    n = which * 2 + part
                    here = slice(part * CW, (part + 1) * CW)
                    tokens = fold[which][:, :].rearrange("p (g c) -> p g c", g=4)[:, :, 16 * part:16 * (part + NCMP)]
                    tokens = tokens.rearrange("p g (n l t) -> p l g n t", l=CB, t=2)[:, :, :, :, 0]
                    at = VC["pos_v" if which else "pos_k"] + part * CB
                    positions = vec[:, at:at + CB].unsqueeze(2).unsqueeze(3).broadcast_to([P, CB, 4, NCMP])
                    if which:
                        dve.wait_ge(win_ready, n - 1)
                    nc.vector.tensor_tensor(win[:, here].rearrange("p (l g n) -> p l g n", l=CB, g=4), tokens, positions,
                                            ALU.add).then_inc(win_summed, 1)
                for part in range(2):
                    n = which * 2 + part
                    here = slice(part * CW, (part + 1) * CW)
                    dve.wait_ge(win_hi_ready, n + 1)
                    nc.vector.tensor_tensor(win_lo[which][:, here], win[:, here], win_hi[which][:, here].bitcast(f32),
                                            ALU.subtract).then_inc(win_ready, 1)
            for which in range(2):
                for n in range(4):
                    split_lo(At(CH["cmp"] + 4 * which + n + 2))
                c, t = At(CH["cmp"] + 4 * which + 3), At(TL["cmp"] + which)
                complete(c)
                nc.vector.tensor_copy(hidx[:, :], pj[t.par][:, 0:2 * P]).then_inc(pj_free[t.par], 1)
                dve.wait_ge(pj_free[t.par], t.half + 2)
                link(nc.vector.tensor_tensor(hidt[:, :], hidx[:, :], hidx[:, :], ALU.mult))
                link(nc.vector.tensor_scalar(hidt[:, :], hidt[:, :], 0.044715, 1.0, ALU.mult, ALU.add))
                nc.vector.tensor_tensor(hidt[:, :], hidt[:, :], hidx[:, :], ALU.mult).then_inc(hid_x, 1)
                dve.wait_ge(hid_th, which + 1)
                link(nc.vector.tensor_scalar(hidt[:, :], hidt[:, :], 0.5, 0.5, ALU.mult, ALU.add))
                nc.vector.tensor_tensor(hidf[which][:, :], hidt[:, :], hidx[:, :], ALU.mult).then_inc(hid_f, 1)
                dve.wait_ge(hid_f, which + 1)

            def hidden_lo(which):
                here = slice(2 * which * P, 2 * (which + 1) * P)
                dve.wait_ge(hid_hi_ready, which + 1)
                nc.vector.tensor_tensor(hid_lo[:, here], HIDDEN[which][:, 0:2 * P], hid_hi[:, here].bitcast(f32),
                                        ALU.subtract).then_inc(hid_ready, 1)

            dve.wait_ge(ld["tab2"], 16)
            dve.wait_ge(zeroed, 3)
            for s, (kn, branch) in enumerate((("nk_s", "slc"), ("nk_w", "win"))):
                if s:
                    c, t = At(CH["cmp2"]), At(TL["cmp2"])
                    split_lo(c + 2)
                    complete(c)
                    for hh in range(2):
                        last = nc.vector.tensor_scalar(
                            cmp_k[:, :].rearrange("p (g h n) -> p g h n", g=4, h=2)[:, :, hh, :],
                            pj[t.par][:, 0:P].rearrange("p (g n) -> p g n", g=4), C("half", hh), None, ALU.mult)
                    last.then_inc(pj_free[t.par], 1)
                stage = ("nkv_s", "nkv_w")[s]
                for k in range(4):
                    c, t = At(CH[stage] + k), At(TL[stage] + k)
                    split_lo(c + 2)
                    if k < 2:
                        link(rope(ktmp[:, 0:S], qraw[:, :], tab64, SHUF64, t))
                        spread_keys(n_k[branch], k).then_inc(roped, 1)
                        if s == 0:
                            hidden_lo(k)
            apply("q2")
            split_lo(At(CH["gates"] + 2))
            dve.wait_ge(gate_done, 1)
            early = gate[:, 0:16]
            link(nc.vector.tensor_scalar(early, early, C("rowvalid"), None, ALU.mult))
            with dve.Fori(0, 4) as i:
                for k in range(2):
                    split_lo(At(CH["nz"] + k + 2, i, 2))
            attention("nq")
            residual("nout", 1)
            norm("final2")

        @block.tensor
        def _(pe):
            pe.sem_inc(chunk_used, 2)
            pe.sem_inc(exp_done, 2)
            pe.sem_inc(p_turned, 2)
            pe.sem_inc(pT_ready, 2)
            pe.sem_inc(pv_done, 2)
            pe.wait_ge(setup, 1)
            pe.wait_ge(ld["cst"], 16)

            def product(acc, w0, cpar, x, first, last):
                col = cpar * CW + w0 * P
                passes = ((w_hi, 0), (w_hi, 1), (w_lo, 0))
                for k, (w, part) in enumerate(passes):
                    mm = nc.tensor.matmul(acc, w[:, col:col + P], x[part], start=first and k == 0, stop=last and k == 2)
                return mm

            def arrived(c):
                pe.wait_ge(lo_ready, c.v + 3)

            def free(t):
                pe.wait_ge(pj_free[t.par], t.half + 1)

            def project(c, t, hi, lo, n=S, norm=None, some=range(CB)):
                if 0 in some:
                    arrived(c)
                    free(t)
                for k in some:
                    if norm:
                        pe.wait_ge(*normed(norm, k))
                    mm = product(pj[t.par][:, 0:n], k, c.par, (hi[:, k * n:(k + 1) * n], lo[:, k * n:(k + 1) * n]),
                                 k == 0, k == CB - 1)
                if CB - 1 in some:
                    mm.then_inc(chunk_used, 1)

            def norm(name):
                sums(name)
                spread(name)

            def sums(name):
                n, k = NORM[name][1], dict(NORMS)[name]
                if name in BEHIND:
                    number = list(BEHIND).index(name)
                    pe.wait_ge(rest_summed, (DT - 2) * (number + 1))
                    for b in range(NB):
                        nc.tensor.matmul(sum_banks(name)[b][:, 0:1], ssum[:, b * P:(b + 1) * P], ones[:, 0:1],
                                         start=True, stop=False)
                    pe.wait_ge(sq_ready, SQBASE[name] + DT)
                    for b in range(NB):
                        mm = nc.tensor.matmul(sum_banks(name)[b][:, 0:1], sq[:, S + b * P:S + (b + 1) * P], ones[:, 0:1],
                                              start=False, stop=True)
                    mm.then_inc(rest_used, 1)
                if name == "final1":
                    pe.wait_ge(gsum_ready, DT - 2)
                    pe.wait_ge(gsq_ready, DT)
                    for b in range(NB):
                        for k, part in enumerate((gsum[:, b * P:(b + 1) * P], gsq[:, S + b * P:S + (b + 1) * P])):
                            mm = nc.tensor.matmul(sum_banks(name)[b][:, 1:2], part, ones[:, 0:1], start=k == 0, stop=k == 1)
                    mm.then_inc(g_used, 1)
                for m in range(0 if name in BEHIND else k):
                    pe.wait_ge(sq_ready, SQBASE[name] + m + 1)
                    for b in range(n // P):
                        mm = nc.tensor.matmul(sum_banks(name)[b][:, 0:1], sq[:, (m % 2) * S + b * P:(m % 2) * S + (b + 1) * P],
                                              ones[:, 0:1], start=m == 0, stop=m == k - 1)
                    mm.then_inc(sq_used, 1)

            def spread(name):
                n, q = NORM[name][1], STATS.index(name)
                pe.wait_ge(rs_ready, q + 1)
                for b in range(n // P):
                    mm = nc.tensor.transpose(px[:, b * P:(b + 1) * P], r4[:, b:b + 1].broadcast_to([P, P]), ident)
                mm.then_inc(factor_ready, 1)

            def turn(t, number, src=None, width=P, blocks=NB):
                pe.wait_ge(pj_free[t.par], t.half + 2)
                src = vraw[:, :] if src is None else src
                for b in range(blocks):
                    mm = nc.tensor.transpose(pt[number % 2][0:width, b * P:(b + 1) * P], src[:, b * width:(b + 1) * width],
                                             ident)
                mm.then_inc(v_turned, 1)

            def query(ph, i, j, some=range(CB)):
                c, t = query_at(ph, i, j)
                project(c, t, h_hi, h_lo, some=some)

            def keys_values(i, j):
                c, t = keys_values_at(i, j)
                arrived(c)
                free(t)
                for k in range(2):
                    product(pj[t.par][:, :], k, c.par, (c_hi[:, k * S:(k + 1) * S], c_lo[:, k * S:(k + 1) * S]),
                            k == 0, k == 1)
                free(t + 1)
                acc = pj[(t + 1).par]
                for b in range(NB):
                    for k in range(2):
                        col = c.par * CW + (2 + k) * P
                        here = slice(k * S + b * P, k * S + (b + 1) * P)
                        for n, (x, w) in enumerate(((c_hi, w_hi), (c_hi, w_lo), (c_lo, w_hi))):
                            mm = nc.tensor.matmul(acc[:, b * P:(b + 1) * P], x[:, here], w[:, col:col + P],
                                                  start=k == 0 and n == 0, stop=k == 1 and n == 2)
                mm.then_inc(chunk_used, 1)

            def score_(ph, i, j, u):
                at = later(ph, i, j, u)
                if at is None:
                    return
                i, j, u = at
                hh, b, branch = ph.units[u]
                t, g, par = i * 2 + j, i + j // 2, j % 2
                k0, w = ph.keys(u)
                if u == 0:
                    if branch in ("mem", "topk"):
                        q = query_at(ph, i, j)[1] if branch == "mem" else keys_values_at(i, j)[1] + 1
                        pe.wait_ge(pj_free[q.par], q.half + 2)
                    if branch != "mem":
                        pe.wait_ge(roped, RP[ph.name] + t + 2)
                q = qn if branch in ("cmp", "mem") else qs
                if branch == "topk":
                    keys = a_k[:, par * S:par * S + w]
                elif branch == "mem":
                    k_at = (2 * t + hh) * MEM
                    keys = mem_k[0 if ph.name == "amem" else 1][:, k_at:k_at + MEM]
                elif branch == "band":
                    keys = b_k[:, sl(g * 2 * S + hh * S + k0, w)]
                elif branch == "cmp":
                    keys = cmp_k[:, sl(g * 2 * NCMP + hh * NCMP, NCMP)]
                else:
                    keys = n_k[branch][:, sl(g * 2 * S + hh * S, w)]
                pe.wait_ge(score_taken, ph.first_score + t * ph.n + u + 1)
                nc.tensor.matmul(ps[u % 2][:, 0:w], q[:, par * S + b * P:par * S + (b + 1) * P], keys,
                                 start=True, stop=True).then_inc(score_done, 1)

            def turn_p(ph, i, j, u):
                at = later(ph, i, j, u)
                if at is None:
                    return
                i, j, u = at
                a = unit_of(ph, i, j, u)
                par = u % 2
                w = ph.keys(u)[1]
                pe.wait_ge(exp_done, a + 3)
                pe.wait_ge(pT_ready, a + 1)
                wide = min(w, P)
                for k in range(w // wide):
                    mm = nc.tensor.transpose(pt[par][0:wide, k * P:(k + 1) * P],
                                             p_sb[:, par * S + k * wide:par * S + (k + 1) * wide], ident)
                mm.then_inc(p_turned, 1)

            def values(ph, i, j, u):
                hh, b, branch = ph.units[u]
                t, g = i * 2 + j, i + j // 2
                a = unit_of(ph, i, j, u)
                par = u % 2
                k0, w = ph.keys(u)
                p, v = ph.split(u)
                r = ph.region(u)
                acc = po[bank_of(ph, j, p)][:, r * ph.dv:(r + 1) * ph.dv]
                if v == 0:
                    if p == (ph.passes + 1) % 3 if ph.passes == 3 else True:
                        n = ph.first_tile + t + (1 if ph.passes == 3 else 0)
                        if not isinstance(n, int) or n > 0:
                            pe.wait_ge(out_ready, n)
                    else:
                        pe.wait_ge(o_scaled, pass_of(ph, i, j, p) - 1)
                pe.wait_ge(pT_ready, a + 3)
                if branch == "cmp":
                    settle(pe)
                    nc.tensor.matmul(acc, pT[0:NCMP, par * S:par * S + P], cmp_v[0:NCMP, sl(g * 64, 64)],
                                     start=True, stop=True).then_inc(pv_done, 1)
                    return
                kbs = w // P
                for k in range(kbs):
                    kb = k0 // P + k
                    if branch == "topk":
                        val = a_v[:, j % 2 * S + kb * P:j % 2 * S + (kb + 1) * P]
                    elif branch == "mem":
                        v_at = kb * 256 + (2 * t + hh) * 64
                        val = mem_v[0 if ph.name == "amem" else 1][:, v_at:v_at + 64]
                    elif branch == "band":
                        val = b_v[:, sl(g * 64 + kb * 256, 64)]
                    else:
                        val = n_v[branch][:, sl(g * 64 + kb * 256, 64)]
                    mm = nc.tensor.matmul(acc, pT[:, par * S + k * P:par * S + (k + 1) * P], val,
                                          start=k == 0, stop=k == kbs - 1)
                mm.then_inc(pv_done, 1)

            def turn_output(ph, i, j):
                pe.wait_ge(o_scaled, pass_of(ph, i, j, ph.passes - 1) + 1)
                out_bank = po[bank_of(ph, j, ph.passes - 1)]
                for b in range(NB):
                    mm = nc.tensor.transpose(out_bank[:, b * P:(b + 1) * P], o_sb[:, b * P:(b + 1) * P], ident)
                mm.then_inc(o_turned, 1)

            def tile(ph, i, j):
                for u in range(ph.n):
                    p, v = ph.split(u)
                    score_(ph, i, j, u + ph.ahead)
                    turn_p(ph, i, j, u + 1)
                    values(ph, i, j, u)
                    last = before(ph, i, j, p)
                    if last and p == 0 and v == ph.at_turn:
                        turn_output(ph, *last[:2])
                    if ph.name == "aq" and u == 0 and more(ph, i, j):
                        keys_values(i, j + 1)
                    if ahead(ph, i, j):
                        if ph.name == "aq" and u:
                            query(ph, i, j + 2, (range(0, 3), range(3, 6), range(6, CB))[u - 1])
                        if ph.name == "bq" and u < CB - 1:
                            query(ph, i, j + 2, range(u + 1 if u else 0, u + 2))
                        if ph.name == "nq" and u in ph.beside:
                            at = ph.beside.index(u)
                            query(ph, i, j + 2, range(at, at + 1))

            def attention(name):
                ph = ATT[name]
                if name in ("bq", "nq"):
                    for j in range(2):
                        query(ph, 0, j)
                if name == "aq":
                    keys_values(0, 0)
                for u in range(ph.ahead):
                    score_(ph, 0, 0, u)
                turn_p(ph, 0, 0, 0)
                attention_tiles(pe, ph, tile)
                turn_output(ph, 0, ph.tiles - 1)

            def down(stage, per, kt, ready, count):
                pe.wait_ge(ready, count - 2)
                def two(i):
                    for j in range(2):
                        t = At(TL[stage] + j, i, 2)
                        free(t)
                        for n in range(per):
                            c = At(CH[stage] + j * per + n, i, 2 * per)
                            arrived(c)
                            for k in range(n * CB, min(kt, (n + 1) * CB)):
                                if isinstance(i, int) and j == 0 and k >= kt - 2:
                                    pe.wait_ge(ready, count - (kt - 1 - k))
                                here = slice(k * S, (k + 1) * S)
                                mm = product(pj[t.par][:, :], k % CB, c.par, (G_hi[:, here], G_lo[:, here]),
                                             k == 0, k == kt - 1)
                            mm.then_inc(chunk_used, 1)

                two(0)
                with pe.Fori(1, DT // 2) as i:
                    two(i)

            def packed_down(stage):
                for j in range(DT):
                    t = At(TL[stage] + j)
                    free(t)
                    for k in range(OT):
                        n, w0 = divmod(j * OT + k, CB)
                        c = At(CH[stage] + n)
                        if w0 == 0:
                            arrived(c)
                        here = slice(k * S, (k + 1) * S)
                        mm = product(pj[t.par][:, :], w0, c.par, (G_hi[:, here], G_lo[:, here]), k == 0, k == OT - 1)
                        if w0 == CB - 1:
                            mm.then_inc(chunk_used, 1)

            def feed_forward(l):
                up, base = CH[f"up{l}"], TL[f"up{l}"]
                for k in range(2):
                    project(At(up + k), At(base + k), h_hi, h_lo, norm=("affn", "bffn")[l] if k == 0 else None)
                with pe.Fori(1, FT) as i:
                    for k in range(2):
                        project(At(up + k, i, 2), At(base + k, i, 2), h_hi, h_lo)
                down(f"down{l}", DOWN_CHUNKS, FT, g_ready, (l + 1) * FT + 1)

            norm("amix")
            project(At(CH["afront"]), At(TL["afront"]), h_hi, h_lo, norm="amix")
            sums("mem")
            for some in (range(4), range(4, CB)):
                project(At(CH["afront"] + 1), At(TL["afront"] + 1), h_hi, h_lo, some=some)
                if 0 in some:
                    spread("mem")
            turn(At(TL["afront"] + 1), TN["widx"], qn[:, S:2 * S])

            def idx_query(i, j, some=range(CB)):
                project(At(CH["idx"] + j, i, 2), At(TL["idx"] + j, i, 2), h_hi, h_lo, some=some)

            def idx_tile(i, j, more):
                t = i * 2 + j
                pe.wait_ge(roped, RP["idx"] + t + 2)
                for u, (hh, b) in enumerate(IDX_UNITS):
                    w = (b + 1) * P
                    pe.wait_ge(score_taken, t * len(IDX_UNITS) + u + 1)
                    nc.tensor.matmul(ps[u % 2][:, 0:w], qs[:, j * S + b * P:j * S + (b + 1) * P],
                                     kidx[:, hh * S:hh * S + w], start=True, stop=True).then_inc(score_done, 1)
                    if u < 4 and more:
                        idx_query(i, j + 2, range(2 * u, 2 * u + 2))

            idx_query(0, 0)
            idx_query(0, 1)
            with pe.Fori(0, 3) as i:
                idx_tile(i, 0, True)
                idx_tile(i, 1, True)
            idx_tile(3, 0, False)
            idx_tile(3, 1, False)
            for k in range(2):
                project(At(CH["ckv"] + k), At(TL["ckv"] + k), h_hi, h_lo)
            sums("ckv")
            number = TN["memv"]
            for k in range(8):
                project(At(CH["mem"] + k), At(TL["mem"] + k), memn_hi, memn_lo, n=MEM, norm="mem" if k == 0 else None)
                if k in (3, 4, 7):
                    turn(At(TL["mem"] + k - 1), number, blocks=MEM // P)
                    number += 1
                if k == 5:
                    spread("ckv")
            query(ATT["aq"], 0, 0)
            turn(At(TL["mem"] + 7), number, blocks=MEM // P)
            query(ATT["aq"], 0, 1)
            all_normed(pe, "ckv")
            attention("aq")
            attention("amem")
            pe.wait_ge(out_ready, ATT["amem"].first_tile + 2 + 1)
            packed_down("aout")
            norm("affn")
            feed_forward(0)

            norm("bmix")
            for k in range(4):
                c, t = At(CH["bfront"] + k), At(TL["bfront"] + k)
                project(c, t, h_hi, h_lo, norm="bmix" if k == 0 else None)
                if k >= 2:
                    turn(t, TN["bv"] + k - 2)
            attention("bq")
            attention("bmem")
            pe.wait_ge(out_ready, ATT["bmem"].first_tile + 2 + 1)
            packed_down("bout")
            norm("bffn")
            feed_forward(1)
            sums("final1")
            pe.wait_ge(r12_ready, 1)
            for bank_, roots in ((po[0], r12), (po[1], r1)):
                for b in range(NB):
                    mm = nc.tensor.transpose(bank_[:, b * P:(b + 1) * P], roots[:, b:b + 1].broadcast_to([P, P]), ident)
                mm.then_inc(factor_ready, 1)

            for k in range(4):
                project(At(CH["conv"] + k), At(TL["conv"] + k), h_hi, h_lo, norm="conv" if k == 0 else None)
            with pe.Fori(1, CT) as i:
                for k in range(4):
                    project(At(CH["conv"] + k, i, 4), At(TL["conv"] + k, i, 4), h_hi, h_lo)
            down("cout", 2, CT, g_ready, 2 * FT + CT + 1)
            norm("kv2")
            for k in range(4):
                project(At(CH["cmp_kv"] + k), At(TL["cmp_kv"] + k), h_hi, h_lo, norm="kv2" if k == 0 else None)
            for which in range(2):
                t = At(TL["cmp"] + which)
                free(t)
                for n in range(4):
                    c = At(CH["cmp"] + 4 * which + n)
                    arrived(c)
                    pe.wait_ge(win_ready, 2 * which + n // 2 + 1)
                    for step in range(4):
                        l = 4 * n + step
                        here = slice(l * P, (l + 1) * P)
                        cols = slice(c.par * CW + 2 * step * P, c.par * CW + 2 * (step + 1) * P)
                        for k, (x, w) in enumerate(((win_hi, w_hi), (win_hi, w_lo), (win_lo, w_hi))):
                            mm = nc.tensor.matmul(pj[t.par][:, 0:2 * P], x[which][:, here], w[:, cols],
                                                  start=l == 0 and k == 0, stop=l == 15 and k == 2)
                    mm.then_inc(chunk_used, 1)

            def turn_hidden(which):
                pe.wait_ge(hid_f, which + 1)
                for m in range(2):
                    mm = nc.tensor.transpose(HIDDEN[which][:, m * P:(m + 1) * P], hidf[which][:, m * P:(m + 1) * P], ident)
                mm.then_inc(hid_turned, 1)

            def kv_tiles(stage, vn):
                for k in range(4):
                    c, t = At(CH[stage] + k), At(TL[stage] + k)
                    project(c, t, h_hi, h_lo)
                    if stage == "nkv_s" and k < 2:
                        turn_hidden(k)
                    if k == 3:
                        turn(At(TL[stage] + 2), TN[vn])
                turn(At(TL[stage] + 3), TN[vn] + 1)

            kv_tiles("nkv_s", "nv_s")
            c = At(CH["cmp2"])
            arrived(c)
            for which in range(2):
                t = At(TL["cmp2"] + which)
                free(t)
                pe.wait_ge(hid_ready, which + 1)
                for m in range(2):
                    here = slice((2 * which + m) * P, (2 * which + m + 1) * P)
                    mm = product(pj[t.par][:, 0:P], 2 * which + m, c.par, (hid_hi[:, here], hid_lo[:, here]), m == 0, m == 1)
            mm.then_inc(chunk_used, 1)
            turn(At(TL["cmp2"] + 1), TN["cmpv"], width=NCMP)
            kv_tiles("nkv_w", "nv_w")
            project(At(CH["gates"]), At(TL["gates"]), h_hi, h_lo, norm="q2")
            turn(At(TL["gates"]), TN["gates"])
            with pe.Fori(0, 4) as i:
                for k in range(2):
                    project(At(CH["nz"] + k, i, 2), At(TL["nz"] + k, i, 2), h_hi, h_lo)
            attention("nq")
            down("nout", 1, DT, out_ready, ATT["nq"].first_tile + 8 + 1)
            norm("final2")


def kernel(**inputs):
    import numpy as np
    import concourse.bacc as bacc
    from concourse.bass_utils import run_bass_kernel_spmd as run

    a = {k: np.asarray(v) for k, v in inputs.items()}
    f = np.float32

    def cols(w, k, c0, n=P):
        b = np.zeros((P, P), f)
        b[:, 0:n] = w[k * P:(k + 1) * P, c0:c0 + n]
        return b

    def picked(w, k, index):
        return w[k * P:(k + 1) * P][:, index]

    zero = np.zeros((P, P), f)
    chunks = []

    def chunk(blocks):
        chunks.append(np.stack(list(blocks) + [zero] * (CB - len(blocks)), axis=1))

    def plain(w, c0, count, kt=CB):
        for m in range(count):
            blocks = [cols(w, k, c0 + m * P) for k in range(kt)]
            for n in range(0, kt, CB):
                chunk(blocks[n:n + CB])

    def packed(w):
        blocks = [cols(w, k, m * P) for m in range(DT) for k in range(OT)]
        for n in range(0, DT * OT, CB):
            chunk(blocks[n:n + CB])

    wa, wb, wn, wkv = a["a_w_in"][0], a["b_w_in"][0], a["b_w_in_2"][0], a["w_kv_2"]
    uk = a["a_w_uk"][0]
    uv = a["a_w_uv"][0].reshape(256, 1024)
    chunk([np.concatenate([wa[k * P:(k + 1) * P, 2336:2400]] * 2, 1) for k in range(DT)])
    chunk([np.concatenate([wa[k * P:(k + 1) * P, 2400:2416], np.zeros((P, 80), f), wa[k * P:(k + 1) * P, 1280:1312]], 1)
           for k in range(DT)])
    plain(wa, 1312, 8)
    plain(wa, 1024, 2)
    for l in range(2):
        plain(a["w_mem_kv"][l], 0, 4)
    def head_query(h):
        if h >= 8:
            plain(wa, 2416 + (h - 8) * P, 1)
            return
        order = h * P + np.concatenate([np.arange(32, P), np.arange(32)])
        chunk([picked(wa, k, order) for k in range(DT)])

    def head_keys_values(h):
        blocks = []
        for k in range(2):
            b = np.zeros((P, P), f)
            b[:, 0:96] = uk[k * P:(k + 1) * P, h, :]
            blocks.append(b)
        chunk(blocks + [cols(uv, k, h * P) for k in range(2)])

    head_query(0)
    head_query(1)
    for h in range(8):
        head_keys_values(h)
        if h:
            head_query(h + 1)
    head_query(9)
    packed(a["a_w_out"][0])

    def feed_forward(l):
        for m in range(FT):
            plain(a["f_w_up"][l], m * P, 1)
            plain(a["f_w_up"][l], FT * P + m * P, 1)
        plain(a["f_w_down"][l], 0, DT, FT)

    feed_forward(0)
    plain(wb, 1024, 4)
    plain(wb, 0, 8)
    plain(wb, 1536, 2)
    packed(a["b_w_out"][0])
    feed_forward(1)
    for m in range(CT):
        for part in (1, 2, 3, 0):
            plain(a["a_w_in_2"][0], part * CT * P + m * P, 1)
    plain(a["a_w_out_2"][0], 0, DT, CT)
    plain(wkv, 0, 4)
    for which in ("k", "v"):
        blocks = [cols(a[f"cmp_w1_{which}_2"], k, m * P) for k in range(16) for m in range(2)]
        for n in range(0, 32, CB):
            chunk(blocks[n:n + CB])
    plain(wkv, 2 * 256, 4)
    w2k, w2v = a["cmp_w2_k_2"], a["cmp_w2_v_2"]
    chunk([np.concatenate([w2k[k * P:(k + 1) * P]] * 2, 1) for k in range(2)] + [cols(w2v, k, 0, 64) for k in range(2)])
    plain(wkv, 4 * 256, 4)
    branchwise = 1024 + np.arange(48).reshape(16, 3).T.reshape(-1)
    chunk([np.concatenate([picked(wn, k, branchwise), np.zeros((P, P - 48), f)], 1) for k in range(DT)])
    plain(wn, 1072, 8)
    plain(wn, 0, 8)
    plain(a["b_w_out_2"][0], 0, DT)
    assert len(chunks) == NCHUNKS, (len(chunks), NCHUNKS)
    stream = np.stack(chunks).reshape(NCHUNKS, P, CW)

    def tiles(v):
        return np.ascontiguousarray(v.reshape(-1, P).T)

    def positions(e):
        return np.concatenate([tiles(e.reshape(-1)), np.zeros((P, 2), f)], 1)

    vec = np.concatenate([
        tiles(a["g_mix"].reshape(-1)), tiles(a["g_ffn"].reshape(-1)), tiles(a["g_mem"]), tiles(a["g_final"]),
        tiles(a["a_norm_2"][0]), tiles(a["kv_norm_2"]), tiles(a["b_norm_2"][0]), tiles(a["final_norm_2"]),
        tiles(a["a_kv_norm"][0]), tiles(a["f_conv_w"].reshape(-1)), tiles(a["f_conv_b"].reshape(-1)),
        tiles(a["a_conv_w_2"][0].reshape(-1)), np.broadcast_to(a["b_sinks"][0], (P, 16)),
        positions(a["cmp_pos_k_2"]), positions(a["cmp_pos_v_2"])], 1)
    assert vec.shape[1] == NVEC

    q, k = np.arange(P)[:, None], np.arange(P)[None, :]
    hide_later = np.where(k > q, NEG, 0.0)
    hide_far = np.where(k <= q, NEG, 0.0)
    n = np.arange(NCMP)[None, :]
    cmp = [np.where((n < NCMP - 1) & (16 * n + 31 <= b * P + q), 0.0, NEG) for b in range(NB)]

    def rotation(dim, at):
        rot = dim // 4
        freq = (np.float64(500000.0) ** (-np.arange(0, rot, 2) / rot)).astype(f)
        inv, sgn = np.zeros(P, f), np.zeros(P, f)
        for h in range(0, P, dim):
            inv[h + at:h + at + rot] = np.concatenate([freq, freq])
            sgn[h + at:h + at + rot] = np.concatenate([-np.ones(rot // 2), np.ones(rot // 2)])
        return inv[:, None], sgn[:, None]

    inv128, sgn128 = rotation(128, 96)
    inv64, sgn64 = rotation(64, 0)
    cst = np.concatenate([np.eye(P), np.zeros((P, S - P)), hide_later, hide_far, hide_later, *cmp,
                          (q < 64), (q >= 64), inv128, sgn128, inv64, sgn64, (q >= 31)], 1).astype(f)
    assert cst.shape[1] == NCONST
    angle = (inv64 * np.arange(S, dtype=f)[None, :]).astype(np.float64)
    tab2 = np.concatenate([np.cos(angle), np.sin(angle) * sgn64], 1).astype(f)

    def feature_major(x, n):
        return np.ascontiguousarray(x.T.reshape(DT, P, n).transpose(1, 0, 2).reshape(P, DT * n))

    arrays = {
        "wstream": stream, "x": feature_major(a["x"][0], S), "mem": feature_major(a["mem"][0], MEM),
        "pos": np.ascontiguousarray(np.broadcast_to(a["positions"], (P, S))).astype(np.int32),
        "vec": np.ascontiguousarray(vec), "cst": cst, "tab2": tab2}
    nc = bacc.Bacc("TRN2", target_bir_lowering=False, num_devices=1)
    args = [nc.dram_tensor(f"in_{n}", v.shape, mybir.dt.from_np(v.dtype), kind="ExternalInput").ap()
            for n, v in arrays.items()]
    args.append(nc.dram_tensor("out_x", (P, DT * S), mybir.dt.float32, kind="ExternalOutput").ap())
    build(nc, *args)
    got = run(nc, [{f"in_{n}": v for n, v in arrays.items()}], core_ids=[0]).results[0]["out_x"]
    return np.ascontiguousarray(got.reshape(P, DT, S).transpose(1, 0, 2).reshape(D, S).T)[None]
```
